# Optimizing a Trainium2 kernel written in Bass

```python
import math
import jax, jax.numpy as jnp
from jax import lax
import numpy as np
import jax
import jax.numpy as jnp

D_MODEL = 1024
BATCH = 1
SEQ = 256
DEPTH = 2

CHUNK = 64
N_A = DEPTH // 2
N_B = DEPTH - N_A
N_DENSE = (DEPTH + 1) // 2
N_MOE = DEPTH // 2
GMLP_CHUNK = 128
A_FFN = 6 * D_MODEL
A_HALF = A_FFN // 2
A_GROUPS = 8
A_GROUP_DIM = A_HALF // A_GROUPS
B_HEAD_DIM = 64
B_HEADS = D_MODEL // B_HEAD_DIM
Q_BLOCK = 128
D_FF = ((8 * D_MODEL // 3 + 255) // 256) * 256
N_EXPERTS = 8
TOP_K = 2
D_EXPERT = 7 * D_MODEL // 2
RMS_EPS = 1e-6
NEG_INF = -1e30


def rms_norm(x, g):
    xf = x.astype(jnp.float32)
    y = xf * lax.rsqrt(jnp.mean(xf * xf, axis=-1, keepdims=True) + RMS_EPS)
    return (y * g.astype(jnp.float32)).astype(x.dtype)

def swiglu(x, w_in, w_out):
    a, b = jnp.split(x @ w_in, 2, axis=-1)
    return (jax.nn.silu(a) * b) @ w_out

def mixer_a(x, w_in, v_norm_g, w_spatial, b_spatial, w_out):
    B, S, _ = x.shape
    uv = jax.nn.gelu(x @ w_in, approximate=False)
    u, v = jnp.split(uv, 2, axis=-1)
    v = rms_norm(v, v_norm_g)
    v = v.reshape(B, S // GMLP_CHUNK, GMLP_CHUNK, A_GROUPS, A_GROUP_DIM)
    pos = jnp.arange(GMLP_CHUNK)
    mask = (pos[None, :] // CHUNK) <= (pos[:, None] // CHUNK)
    w = jnp.where(mask[None], w_spatial, jnp.zeros_like(w_spatial))
    v = jnp.einsum('gij,bcjgd->bcigd', w, v) + b_spatial.T[None, None, :, :, None]
    return (u * v.reshape(B, S, A_HALF)) @ w_out

def shared_kv(h, norm_g, w_kvf, b_f, k_norm_g):
    B, S, _ = h.shape
    s = rms_norm(h, norm_g)
    kvf = s @ w_kvf
    k = kvf[..., :D_MODEL].reshape(B, S, B_HEADS, B_HEAD_DIM)
    v = kvf[..., D_MODEL:2 * D_MODEL].reshape(B, S, B_HEADS, B_HEAD_DIM)
    f = kvf[..., 2 * D_MODEL:]
    k = rms_norm(k, k_norm_g).transpose(0, 2, 1, 3)
    v = v.transpose(0, 2, 1, 3)
    log_f = jax.nn.log_sigmoid((f + b_f).astype(jnp.float32))
    cum_log_f = jnp.cumsum(log_f, axis=1).transpose(0, 2, 1)
    return k, v, cum_log_f

def mixer_b(x, k, v, cum_log_f, w_in, q_norm_g, w_out):
    B, S, _ = x.shape
    qg = x @ w_in
    q, gate = jnp.split(qg, 2, axis=-1)
    q = rms_norm(q.reshape(B, S, B_HEADS, B_HEAD_DIM), q_norm_g).transpose(0, 2, 1, 3)
    scale = B_HEAD_DIM ** -0.5
    outs = []
    for blk in range(S // Q_BLOCK):
        qs, qe = blk * Q_BLOCK, (blk + 1) * Q_BLOCK
        logits = jnp.einsum('bhqd,bhkd->bhqk', q[:, :, qs:qe], k[:, :, :qe]).astype(jnp.float32) * scale
        logits = logits + cum_log_f[:, :, qs:qe, None] - cum_log_f[:, :, None, :qe]
        causal = jnp.arange(qs, qe)[:, None] >= jnp.arange(qe)[None, :]
        logits = jnp.where(causal[None, None], logits, NEG_INF)
        p = jax.nn.softmax(logits, axis=-1).astype(v.dtype)
        outs.append(jnp.einsum('bhqk,bhkd->bhqd', p, v[:, :, :qe]))
    o = jnp.concatenate(outs, axis=2).transpose(0, 2, 1, 3).reshape(B, S, D_MODEL)
    o = o * jax.nn.sigmoid(gate)
    return o @ w_out

def moe_swiglu(x, w_router, w_in, w_out):
    B, S, D = x.shape
    xt = x.reshape(B * S, D)
    logits = (xt @ w_router).astype(jnp.float32)
    top_v, top_i = lax.top_k(logits, TOP_K)
    top_w = jax.nn.softmax(top_v, axis=-1)
    gates = jnp.sum(jax.nn.one_hot(top_i, N_EXPERTS, dtype=jnp.float32) * top_w[..., None], axis=1)
    y = jnp.zeros_like(xt)
    for e in range(N_EXPERTS):
        y = y + gates[:, e:e + 1].astype(xt.dtype) * swiglu(xt, w_in[e], w_out[e])
    return y.reshape(B, S, D)

def first_inputs(seed: int = 0) -> dict:
    key = jax.random.key(seed)
    ks = jax.random.split(key, 24)

    def dense(k, shape, fan_in, s=1.0):
        return jax.random.normal(k, shape, jnp.float32) * (s * fan_in ** -0.5)

    def gain(k, shape):
        return 1.0 + 0.02 * jax.random.normal(k, shape, jnp.float32)

    return {
        "x": jax.random.normal(ks[0], (BATCH, SEQ, D_MODEL), jnp.float32),
        "a_norm_g": gain(ks[1], (N_A, D_MODEL)),
        "a_w_in": dense(ks[2], (N_A, D_MODEL, A_FFN), D_MODEL),
        "a_v_norm_g": gain(ks[3], (N_A, A_HALF)),
        "a_w_spatial": dense(ks[4], (N_A, A_GROUPS, GMLP_CHUNK, GMLP_CHUNK), GMLP_CHUNK, 0.5),
        "a_b_spatial": 1.0 + 0.1 * jax.random.normal(ks[5], (N_A, A_GROUPS, GMLP_CHUNK), jnp.float32),
        "a_w_out": dense(ks[6], (N_A, A_HALF, D_MODEL), A_HALF),
        "f_norm_g": gain(ks[7], (N_DENSE, D_MODEL)),
        "f_w_in": dense(ks[8], (N_DENSE, D_MODEL, 2 * D_FF), D_MODEL),
        "f_w_out": dense(ks[9], (N_DENSE, D_FF, D_MODEL), D_FF),
        "kv_norm_g": gain(ks[10], (D_MODEL,)),
        "kv_w": dense(ks[11], (D_MODEL, 2 * D_MODEL + B_HEADS), D_MODEL),
        "kv_b_f": 4.0 + 0.1 * jax.random.normal(ks[12], (B_HEADS,), jnp.float32),
        "k_norm_g": gain(ks[13], (B_HEAD_DIM,)),
        "b_norm_g": gain(ks[14], (N_B, D_MODEL)),
        "b_w_in": dense(ks[15], (N_B, D_MODEL, 2 * D_MODEL), D_MODEL),
        "q_norm_g": gain(ks[16], (N_B, B_HEAD_DIM)),
        "b_w_out": dense(ks[17], (N_B, D_MODEL, D_MODEL), D_MODEL),
        "m_norm_g": gain(ks[18], (N_MOE, D_MODEL)),
        "m_w_router": dense(ks[19], (N_MOE, D_MODEL, N_EXPERTS), D_MODEL),
        "m_w_in": dense(ks[20], (N_MOE, N_EXPERTS, D_MODEL, 2 * D_EXPERT), D_MODEL),
        "m_w_out": dense(ks[21], (N_MOE, N_EXPERTS, D_EXPERT, D_MODEL), D_EXPERT),
    }

def first_block(x, a_norm_g, a_w_in, a_v_norm_g, a_w_spatial, a_b_spatial, a_w_out,
              f_norm_g, f_w_in, f_w_out,
              kv_norm_g, kv_w, kv_b_f, k_norm_g,
              b_norm_g, b_w_in, q_norm_g, b_w_out,
              m_norm_g, m_w_router, m_w_in, m_w_out):
    h = x
    k = v = cum_log_f = None
    for layer in range(DEPTH):
        if layer < N_A:
            i = layer
            h = h + mixer_a(rms_norm(h, a_norm_g[i]), a_w_in[i], a_v_norm_g[i],
                            a_w_spatial[i], a_b_spatial[i], a_w_out[i])
        else:
            if layer == N_A:
                k, v, cum_log_f = shared_kv(h, kv_norm_g, kv_w, kv_b_f, k_norm_g)
            i = layer - N_A
            h = h + mixer_b(rms_norm(h, b_norm_g[i]), k, v, cum_log_f,
                            b_w_in[i], q_norm_g[i], b_w_out[i])
        if layer % 2 == 0:
            j = layer // 2
            h = h + swiglu(rms_norm(h, f_norm_g[j]), f_w_in[j], f_w_out[j])
        else:
            j = layer // 2
            h = h + moe_swiglu(rms_norm(h, m_norm_g[j]), m_w_router[j], m_w_in[j], m_w_out[j])
    return h


HEAD_DIM = 64
ROT_DIM = HEAD_DIM // 4
ROPE_THETA = 500000.0
DIL_GROUPS = ((128, 1), (512, 4), (2048, 16))
HEADS_PER_DIL_GROUP = 2
N_HEADS_A = len(DIL_GROUPS) * HEADS_PER_DIL_GROUP
N_HEADS_B = 6
N_HEADS_M = 4
MOBA_BLOCK = 256
MOBA_TOPK = 3
MOBA_Q_CHUNK = 32
N_MEM = 256
D_FF_2 = 4 * D_MODEL
N_BRANCH = 3
WIDTH_A = N_HEADS_A * HEAD_DIM
WIDTH_A_OUT = HEADS_PER_DIL_GROUP * HEAD_DIM
WIDTH_B = N_HEADS_B * HEAD_DIM
WIDTH_M = N_HEADS_M * HEAD_DIM
D_IN = 3 * WIDTH_A + 3 * WIDTH_B + WIDTH_M + N_BRANCH * D_MODEL
NEG_INF_2 = -1e30


def rms_norm_2(x, g):
    xf = x.astype(jnp.float32)
    y = xf * lax.rsqrt(jnp.mean(xf * xf, axis=-1, keepdims=True) + RMS_EPS)
    return (y * g.astype(jnp.float32)).astype(x.dtype)

def partial_rope(x, pos):
    inv_freq = 1.0 / (ROPE_THETA ** (jnp.arange(0, ROT_DIM, 2, dtype=jnp.float32) / ROT_DIM))
    ang = pos.astype(jnp.float32)[:, None] * inv_freq[None, :]
    cos = jnp.cos(ang)[None, :, None, :]
    sin = jnp.sin(ang)[None, :, None, :]
    xr = x[..., :ROT_DIM].astype(jnp.float32)
    x1, x2 = xr[..., :ROT_DIM // 2], xr[..., ROT_DIM // 2:]
    rot = jnp.concatenate([x1 * cos - x2 * sin, x2 * cos + x1 * sin], axis=-1).astype(x.dtype)
    return jnp.concatenate([rot, x[..., ROT_DIM:]], axis=-1)

def dilated_window_attn(q, k, v, window, dilation):
    B, S, H, Dh = q.shape
    n = window // dilation
    span = n * dilation
    Sp = -(-S // span) * span
    L = Sp // dilation
    nblk = L // n

    def to_blocks(t):
        t = jnp.pad(t, ((0, 0), (0, Sp - S), (0, 0), (0, 0)))
        t = t.reshape(B, L, dilation, H, Dh).transpose(0, 2, 3, 1, 4)
        return t.reshape(B, dilation, H, nblk, n, Dh)

    def with_prev(t):
        prev = jnp.pad(t, ((0, 0), (0, 0), (0, 0), (1, 0), (0, 0), (0, 0)))[:, :, :, :-1]
        return jnp.concatenate([prev, t], axis=-2)

    qb = to_blocks(q)
    kk = with_prev(to_blocks(k))
    vv = with_prev(to_blocks(v))
    s = jnp.einsum('brhnqd,brhnkd->brhnqk', qb, kk).astype(jnp.float32)
    i = jnp.arange(n)[:, None]
    j = jnp.arange(2 * n)[None, :]
    band = (j >= i) & (j <= i + n)
    first = (jnp.arange(nblk) == 0)[:, None, None] & (j < n)[None]
    mask = band[None] & ~first
    s = jnp.where(mask, s, NEG_INF_2)
    mx = jnp.max(s, axis=-1, keepdims=True)
    p = jnp.exp(s - mx)
    den = jnp.sum(p, axis=-1, keepdims=True)
    o = jnp.einsum('brhnqk,brhnkd->brhnqd', (p / den).astype(v.dtype), vv)
    lse = (mx + jnp.log(den))[..., 0]
    o = o.reshape(B, dilation, H, L, Dh).transpose(0, 3, 1, 2, 4).reshape(B, Sp, H, Dh)[:, :S]
    lse = lse.reshape(B, dilation, H, L).transpose(0, 3, 1, 2).reshape(B, Sp, H)[:, :S]
    return o, lse

def dilated_mixer(q, k, v):
    B, S = q.shape[0], q.shape[1]
    outs, lses = [], []
    for g, (win, dil) in enumerate(DIL_GROUPS):
        sl = slice(g * HEADS_PER_DIL_GROUP, (g + 1) * HEADS_PER_DIL_GROUP)
        o, l = dilated_window_attn(q[:, :, sl], k[:, :, sl], v[:, :, sl], win, dil)
        outs.append(o)
        lses.append(l)
    w = jax.nn.softmax(jnp.stack(lses, axis=0), axis=0)
    o = jnp.einsum('gbsh,gbshd->bshd', w, jnp.stack(outs, axis=0).astype(jnp.float32))
    return o.astype(q.dtype).reshape(B, S, WIDTH_A_OUT)

def moba_attn(q, k, v):
    B, S, H, Dh = q.shape
    nB = -(-S // MOBA_BLOCK)
    Sp = nB * MOBA_BLOCK
    padw = ((0, 0), (0, Sp - S), (0, 0), (0, 0))
    qt = jnp.pad(q, padw).transpose(0, 2, 1, 3)
    kt = jnp.pad(k, padw).transpose(0, 2, 1, 3)
    vt = jnp.pad(v, padw).transpose(0, 2, 1, 3)
    kb = kt.reshape(B, H, nB, MOBA_BLOCK, Dh)
    vb = vt.reshape(B, H, nB, MOBA_BLOCK, Dh)
    qpos = jnp.arange(Sp, dtype=jnp.int32)
    qblk = qpos // MOBA_BLOCK
    own = jnp.broadcast_to(qblk[None, None, :, None], (B, H, Sp, 1))
    n_sel = min(MOBA_TOPK, nB - 1)
    if n_sel > 0:
        kmean = jnp.mean(kb.astype(jnp.float32), axis=3)
        gate = jnp.einsum('bhsd,bhnd->bhsn', qt.astype(jnp.float32), kmean)
        past = jnp.arange(nB, dtype=jnp.int32)[None, :] < qblk[:, None]
        _, top_idx = lax.top_k(jnp.where(past, gate, NEG_INF_2), n_sel)
        top_ok = jnp.take_along_axis(jnp.broadcast_to(past, gate.shape), top_idx, axis=-1)
        blk_idx = jnp.concatenate([top_idx.astype(jnp.int32), own], axis=-1)
        blk_ok = jnp.concatenate([top_ok, jnp.ones_like(own, dtype=bool)], axis=-1)
    else:
        blk_idx = own
        blk_ok = jnp.ones_like(own, dtype=bool)
    n_tot = blk_idx.shape[-1]
    nc = Sp // MOBA_Q_CHUNK
    C = MOBA_Q_CHUNK
    q_c = qt.reshape(B, H, nc, C, Dh).transpose(2, 0, 1, 3, 4)
    idx_c = blk_idx.reshape(B, H, nc, C, n_tot).transpose(2, 0, 1, 3, 4)
    ok_c = blk_ok.reshape(B, H, nc, C, n_tot).transpose(2, 0, 1, 3, 4)
    pos_c = qpos.reshape(nc, C)
    bi = jnp.arange(B)[:, None, None, None]
    hi = jnp.arange(H)[None, :, None, None]
    offs = jnp.arange(MOBA_BLOCK, dtype=jnp.int32)

    def chunk(args):
        qc, ic, okc, pc = args
        ks = kb[bi, hi, ic]
        vs = vb[bi, hi, ic]
        s = jnp.einsum('bhcd,bhcnkd->bhcnk', qc, ks).astype(jnp.float32)
        kpos = ic[..., None] * MOBA_BLOCK + offs
        mask = okc[..., None] & (kpos <= pc[None, None, :, None, None])
        s = jnp.where(mask, s, NEG_INF_2).reshape(B, H, C, n_tot * MOBA_BLOCK)
        p = jax.nn.softmax(s, axis=-1).reshape(B, H, C, n_tot, MOBA_BLOCK)
        return jnp.einsum('bhcnk,bhcnkd->bhcd', p.astype(vs.dtype), vs)

    o = lax.map(chunk, (q_c, idx_c, ok_c, pos_c))
    o = o.transpose(1, 2, 0, 3, 4).reshape(B, H, Sp, Dh)
    return o.transpose(0, 2, 1, 3)[:, :S]

def memory_attn(q, mem_n, w_mkv):
    B, S = q.shape[0], q.shape[1]
    M = mem_n.shape[1]
    kv = (mem_n @ w_mkv).reshape(B, M, 2, N_HEADS_M, HEAD_DIM)
    s = jnp.einsum('bshd,bmhd->bhsm', q, kv[:, :, 0]).astype(jnp.float32)
    p = jax.nn.softmax(s, axis=-1)
    o = jnp.einsum('bhsm,bmhd->bshd', p.astype(q.dtype), kv[:, :, 1])
    return o.reshape(B, S, WIDTH_M)

def hybrid_layer(x, mem, pos, g_mix, w_in, w_pa, w_pb, w_pm, w_o, g_mem, w_mkv, g_mlp, w_up, w_down):
    B, S, _ = x.shape
    scale = HEAD_DIM ** -0.5
    h = rms_norm_2(x, g_mix)
    z = h @ w_in
    o1 = 3 * WIDTH_A
    o2 = o1 + 3 * WIDTH_B
    o3 = o2 + WIDTH_M
    qkv_a = z[..., :o1].reshape(B, S, 3, N_HEADS_A, HEAD_DIM)
    qkv_b = z[..., o1:o2].reshape(B, S, 3, N_HEADS_B, HEAD_DIM)
    q_m = z[..., o2:o3].reshape(B, S, N_HEADS_M, HEAD_DIM)
    gates = jax.nn.sigmoid(z[..., o3:].reshape(B, S, N_BRANCH, D_MODEL))
    o_a = dilated_mixer(partial_rope(qkv_a[:, :, 0], pos) * scale,
                        partial_rope(qkv_a[:, :, 1], pos), qkv_a[:, :, 2])
    o_b = moba_attn(partial_rope(qkv_b[:, :, 0], pos) * scale,
                    partial_rope(qkv_b[:, :, 1], pos), qkv_b[:, :, 2]).reshape(B, S, WIDTH_B)
    o_m = memory_attn(q_m * scale, rms_norm_2(mem, g_mem), w_mkv)
    y = (gates[:, :, 0] * (o_a @ w_pa) + gates[:, :, 1] * (o_b @ w_pb)
         + gates[:, :, 2] * (o_m @ w_pm))
    x = x + y @ w_o
    hm = rms_norm_2(x, g_mlp)
    x = x + jnp.square(jax.nn.relu(hm @ w_up)) @ w_down
    return x

def second_inputs(seed: int = 0) -> dict:
    key = jax.random.key(seed)
    ks = jax.random.split(key, 16)

    def nrm(k, shape, fan_in):
        return jax.random.normal(k, shape, jnp.float32) * (fan_in ** -0.5)

    def gain(k, shape):
        return 1.0 + 0.05 * jax.random.normal(k, shape, jnp.float32)

    return {
        'x': jax.random.normal(ks[0], (BATCH, SEQ, D_MODEL), jnp.float32),
        'mem': jax.random.normal(ks[1], (BATCH, N_MEM, D_MODEL), jnp.float32),
        'norm_mix': gain(ks[2], (DEPTH, D_MODEL)),
        'w_in': nrm(ks[3], (DEPTH, D_MODEL, D_IN), D_MODEL),
        'w_proj_a': nrm(ks[4], (DEPTH, WIDTH_A_OUT, D_MODEL), WIDTH_A_OUT),
        'w_proj_b': nrm(ks[5], (DEPTH, WIDTH_B, D_MODEL), WIDTH_B),
        'w_proj_m': nrm(ks[6], (DEPTH, WIDTH_M, D_MODEL), WIDTH_M),
        'w_out': nrm(ks[7], (DEPTH, D_MODEL, D_MODEL), D_MODEL),
        'norm_mem': gain(ks[8], (DEPTH, D_MODEL)),
        'w_mem_kv': nrm(ks[9], (DEPTH, D_MODEL, 2 * WIDTH_M), D_MODEL),
        'norm_mlp': gain(ks[10], (DEPTH, D_MODEL)),
        'w_up': nrm(ks[11], (DEPTH, D_MODEL, D_FF_2), D_MODEL),
        'w_down': nrm(ks[12], (DEPTH, D_FF_2, D_MODEL), D_FF_2),
        'norm_final': gain(ks[13], (D_MODEL,)),
    }

def second_block(x, mem, norm_mix, w_in, w_proj_a, w_proj_b, w_proj_m, w_out, norm_mem, w_mem_kv,
              norm_mlp, w_up, w_down, norm_final):
    pos = jnp.arange(x.shape[1], dtype=jnp.int32)
    for l in range(DEPTH):
        x = hybrid_layer(x, mem, pos, norm_mix[l], w_in[l], w_proj_a[l], w_proj_b[l], w_proj_m[l],
                         w_out[l], norm_mem[l], w_mem_kv[l], norm_mlp[l], w_up[l], w_down[l])
    return rms_norm_2(x, norm_final)


def setup_inputs(seed=0):
    out = dict(first_inputs(seed))
    for name, value in second_inputs(seed + 1).items():
        if name != "x":
            out[name + "_2"] = value
    return out


def reference(
    x, a_norm_g, a_w_in, a_v_norm_g, a_w_spatial, a_b_spatial, a_w_out, f_norm_g, f_w_in,
    f_w_out, kv_norm_g, kv_w, kv_b_f, k_norm_g, b_norm_g, b_w_in, q_norm_g, b_w_out, m_norm_g,
    m_w_router, m_w_in, m_w_out, mem_2, norm_mix_2, w_in_2, w_proj_a_2, w_proj_b_2, w_proj_m_2,
    w_out_2, norm_mem_2, w_mem_kv_2, norm_mlp_2, w_up_2, w_down_2, norm_final_2,
):
    x = first_block(
        x, a_norm_g, a_w_in, a_v_norm_g, a_w_spatial, a_b_spatial, a_w_out, f_norm_g, f_w_in,
        f_w_out, kv_norm_g, kv_w, kv_b_f, k_norm_g, b_norm_g, b_w_in, q_norm_g, b_w_out,
        m_norm_g, m_w_router, m_w_in, m_w_out,
    )
    return second_block(
        x, mem_2, norm_mix_2, w_in_2, w_proj_a_2, w_proj_b_2, w_proj_m_2, w_out_2, norm_mem_2,
        w_mem_kv_2, norm_mlp_2, w_up_2, w_down_2, norm_final_2,
    )


_drawn_inputs = setup_inputs


def setup_inputs(seed=0):
    import zlib

    import numpy as np

    out = dict(_drawn_inputs(seed))
    spreads = {}
    factors = {'a_v_norm_g': 3.173,
     'kv_norm_g': 8.0,
     'kv_b_f': 3.658,
     'k_norm_g': 3.925,
     'b_norm_g': 4.478,
     'q_norm_g': 8.0,
     'norm_mix_2': 3.945,
     'norm_mem_2': 8.0}
    for name, (base, spread) in spreads.items():
        noise = np.random.default_rng([zlib.crc32(name.encode()), seed]).standard_normal(out[name].shape)
        drawn = base * np.exp(spread * noise) if base else spread * noise
        out[name] = jnp.asarray(drawn.astype(out[name].dtype))
    for name, factor in factors.items():
        out[name] = (out[name] * factor).astype(out[name].dtype)
    return out
```

```python
from contextlib import ExitStack

import concourse.bass as bass
from concourse import mybir

F32 = mybir.dt.float32
F32R = mybir.dt.float32r
BF16 = mybir.dt.bfloat16
I32 = mybir.dt.int32
U32 = mybir.dt.uint32
ALU = mybir.AluOpType
ACT = mybir.ActivationFunctionType
AX = mybir.AxisListType

P = 128
S = 256
NT = S // P
D = 1024
KC = D // P
BANK = 512
EPS = 1e-6
DEPTH = 2
HD = 64
A_HALF = 3072
A_GROUPS = 8
A_GD = A_HALF // A_GROUPS
NA = A_HALF // BANK
D_FF = 2816
NF = D_FF // 256
HEADS = D // HD
N_EXP = 8
D_EXP = 3584
NS = D_EXP // BANK
SLOTS = P
D_FF2 = 4096
NU = D_FF2 // BANK
W_A, W_B, W_M = 384, 384, 256
NQ = (3 * W_A + 3 * W_B + W_M) // BANK
NG = 3 * D // BANK
H_A, H_B, H_M = 2, 6, 4
ROT = 8
UNIT = 2048
RING = 3
AHEAD = RING - 1
E_RAW = 7

C_ID, C_TRI, C_IOTA, C_ONES, C_COS = 0, 128, 256, 384, 640
N_MASK = 6
C_SIN = C_COS + NT * ROT
N_CST = C_SIN + NT * ROT
G_A, G_F, G_KV, G_B, G_BT = 0, 8, 16, 24, 32
G_K, G_Q, G_BF, G_L = 40, 41, 42, 43
N_SML = G_L + DEPTH * 3 * KC


def unit_numbers():
    first, layer = [], []
    two = lambda *k: [(*k, 0), (*k, 1)]
    for c in range(NA):
        first += two("av", c)
    first += two("au", 0)
    for c in range(1, NA):
        first += two("au", c) + two("ad", c - 1)
    first += two("ad", NA - 1)
    first += two("fu", 0)
    for c in range(1, NF):
        first += two("fu", c) + [("fd", c - 1)]
    first += [("fd", NF - 1)]
    for c in range(4):
        first += two("kv", c)
    for c in range(4):
        first += two("bi", c)
    first += [("bo", i) for i in range(4)]
    for c in range(NQ):
        layer += two("in", c)
    layer += two("mk", 0)
    for c in range(NQ, NQ + NG):
        layer += two("in", c)
    layer += [("pj", i) for i in range(3)] + [("wo", i) for i in range(4)]
    layer += two("mu", 0)
    for c in range(1, NU):
        layer += two("mu", c) + two("md", c - 1)
    layer += two("md", NU - 1)
    return first, layer


FIRST, LAYER = unit_numbers()
N_FIRST, N_LAYER = len(FIRST), len(LAYER)
UNITS = {k: n for n, k in enumerate(FIRST)}
UNITS.update({k: N_FIRST + n for n, k in enumerate(LAYER)})
assert N_LAYER % RING == 0
LANDED = []
for n, k in enumerate(FIRST + LAYER):
    LANDED.append((LANDED[n - RING] if n >= RING else 0) + (32 if k[0] == "fu" else 16))

T_FIRST = ([("wsT", i) for i in range(2)] + [("nA", g) for g in range(4)] + [("sp", j) for j in range(2 * A_GROUPS)]
           + [("au", c, b) for c in range(NA) for b in range(2)]
           + [("nF", g) for g in range(4)] + [("fu", c) for c in range(NF)]
           + [("nKV", g) for g in range(4)] + [("fT", 0)]
           + [("kT", g) for g in range(4)] + [("qT", g) for g in range(4)]
           + [("oT", g) for g in range(4)] + [("nM", g) for g in range(4)])
T_LAYER = ([("nX", g) for g in range(4)] + [("nMem", g) for g in range(4)]
           + [("qT2", g) for g in range(4)] + [("kT2", g) for g in range(4)]
           + [("oT2", g) for g in range(3)] + [("yT", g) for g in range(4)] + [("nU", g) for g in range(4)]
           + [("mu", c, b) for c in range(NU) for b in range(2)])
NOT_SPLIT = ("wsT", "sp", "fT", "kT", "qT", "qT2", "kT2")
N_TL = len(T_LAYER)
T_NUM, T_BANK, T_PREV = {}, {}, {}


def number_fills():
    last = [None, None]
    for where, keys in (("first", T_FIRST), ("layer", T_LAYER)):
        if where == "layer":
            last = [None, None]
        for n, k in enumerate(keys):
            bank = k[-1] % 2
            T_NUM[k] = n + (len(T_FIRST) if where == "layer" else 0)
            T_BANK[k] = bank
            T_PREV[k] = last[bank]
            last[bank] = k


number_fills()
H_FIRST = [k for k in T_FIRST if k[0] not in NOT_SPLIT]
H_LAYER = [k for k in T_LAYER if k[0] not in NOT_SPLIT]
H_NUM = {k: n for n, k in enumerate(H_FIRST + H_LAYER)}
N_HL = len(H_LAYER)

PROJ = {k: n for n, k in enumerate([("av", c) for c in range(NA)] + [("kv", c) for c in range(4)]
                                   + [("bi", c) for c in range(4)] + [("in", c) for c in range(NQ)] + [("mk", 0)]
                                   + [("in", c) for c in range(NQ, NQ + NG)])}
N_PL = NQ + NG + 1
HID = {k: n for n, k in enumerate([("au", c) for c in range(NA)] + [("fu", c) for c in range(NF)]
                                  + [("mu", c) for c in range(NU)])}
NORMS = {k: n for n, k in enumerate(["A", "V", "F", "KV", "K", "Q", "M", "X", "Mem", "U"])}
XRS = {k: n for n, k in enumerate(["A", "F", "KV", "O", "M", "X", "Mem", "O2", "Y", "U"])}


def expert_units():
    keys = [("up", 0, j) for j in range(4)]
    for s in range(1, NS):
        keys += [("up", s, j) for j in range(4)] + [("dn", s - 1, i) for i in range(2)]
    return keys + [("dn", NS - 1, i) for i in range(2)]


EXPERT = expert_units()
N_EU = len(EXPERT)
EU = {k: n for n, k in enumerate(EXPERT)}
assert N_EU % RING == 0 and N_EU % E_RAW == 0
E_SCAT = 4

CAUSAL, NEAR, D4, D4OFF, D16, D16OFF = range(N_MASK)


def items_first():
    out = []
    for t in range(NT):
        n = 8 // (t + 1)
        for h0 in range(0, HEADS, n):
            out.append((t, [(h, [(h, h // 2, kt, ("v", h), CAUSAL if kt == t else None, h) for kt in range(t + 1)])
                            for h in range(h0, h0 + n)]))
    return out


def items_layer():
    out = []
    for t in range(NT):
        a = []
        for hh in range(H_A):
            tiles = []
            for g, (diag, off) in enumerate(((CAUSAL, NEAR), (D4, D4OFF), (D16, D16OFF))):
                head = 2 * g + hh
                tiles += [(head, head // 2, kt, ("a", head), diag if kt == t else off, None) for kt in range(t + 1)]
            a.append((hh, tiles))
        b = [(H_A + h, [(6 + h, 3 + h // 2, kt, ("b", h), CAUSAL if kt == t else None, None) for kt in range(t + 1)])
             for h in range(H_B)]
        m = [(H_A + H_B + h, [(12 + h, 6 + h // 2, kt, ("m", h), None, None) for kt in range(NT)])
             for h in range(H_M)]
        if t == 0:
            out += [(t, a), (t, b)]
        else:
            out += [(t, a[0:1]), (t, a[1:2]), (t, b[0:3]), (t, b[3:6])]
        out.append((t, m))
    return out


ITEMS1, ITEMS2 = items_first(), items_layer()
N_I1, N_I2 = len(ITEMS1), len(ITEMS2)
V_STEPS_LAYER = 24


def program(nc, x, mem, cst_d, masks_d, sml_d, gv_d, gm_d, gfin_d, a_w_in, a_w_spatial, a_w_out, f_w_in, f_w_out, kv_w,
            b_w_in, b_w_out, m_w_router, m_w_in, m_w_out, w_in_2, w_proj_2, w_out_2, w_mem_kv_2, w_up_2, w_down_2,
            out):
    ctx = ExitStack()
    with ctx:
        def sb(name, shape, dt=F32):
            return ctx.enter_context(nc.sbuf_tensor(name, shape, dt))

        def sem(name):
            return ctx.enter_context(nc.semaphore(name))

        raw = sb("raw", [P, RING, UNIT])
        w_hi = sb("w_hi", [P, RING, UNIT], F32R)
        w_lo = sb("w_lo", [P, RING, UNIT], F32R)
        h = sb("h", [P, NT, D])
        xr = sb("xr", [P, NT, D])
        x_hi = sb("x_hi", [P, KC, S], F32R)
        x_lo = sb("x_lo", [P, KC, S], F32R)
        t_hi = sb("t_hi", [P, KC, S], F32R)
        t_lo = sb("t_lo", [P, KC, S], F32R)
        gu = sb("gu", [P, NT, BANK])
        pr = sb("pr", [P, NT, BANK])
        arena = sb("arena", [P, 6 * NT * D])
        qz = sb("qz", [P, HEADS, S])
        kT = sb("kT", [P, KC, S])
        cst = sb("cst", [P, N_CST])
        sml = sb("sml", [P, N_SML])
        gcur = sb("gcur", [P, 3 * KC])
        identb = sb("identb", [P, P], BF16)
        maskb = sb("maskb", [P, N_MASK, P], BF16)
        wf = sb("wf", [P, KC, HEADS])
        wr = sb("wr", [P, KC, N_EXP])
        ss = sb("ss", [P, NT])
        var = sb("var", [P, 2 * HEADS])
        sd = sb("sd", [P, 2 * HEADS])
        rs = sb("rs", [P, 2 * HEADS])
        ssv = sb("ssv", [P, NT, NA])
        nmx = sb("nmx", [P, 2, 8])
        sums = sb("sums", [P, NT, HEADS])
        rsum = sb("rsum", [P, NT, HEADS])
        npass_i = sb("npass_i", [P, 1], I32)

        ident = cst[:, C_ID:C_ID + P]
        tri = cst[:, C_TRI:C_TRI + P]
        iota = cst[:, C_IOTA:C_IOTA + P]
        iota8 = cst[:, C_IOTA:C_IOTA + N_EXP]
        ones = cst[:, C_ONES:C_ONES + P]
        ones2 = cst[:, C_ONES:C_ONES + S]

        mask_f = pr[:, :, :].rearrange("p t n -> p (t n)")[:, 0:N_MASK * P]

        def slab(n, width=NT * D, at=0):
            return arena[:, n * NT * D + at:n * NT * D + at + width]

        v_a = slab(0, NT * A_HALF).rearrange("p (t n) -> p t n", t=NT)
        gv_b = slab(3, A_HALF)
        wsT = slab(4, A_GROUPS * P, at=D).rearrange("p (g i) -> p g i", g=A_GROUPS)
        ws = slab(5, A_GROUPS * P).rearrange("p (g j) -> p g j", g=A_GROUPS)
        k_t = slab(0).rearrange("p (t n) -> p t n", t=NT)
        v_t = slab(1).rearrange("p (t n) -> p t n", t=NT)
        q_t = slab(2).rearrange("p (t n) -> p t n", t=NT)
        gate_t = slab(3).rearrange("p (t n) -> p t n", t=NT)
        sq_t = slab(4).rearrange("p (t n) -> p t n", t=NT)
        sel = slab(5).rearrange("p (h j) -> p h j", h=HEADS)
        fz = sq_t[:, 0, 0:S]
        fa = sq_t[:, 0, S:2 * S]
        fe = sq_t[:, 0, 2 * S:3 * S]
        ncum = sq_t[:, 1, 0:S]
        gm_b = slab(0, D)
        disp = slab(0, NT * SLOTS, at=D).rearrange("p (t n) -> p t n", t=NT)
        dispg = slab(0, NT * SLOTS, at=D + 256).rearrange("p (t n) -> p t n", t=NT)
        comb = slab(0, S, at=D + 512)
        ye = slab(1, D)
        lg = slab(1, NT * 8, at=D).rearrange("p (t n) -> p t n", t=NT)
        mx8 = slab(1, NT * 8, at=D + 16).rearrange("p (t n) -> p t n", t=NT)
        mi8 = slab(1, NT * 8, at=D + 32).bitcast(U32).rearrange("p (t n) -> p t n", t=NT)
        mif = slab(1, NT * 8, at=D + 48).rearrange("p (t n) -> p t n", t=NT)
        gw = slab(1, NT * 4, at=D + 64).rearrange("p (t n) -> p t n", t=NT)
        one1 = slab(1, NT * 8, at=D + 80).rearrange("p (t n) -> p t n", t=NT)
        chosen = slab(1, NT * 8, at=D + 96).rearrange("p (t n) -> p t n", t=NT)
        gate1 = slab(1, NT * 8, at=D + 112).rearrange("p (t n) -> p t n", t=NT)
        gate2 = slab(1, NT * 8, at=D + 128).rearrange("p (t n) -> p t n", t=NT)
        gates = slab(1, NT * 16, at=D + 144).rearrange("p (t n) -> p t n", t=NT)
        place = slab(1, NT * 16, at=D + 176).rearrange("p (t n) -> p t n", t=NT)
        most = slab(1, 2, at=D + 208)
        qkv = slab(0, NT * 3 * D).rearrange("p (t n) -> p t n", t=NT)
        km = qkv[:, :, NQ * BANK:NQ * BANK + 2 * W_M]
        memr = slab(3).rearrange("p (t n) -> p t n", t=NT)
        gat = slab(3, NT * 3 * D).rearrange("p (t n) -> p t n", t=NT)
        rot = pr[:, :, :].rearrange("p t n -> p (t n)")[:, 0:768].rearrange("p (f g h r) -> p f g h r", f=4, g=2, h=12)
        gfin = slab(0, D)

        Y = ctx.enter_context(nc.psum_tensor("Y", [P, 4, BANK], F32))
        U = ctx.enter_context(nc.psum_tensor("U", [P, 2, BANK], F32))
        T = ctx.enter_context(nc.psum_tensor("T", [P, 2, BANK], F32))

        def logit_bank(i):
            return Y[:, 2 * (i % 2):2 * (i % 2) + 2, :].rearrange("p a n -> p (a n)")

        o_bank = T[:, :, :].rearrange("p a n -> p (a n)")
        p_sb = gu[:, :, :].rearrange("p a n -> p (a n)")
        pT_sb = pr[:, :, :].rearrange("p a n -> p (a n)")

        def pair(n):
            return [U[:, t, :] for t in range(NT)] if n % 2 == 0 else [Y[:, t, :] for t in range(NT)]

        s_const = sem("s_const")
        s_wsp = sem("s_wsp")
        s_gv = sem("s_gv")
        s_wf = sem("s_wf")
        s_wr = sem("s_wr")
        s_gm = sem("s_gm")
        s_mem = sem("s_mem")
        s_gfin = sem("s_gfin")
        s_zero = sem("s_zero")
        s_bf = sem("s_bf")
        loaded = [sem(f"loaded{i}") for i in range(RING)]
        hi_ready = sem("hi_ready")
        lo_ready = sem("lo_ready")
        unit_used = sem("unit_used")
        t_filled = sem("t_filled")
        t_split = sem("t_split")
        t_done = sem("t_done")
        n_var = sem("n_var")
        n_sd = sem("n_sd")
        xr_ready = sem("xr_ready")
        proj_out = sem("proj_out")
        hid_act = sem("hid_act")
        hid_ready = sem("hid_ready")
        v_ready = sem("v_ready")
        h_done = sem("h_done")
        v_step = sem("v_step")
        f_z = sem("f_z")
        f_e = sem("f_e")
        ncum_ready = sem("ncum_ready")
        l_filled = sem("l_filled")
        mx_ready = sem("mx_ready")
        p_ready = sem("p_ready")
        p_turned = sem("p_turned")
        pT_a = sem("pT_a")
        pT_v = sem("pT_v")
        pv_done = sem("pv_done")
        o_done = sem("o_done")
        branch = sem("branch")
        r_logits = sem("r_logits")
        r_diff = sem("r_diff")
        r_exp = sem("r_exp")
        r_chosen = sem("r_chosen")
        r_place = sem("r_place")
        r_done = sem("r_done")
        e_loaded = [sem(f"e_loaded{i}") for i in range(E_RAW)]
        e_hi = sem("e_hi")
        e_lo = sem("e_lo")
        e_used = sem("e_used")
        e_disp = sem("e_disp")
        e_gath = sem("e_gath")
        e_ghi = sem("e_ghi")
        e_glo = sem("e_glo")
        e_turn = sem("e_turn")
        e_comb = sem("e_comb")
        e_silu = sem("e_silu")
        e_hid = sem("e_hid")
        e_tf = sem("e_tf")
        e_thi = sem("e_thi")
        e_tlo = sem("e_tlo")
        e_y = sem("e_y")
        e_scat = sem("e_scat")
        e_add = sem("e_add")
        e_pass = sem("e_pass")
        s_out = sem("s_out")

        block = ctx.enter_context(nc.Block())

        def used(key, l=None):
            n = UNITS[key] + 1
            return n if l is None else l * N_LAYER + n

        def filled(key, l=None):
            n = T_NUM[key] + 1
            return n if l is None else l * N_TL + n

        def split(key, l=None):
            n = H_NUM[key] + 1
            return n if l is None else l * N_HL + n

        def proj(key, l=None):
            n = PROJ[key] + 1
            return n if l is None else l * N_PL + n

        def hid(key, l=None):
            n = HID[key] + 1
            return n if l is None else l * NU + n

        def norm_no(key, l=None):
            n = NORMS[key] + 1
            return n if l is None else l * 3 + n

        def xr_no(key, l=None):
            n = XRS[key] + 1
            return n if l is None else l * 5 + n

        def item_no(i, l=None):
            return i + 1 if l is None else l * N_I2 + N_I1 + i + 1

        def o_no(t, l=None):
            return t + 1 if l is None else l * NT + NT + t + 1

        def unit_slot(u):
            return u % RING

        def e_raw(k):
            i = k % E_RAW
            return raw[:, i, :] if i < RING else slab(2 + i - RING)


        @block.sync
        def _(sp):
            col = "(hf kc p) (c n) -> c hf p kc n"
            colf = dict(hf=2, kc=4, p=P, n=BANK)
            row2 = dict(i=2, kc=2, p=P)
            a_in = a_w_in[0].rearrange(col, **colf)
            a_out = a_w_out[0].rearrange("(c i kc p) n -> c i p kc n", **row2)
            f_in = f_w_in[0].rearrange("(hf kc p) (ab c n) -> c hf ab p kc n", hf=2, kc=4, p=P, ab=2, n=256)
            f_out = f_w_out[0].rearrange("(c kc p) n -> c p kc n", kc=2, p=P)
            kv_in = kv_w[:, 0:2 * D].rearrange(col, **colf)
            b_in = b_w_in[0].rearrange(col, **colf)
            b_out = b_w_out[0].rearrange("(i kc p) n -> i p kc n", kc=2, p=P)
            lcol = "l (hf kc p) (c n) -> l c hf p kc n"
            in2 = w_in_2.rearrange(lcol, **colf)
            mkv2 = w_mem_kv_2.rearrange(lcol, **colf)
            pj2 = w_proj_2.rearrange("l (i kc p) n -> l i p kc n", kc=2, p=P)
            wo2 = w_out_2.rearrange("l (i kc p) n -> l i p kc n", kc=2, p=P)
            up2 = w_up_2.rearrange(lcol, **colf)
            dn2 = w_down_2.rearrange("l (c i kc p) n -> l c i p kc n", **row2)
            first_src = {"av": lambda c, i: a_in[NA + c, i], "au": lambda c, i: a_in[c, i],
                         "ad": lambda c, i: a_out[c, i], "fd": lambda c: f_out[c],
                         "kv": lambda c, i: kv_in[c, i], "bi": lambda c, i: b_in[c, i], "bo": lambda i: b_out[i]}
            layer_src = {"in": lambda l, c, i: in2[l, c, i], "mk": lambda l, c, i: mkv2[l, c, i],
                         "pj": lambda l, i: pj2[l, i], "wo": lambda l, i: wo2[l, i],
                         "mu": lambda l, c, i: up2[l, c, i], "md": lambda l, c, i: dn2[l, c, i]}

            def dst(u, source):
                d = raw[:, unit_slot(u), :]
                return d.rearrange("p (kc n) -> p kc n", kc=source.shape[1])

            for u, key in enumerate(FIRST):
                if u >= RING:
                    sp.wait_ge(lo_ready, u + 1 - RING)
                if key[0] == "fu":
                    both = raw[:, unit_slot(u), :].rearrange("p (kc ab n) -> p ab kc n", kc=4, ab=2)
                    for ab in range(2):
                        sp.dma_start(both[:, ab], f_in[key[1], key[2], ab]).then_inc(loaded[unit_slot(u)], 16)
                    continue
                source = first_src[key[0]](*key[1:])
                sp.dma_start(dst(u, source), source).then_inc(loaded[unit_slot(u)], 16)

            up_src = m_w_in[0].rearrange("e (hf kc p) (ab s n) -> e s ab hf p kc n", hf=2, kc=4, p=P, ab=2, n=BANK)
            dn_src = m_w_out[0].rearrange("e (s i kc p) n -> e s i p kc n", i=2, kc=2, p=P)
            sp.wait_ge(lo_ready, N_FIRST)
            sp.wait_ge(r_done, 1)
            sp.sem_inc(e_lo, E_RAW)
            npass = sp.value_load(npass_i[0:1, 0:1], min_val=1, max_val=2)
            with sp.Fori(0, npass) as ps:
                with sp.Fori(0, N_EXP) as e:
                    base = sp.snap((ps * N_EXP + e) * N_EU)
                    for k, key in enumerate(EXPERT):
                        sp.wait_ge(e_lo, base + (k + 1))
                        if key[0] == "up":
                            source = up_src[e, key[1], key[2] // 2, key[2] % 2]
                        else:
                            source = dn_src[e, key[1], key[2]]
                        d = e_raw(k).rearrange("p (kc n) -> p kc n", kc=source.shape[1])
                        sp.dma_start(d, source).then_inc(e_loaded[k % E_RAW], 16)
            with sp.Fori(0, DEPTH) as l:
                sp.wait_ge(e_lo, npass * (N_EXP * N_EU) + E_RAW)
                for key in LAYER:
                    u = UNITS[key]
                    if u == N_FIRST + RING:
                        sp.wait_ge(h_done, l * 2 + 4)
                        sp.dma_start(memr, mem.rearrange("b (t p) d -> p (b t) d", p=P)).then_inc(s_mem, 16)
                    sp.wait_ge(lo_ready, l * N_LAYER + (u + 1 - RING))
                    source = layer_src[key[0]](l, *key[1:])
                    sp.dma_start(dst(u, source), source).then_inc(loaded[unit_slot(u)], 16)
            sp.wait_ge(xr_ready, xr_no("X") + DEPTH * 5)
            sp.dma_start(out.rearrange("b (t p) d -> p (b t) d", p=P), xr[:, :, :]).then_inc(s_out, 16)
            sp.wait_ge(s_out, 16)

        @block.gpsimd
        def _(pool):
            pool.dma_start(cst[:, :], cst_d).then_inc(s_const, 16)
            pool.dma_start(h[:, :, :], x.rearrange("b (t p) d -> p (b t) d", p=P)).then_inc(s_const, 16)
            pool.dma_start(sml[:, :], sml_d).then_inc(s_const, 16)
            pool.dma_start(mask_f, masks_d).then_inc(s_const, 16)
            pool.dma_start(ws, a_w_spatial[0].rearrange("g i j -> i g j")).then_inc(s_wsp, 16)
            pool.dma_start(gv_b, gv_d.partition_broadcast(P)).then_inc(s_gv, 16)
            pool.dma_start(wf[:, :, :], kv_w[:, 2 * D:2 * D + HEADS].rearrange("(kc p) n -> p kc n", p=P)).then_inc(s_wf, 16)
            pool.dma_start(wr[:, :, :], m_w_router[0].rearrange("(kc p) n -> p kc n", p=P)).then_inc(s_wr, 16)
            pool.memset(qz[:, :, :], 0.0).then_inc(s_zero, 1)
            pool.wait_ge(h_done, 3)
            pool.dma_start(gm_b, gm_d.partition_broadcast(P)).then_inc(s_gm, 16)
            pool.wait_ge(h_done, DEPTH * 2 + 4)
            pool.dma_start(gfin, gfin_d.partition_broadcast(P)).then_inc(s_gfin, 16)

        @block.scalar
        def _(act):
            at = [0]

            def hi(u, l=None):
                s = unit_slot(u)
                n = LANDED[u]
                act.wait_ge(loaded[s], n if l is None else l * (N_LAYER // RING * 16) + n)
                if u >= RING:
                    n = u + 1 - RING
                    act.wait_ge(unit_used, n if l is None else l * N_LAYER + n)
                act.activation(w_hi[:, s, :], raw[:, s, :], ACT.Copy).then_inc(hi_ready, 1)

            def ahead(key, l=None):
                end = N_FIRST if l is None else N_FIRST + N_LAYER
                while at[0] < min(UNITS[key] + AHEAD + 1, end):
                    hi(at[0], l)
                    at[0] += 1

            def root(key, n, l=None):
                act.wait_ge(n_var, norm_no(key, l))
                act.activation(sd[:, 0:n], var[:, 0:n], ACT.Sqrt).then_inc(n_sd, 1)

            def split_rows(name, dest, gain, l=None, groups=4, also=None):
                for g in range(groups):
                    act.wait_ge(t_filled, filled((name, g), l))
                    b = T_BANK[name, g]
                    if gain is None:
                        last = act.activation(dest[:, 2 * g:2 * g + 2, :].rearrange("p k n -> p (k n)"), T[:, b, :], ACT.Copy)
                    else:
                        for d, gn in ((dest, gain),) + (also or ()):
                            for i in range(2):
                                kc = 2 * g + i
                                last = act.activation(d[:, kc, :], T[:, b, i * S:(i + 1) * S], ACT.Copy,
                                                      scale=gn[:, kc:kc + 1])
                    last.then_inc(t_split, 1)

            def gains(c):
                return sml[:, c:c + KC]

            def evac(key, dest, func, n, l=None):
                ahead((*key, 1), l)
                act.wait_ge(unit_used, used((*key, 1), l))
                for t in range(NT):
                    last = act.activation(dest(t), pair(n)[t], func)
                last.then_inc(proj_out, 1)

            def hidden(key, func, l=None, width=BANK):
                ahead((*key, 1), l)
                act.wait_ge(unit_used, used((*key, 1), l))
                n = hid(key, l)
                if key != ("au", 0):
                    act.wait_ge(hid_ready, n - 1)
                for t in range(NT):
                    last = act.activation(gu[:, t, 0:width], U[:, t, 0:width], func)
                last.then_inc(hid_act, 1)

            def split_hidden(key, chunks, buf, after, l=None):
                ahead(after, l)
                for b in range(chunks // 2):
                    k = (*key, b) if chunks == 4 else key
                    act.wait_ge(t_filled, filled(k, l))
                    d = t_hi[:, 4 * buf + 2 * b:4 * buf + 2 * b + 2, :]
                    act.activation(d.rearrange("p k n -> p (k n)"), T[:, T_BANK[k], :], ACT.Copy).then_inc(t_split, 1)

            def softmax(items, l=None):
                for i in range(len(items)):
                    t, outs = items[i]
                    act.wait_ge(mx_ready, item_no(i, l))
                    if i >= 1:
                        pT_copy(i - 1, l)
                    at_col = 0
                    for j, (o, tiles) in enumerate(outs):
                        w = len(tiles) * P
                        last = act.activation(p_sb[:, at_col:at_col + w], logit_bank(i)[:, at_col:at_col + w], ACT.Exp,
                                              bias=nmx[:, i % 2, j:j + 1], accum_out=sums[:, t, o:o + 1])
                        at_col += w
                    last.then_inc(p_ready, 1)
                pT_copy(len(items) - 1, l)

            def pT_copy(i, l):
                act.wait_ge(p_turned, item_no(i, l))
                act.activation(pT_sb[:, 0:BANK], U[:, 0, :], ACT.Copy).then_inc(pT_a, 1)

            act.wait_ge(s_const, 64)
            root("A", NT)
            ahead(("av", 0, 0))
            split_rows("nA", x_hi, gains(G_A))
            for c in range(NA):
                evac(("av", c), lambda t: v_a[:, t, c * BANK:(c + 1) * BANK], ACT.Gelu, c)
            root("V", NT)
            for c in range(NA):
                hidden(("au", c), ACT.Gelu)
                split_hidden(("au", c), 4, c % 2, ("au", 0, 1) if c == 0 else ("ad", c - 1, 1))
            ahead(("ad", NA - 1, 1))
            root("F", NT)
            split_rows("nF", x_hi, gains(G_F))
            for c in range(NF):
                hidden(("fu", c), ACT.Silu, width=256)
                split_hidden(("fu", c), 2, c % 2, ("fu", 0, 1) if c == 0 else ("fd", c - 1))
            ahead(("fd", NF - 1))
            root("KV", NT)
            split_rows("nKV", x_hi, gains(G_KV), also=((t_hi, gains(G_B)),))
            for c in range(4):
                dest = k_t if c < 2 else v_t
                evac(("kv", c), lambda t: dest[:, t, c % 2 * BANK:(c % 2 + 1) * BANK], ACT.Copy, c)
            root("K", 2 * HEADS)
            for c in range(4):
                dest = q_t if c < 2 else gate_t
                evac(("bi", c), lambda t: dest[:, t, c % 2 * BANK:(c % 2 + 1) * BANK],
                     ACT.Copy if c < 2 else ACT.Sigmoid, c)
            root("Q", 2 * HEADS)
            act.wait_ge(f_z, 1)
            act.activation(fe[0:HEADS, :], fa[0:HEADS, :], ACT.Exp).then_inc(f_e, 1)
            act.wait_ge(f_z, 2)
            act.activation(fe[0:HEADS, :], fa[0:HEADS, :], ACT.Ln).then_inc(f_e, 1)
            softmax(ITEMS1)
            split_rows("oT", x_hi, None)
            ahead(("bo", 3))
            root("M", NT)
            split_rows("nM", x_hi, None)
            act.wait_ge(r_diff, 1)
            act.activation(gw[:, :, 1:2], gw[:, :, 0:1], ACT.Exp).then_inc(r_exp, 1)
            act.wait_ge(unit_used, N_FIRST)
            act.sem_inc(e_used, RING)
            act.wait_ge(r_done, 1)
            npass = act.value_load(npass_i[0:1, 0:1], min_val=1, max_val=2)
            def gather_hi(b, buf, n):
                act.wait_ge(e_gath, n)
                act.activation(x_hi[:, 4 * b:4 * b + 4, buf * SLOTS:(buf + 1) * SLOTS],
                               Y[:, 3 - b, :].rearrange("p (k n) -> p k n", k=4), ACT.Copy).then_inc(e_ghi, 1)

            def output():
                for n in range(2):
                    last = act.activation(ye[:, n * BANK:(n + 1) * BANK], Y[:, n, :], ACT.Copy)
                last.then_inc(e_y, 1)

            with act.Fori(0, npass) as ps:
                g0 = act.snap(ps * (2 * (N_EXP + 1)))
                for b in range(2):
                    gather_hi(b, 0, g0 + (b + 1))
                with act.Fori(0, N_EXP // 2) as two:
                    n2 = act.snap(ps * (N_EXP // 2) + two)
                    base = act.snap(n2 * (2 * N_EU))
                    ld = act.snap(n2 * (2 * N_EU // E_RAW * 16))
                    step0 = act.snap(n2 * (2 * NS))
                    gath0 = act.snap(g0 + two * 4)
                    for half in range(2):
                        k, u0 = 0, half * N_EU

                        def e_ahead(n):
                            nonlocal k
                            while k < min(n + AHEAD + 1, N_EU):
                                s = unit_slot(k)
                                act.wait_ge(e_loaded[k % E_RAW], ld + ((u0 + k) // E_RAW + 1) * 16)
                                act.wait_ge(e_used, base + (u0 + k + 1))
                                act.activation(w_hi[:, s, :], e_raw(k), ACT.Copy).then_inc(e_hi, 1)
                                k += 1

                        e_ahead(-1)
                        act.wait_ge(e_used, base + (u0 + RING))
                        output()
                        for s in range(NS):
                            e_ahead(EU["up", s, 3])
                            act.wait_ge(e_used, base + (u0 + EU["up", s, 3] + 1 + RING))
                            if s >= 1:
                                act.wait_ge(e_hid, step0 + (half * NS + s))
                            act.activation(gu[:, 0, :], U[:, 0, :], ACT.Silu).then_inc(e_silu, 1)
                            if s >= 1:
                                e_ahead(EU["dn", s - 1, 1])
                            act.wait_ge(e_tf, step0 + (half * NS + s + 1))
                            act.activation(t_hi[:, 4 * (s % 2):4 * (s % 2) + 4, 0:SLOTS],
                                           T[:, s % 2, :].rearrange("p (k n) -> p k n", k=4), ACT.Copy).then_inc(e_thi, 1)
                            if s in (3, 4):
                                gather_hi(s - 3, 1 - half, gath0 + (2 * half + 2 + s - 2))
                        e_ahead(N_EU)
            act.wait_ge(e_used, npass * (N_EXP * N_EU) + RING)
            output()
            with act.Fori(0, DEPTH) as l:
                at[0] = N_FIRST
                root("X", NT, l)
                ahead(("in", 0, 0), l)
                split_rows("nX", x_hi, gcur[:, 0:KC], l)
                root("Mem", NT, l)
                split_rows("nMem", t_hi, gcur[:, KC:2 * KC], l)
                for c in range(NQ):
                    evac(("in", c), lambda t: qkv[:, t, c * BANK:(c + 1) * BANK], ACT.Copy, c, l)
                evac(("mk", 0), lambda t: km[:, t, :], ACT.Copy, NQ, l)
                for c in range(NG):
                    evac(("in", NQ + c), lambda t: gat[:, t, c * BANK:(c + 1) * BANK], ACT.Sigmoid, NQ + 1 + c, l)
                softmax(ITEMS2, l)
                split_rows("oT2", x_hi, None, l, groups=3)
                ahead(("pj", 2), l)
                split_rows("yT", x_hi, None, l)
                ahead(("wo", 3), l)
                root("U", NT, l)
                split_rows("nU", x_hi, gcur[:, 2 * KC:3 * KC], l)
                for c in range(NU):
                    hidden(("mu", c), ACT.Relu, l)
                    split_hidden(("mu", c), 4, c % 2, ("mu", 0, 1) if c == 0 else ("md", c - 1, 1), l)
                ahead(("md", NU - 1, 1), l)
            act.wait_ge(n_var, norm_no("X") + DEPTH * 3)
            act.activation(sd[:, 0:NT], var[:, 0:NT], ACT.Sqrt).then_inc(n_sd, 1)

        @block.vector
        def _(dve):
            at = [0]
            steps = [0, None]

            def order(ins):
                steps[0] += 1
                ins.then_inc(v_step, 1)
                dve.wait_ge(v_step, steps[0] if steps[1] is None else steps[1] + steps[0])

            def lo(u, l=None):
                s = unit_slot(u)
                dve.wait_ge(hi_ready, u + 1 if l is None else l * N_LAYER + (u + 1))
                dve.tensor_tensor(w_lo[:, s, :], raw[:, s, :], w_hi[:, s, :].bitcast(F32), ALU.subtract).then_inc(lo_ready, 1)

            def ahead(key, l=None):
                end = N_FIRST if l is None else N_FIRST + N_LAYER
                while at[0] < min(UNITS[key] + AHEAD + 1, end):
                    lo(at[0], l)
                    at[0] += 1

            def row_scale(src, l=None, key=None):
                for t in range(NT):
                    last = dve.scalar_tensor_tensor(xr[:, t, :], src[:, t, :], 1.0, src[:, t, :], ALU.mult, ALU.mult,
                                                    accum_out=ss[:, t:t + 1])
                order(last)
                dve.tensor_scalar(var[:, 0:NT], ss[:, 0:NT], 1.0 / D, EPS, ALU.mult, ALU.add).then_inc(n_var, 1)
                inverse(NT, key, l)

            def inverse(n, key, l=None):
                dve.wait_ge(n_sd, norm_no(key, l))
                refine(n)

            def refine(n):
                order(dve.reciprocal(rs[:, 0:n], sd[:, 0:n]))
                order(dve.tensor_tensor(sd[:, 0:n], rs[:, 0:n], rs[:, 0:n], ALU.mult))
                order(dve.tensor_tensor(sd[:, 0:n], sd[:, 0:n], var[:, 0:n], ALU.mult))
                order(dve.tensor_scalar(sd[:, 0:n], sd[:, 0:n], -0.5, 1.5, ALU.mult, ALU.add))
                order(dve.tensor_tensor(rs[:, 0:n], rs[:, 0:n], sd[:, 0:n], ALU.mult))

            def norm(key, l=None):
                row_scale(h, l, key)
                for t in range(NT):
                    last = dve.tensor_scalar(xr[:, t, :], h[:, t, :], rs[:, t:t + 1], None, ALU.mult)
                last.then_inc(xr_ready, 1)

            def split_rows(name, hi_d, lo_d, gain, l=None, groups=4, also=None):
                for g in range(groups):
                    dve.wait_ge(t_split, split((name, g), l))
                    b = T_BANK[name, g]
                    if gain is None:
                        sl = slice(2 * g, 2 * g + 2)
                        last = dve.tensor_tensor(lo_d[:, sl, :].rearrange("p k n -> p (k n)"), T[:, b, :],
                                                 hi_d[:, sl, :].rearrange("p k n -> p (k n)").bitcast(F32), ALU.subtract)
                    else:
                        for hd, ld, gn in ((hi_d, lo_d, gain),) + (also or ()):
                            for i in range(2):
                                kc = 2 * g + i
                                last = dve.scalar_tensor_tensor(ld[:, kc, :], T[:, b, i * S:(i + 1) * S], gn[:, kc:kc + 1],
                                                                hd[:, kc, :].bitcast(F32), ALU.mult, ALU.subtract)
                    last.then_inc(t_done, 1)

            def gains(c):
                return sml[:, c:c + KC]

            def gated(key, other, l=None, width=BANK):
                ahead((*key, 1), l)
                dve.wait_ge(hid_act, hid(key, l))
                for t in range(NT):
                    last = dve.tensor_tensor(pr[:, t, 0:width], gu[:, t, 0:width], other(t), ALU.mult)
                last.then_inc(hid_ready, 1)

            def split_hidden(key, chunks, buf, after, l=None):
                ahead(after, l)
                for b in range(chunks // 2):
                    k = (*key, b) if chunks == 4 else key
                    dve.wait_ge(t_split, split(k, l))
                    sl = slice(4 * buf + 2 * b, 4 * buf + 2 * b + 2)
                    dve.tensor_tensor(t_lo[:, sl, :].rearrange("p k n -> p (k n)"), T[:, T_BANK[k], :],
                                      t_hi[:, sl, :].rearrange("p k n -> p (k n)").bitcast(F32),
                                      ALU.subtract).then_inc(t_done, 1)

            def add_residual(key, l=None):
                ahead(key, l)
                dve.wait_ge(unit_used, used(key, l))
                for t in range(NT):
                    for n in range(2):
                        hs = h[:, t, n * BANK:(n + 1) * BANK]
                        last = dve.tensor_tensor(hs, hs, Y[:, 2 * t + n, :], ALU.add)
                last.then_inc(h_done, 1)

            def after_h(n):
                dve.wait_ge(h_done, n)

            def softmax(items, finish, l=None):
                for i in range(len(items) + 1):
                    if i < len(items):
                        t, outs = items[i]
                        w = len(outs[0][1]) * P
                        dve.wait_ge(l_filled, item_no(i, l))
                        dve.tensor_reduce(nmx[:, i % 2, 0:len(outs)],
                                          logit_bank(i)[:, 0:len(outs) * w].rearrange("p (o w) -> p o w", w=w),
                                          AX.X, ALU.max, negate=True).then_inc(mx_ready, 1)
                    if i >= 1:
                        t, outs = items[i - 1]
                        n = sum(len(o[1]) for o in outs) * P
                        dve.wait_ge(p_turned, item_no(i - 1, l))
                        dve.tensor_copy(pT_sb[:, BANK:n], U[:, 1, 0:n - BANK]).then_inc(pT_v, 1)
                        if i == len(items) or items[i][0] != t:
                            dve.wait_ge(pv_done, item_no(i - 1, l))
                            finish(t)

            def over_sums(t, n):
                order(dve.reciprocal(rsum[:, t, 0:n], sums[:, t, 0:n]))
                return dve.tensor_tensor(xr[:, t, 0:n * HD].rearrange("p (o d) -> p o d", d=HD),
                                         o_bank[:, 0:n * HD].rearrange("p (o d) -> p o d", d=HD),
                                         rsum[:, t, 0:n].unsqueeze(2).to_broadcast([P, n, HD]), ALU.mult)

            dve.wait_ge(s_const, 64)
            dve.tensor_copy(identb[:, :], ident).then_inc(s_bf, 1)
            dve.tensor_copy(maskb[:, :, :].rearrange("p m n -> p (m n)"), mask_f).then_inc(s_bf, 1)
            norm("A")
            for i in range(2):
                dve.wait_ge(t_filled, filled(("wsT", i)))
                last = dve.tensor_copy(wsT[:, 4 * i:4 * i + 4, :].rearrange("p g n -> p (g n)"), T[:, T_BANK["wsT", i], :])
                last.then_inc(t_done, 1)
            dve.wait_ge(t_done, filled(("wsT", 1)))
            dve.memset(wsT[HD:P, :, 0:HD], 0.0)
            ahead(("av", 0, 0))
            split_rows("nA", x_hi, x_lo, gains(G_A))
            for c in range(NA):
                ahead(("av", c, 1))
                dve.wait_ge(proj_out, proj(("av", c)))
                for t in range(NT):
                    vs = v_a[:, t, c * BANK:(c + 1) * BANK]
                    last = dve.scalar_tensor_tensor(pr[:, t, :], vs, 1.0, vs, ALU.mult, ALU.mult,
                                                    accum_out=ssv[:, t, c:c + 1])
                order(last)
            order(dve.tensor_reduce(ss[:, :], ssv[:, :, :], AX.X, ALU.add))
            dve.tensor_scalar(var[:, 0:NT], ss[:, :], 1.0 / A_HALF, EPS, ALU.mult, ALU.add).then_inc(n_var, 1)
            inverse(NT, "V")
            dve.wait_ge(s_gv, 16)
            for t in range(NT):
                dve.scalar_tensor_tensor(v_a[:, t, :], v_a[:, t, :], rs[:, t:t + 1], gv_b, ALU.mult, ALU.mult).then_inc(v_ready, 1)
            for j in range(NT * A_GROUPS):
                t, g = j // A_GROUPS, j % A_GROUPS
                dve.wait_ge(t_filled, filled(("sp", j)))
                last = dve.tensor_scalar(v_a[:, t, g * A_GD:(g + 1) * A_GD], T[:, T_BANK["sp", j], 0:A_GD],
                                         sml[:, G_BT + g:G_BT + g + 1], None, ALU.add)
                last.then_inc(t_done, 1)
            dve.wait_ge(t_done, filled(("sp", NT * A_GROUPS - 1)))
            for c in range(NA):
                gated(("au", c), lambda t: v_a[:, t, c * BANK:(c + 1) * BANK])
                split_hidden(("au", c), 4, c % 2, ("au", 0, 1) if c == 0 else ("ad", c - 1, 1))
            add_residual(("ad", NA - 1, 1))
            after_h(1)
            norm("F")
            split_rows("nF", x_hi, x_lo, gains(G_F))
            for c in range(NF):
                gated(("fu", c), lambda t: U[:, t, 256:512], width=256)
                split_hidden(("fu", c), 2, c % 2, ("fu", 0, 1) if c == 0 else ("fd", c - 1))
            add_residual(("fd", NF - 1))
            after_h(2)
            norm("KV")
            split_rows("nKV", x_hi, x_lo, gains(G_KV), also=((t_hi, t_lo, gains(G_B)),))
            dve.tensor_copy(sel, ident[:, 0:HEADS].unsqueeze(2).to_broadcast([P, HEADS, P]))

            def head_norm(rows, key):
                for t in range(NT):
                    order(dve.tensor_tensor(sq_t[:, t, :], rows[:, t, :], rows[:, t, :], ALU.mult))
                    last = dve.tensor_reduce(var[:, t * HEADS:(t + 1) * HEADS],
                                             sq_t[:, t, :].rearrange("p (o d) -> p o d", d=HD), AX.X, ALU.add)
                order(last)
                dve.tensor_scalar(var[:, :], var[:, :], 1.0 / HD, EPS, ALU.mult, ALU.add).then_inc(n_var, 1)
                inverse(2 * HEADS, key)
                for t in range(NT):
                    r3 = rows[:, t, :].rearrange("p (o d) -> p o d", d=HD)
                    last = dve.tensor_tensor(r3, r3, rs[:, t * HEADS:(t + 1) * HEADS].unsqueeze(2).to_broadcast([P, HEADS, HD]),
                                             ALU.mult)
                last.then_inc(v_ready, 1)

            ahead(("kv", 2, 1))
            dve.wait_ge(proj_out, proj(("kv", 1)))
            head_norm(k_t, "K")
            ahead(("bi", 2, 1))
            dve.wait_ge(proj_out, proj(("bi", 1)))
            head_norm(q_t, "Q")
            ahead(("bi", 3, 1))
            order(dve.memset(sq_t[:, :, :], 0.0))
            dve.wait_ge(t_filled, filled(("fT", 0)))
            ins = dve.tensor_scalar(fz[0:HEADS, :], T[0:HEADS, 0, 0:S], sml[0:HEADS, G_BF:G_BF + 1], None, ALU.add)
            ins.then_inc(t_done, 1)
            dve.wait_ge(t_done, filled(("fT", 0)))
            order(dve.tensor_scalar(fe[0:HEADS, :], fz[0:HEADS, :], -1.0, None, ALU.mult))
            dve.tensor_tensor(fa[0:HEADS, :], fe[0:HEADS, :], fz[0:HEADS, :], ALU.min).then_inc(f_z, 1)
            dve.wait_ge(f_e, 1)
            dve.tensor_scalar(fa[0:HEADS, :], fe[0:HEADS, :], 1.0, None, ALU.add).then_inc(f_z, 1)
            dve.wait_ge(f_e, 2)
            order(dve.scalar_tensor_tensor(fa[0:HEADS, :], fz[0:HEADS, :], 0.0, fe[0:HEADS, :], ALU.min, ALU.subtract))
            dve.tensor_tensor_scan(ncum[0:HEADS, :], ones2[0:HEADS, :], fa[0:HEADS, :], 0.0, ALU.mult, ALU.subtract).then_inc(ncum_ready, 1)
            for g in range(4):
                dve.wait_ge(t_filled, filled(("kT", g)))
                dve.tensor_scalar(kT[:, 2 * g:2 * g + 2, :].rearrange("p k n -> p (k n)"), T[:, T_BANK["kT", g], :],
                                  sml[:, G_K:G_K + 1], None, ALU.mult).then_inc(t_done, 1)
            dve.wait_ge(s_zero, 1)
            for g in range(4):
                dve.wait_ge(t_filled, filled(("qT", g)))
                for half in range(2):
                    r = slice(half * HD, (half + 1) * HD)
                    last = dve.tensor_scalar(qz[r, 4 * g + half:4 * g + 4:2, :],
                                             T[r, T_BANK["qT", g], :].rearrange("p (k n) -> p k n", k=2),
                                             sml[r, G_Q:G_Q + 1], HD ** -0.5, ALU.mult, ALU.mult)
                last.then_inc(t_done, 1)

            def finish1(t):
                order(over_sums(t, HEADS))
                dve.wait_ge(proj_out, proj(("bi", 3)))
                dve.tensor_tensor(xr[:, t, :], xr[:, t, :], gate_t[:, t, :], ALU.mult).then_inc(o_done, 1)

            softmax(ITEMS1, finish1)
            dve.wait_ge(o_done, o_no(1))
            dve.sem_inc(xr_ready, 1)
            split_rows("oT", x_hi, x_lo, None)
            add_residual(("bo", 3))
            after_h(3)
            row_scale(h, None, "M")
            dve.wait_ge(s_gm, 16)
            for t in range(NT):
                last = dve.scalar_tensor_tensor(xr[:, t, :], h[:, t, :], rs[:, t:t + 1], gm_b, ALU.mult, ALU.mult)
            last.then_inc(xr_ready, 1)
            split_rows("nM", x_hi, x_lo, None)
            dve.wait_ge(r_logits, 1)
            order(dve.tensor_copy(lg, U[:, :, 0:N_EXP]))
            for t in range(NT):
                last = dve.max(mx8[:, t, :], lg[:, t, :])
            order(last)
            for t in range(NT):
                last = dve.max_index(mi8[:, t, :], mx8[:, t, :], lg[:, t, :])
            order(last)
            dve.tensor_tensor(gw[:, :, 0:1], mx8[:, :, 1:2], mx8[:, :, 0:1], ALU.subtract).then_inc(r_diff, 1)
            order(dve.tensor_copy(mif, mi8))
            for t in range(NT):
                last = dve.tensor_scalar(one1[:, t, :], iota8, mif[:, t, 0:1], None, ALU.is_equal)
            order(last)
            for t in range(NT):
                last = dve.scalar_tensor_tensor(chosen[:, t, :], iota8, mif[:, t, 1:2], one1[:, t, :], ALU.is_equal, ALU.add)
            last.then_inc(r_chosen, 1)
            dve.wait_ge(r_exp, 1)
            order(dve.tensor_scalar(gw[:, :, 2:3], gw[:, :, 1:2], 1.0, None, ALU.add))
            order(dve.reciprocal(gw[:, :, 2:3], gw[:, :, 2:3]))
            order(dve.tensor_tensor(gw[:, :, 3:4], gw[:, :, 1:2], gw[:, :, 2:3], ALU.mult))
            for t in range(NT):
                dve.tensor_scalar(gate1[:, t, :], iota8, mif[:, t, 0:1], gw[:, t, 2:3], ALU.is_equal, ALU.mult)
                last = dve.tensor_scalar(gate2[:, t, :], iota8, mif[:, t, 1:2], gw[:, t, 3:4], ALU.is_equal, ALU.mult)
            order(last)
            order(dve.memset(gates, 0.0))
            dve.memset(place, -1.0)
            dve.memset(comb, 0.0).then_inc(e_comb, 1)
            order(dve.tensor_tensor(gates[:, :, 0:N_EXP], gate1, gate2, ALU.add))
            dve.wait_ge(r_place, 1)
            order(dve.scalar_tensor_tensor(place[:, :, 0:N_EXP], U[:, :, 16:16 + N_EXP], 1.0, chosen, ALU.add, ALU.mult))
            dve.tensor_scalar(place[:, :, 0:N_EXP], place[:, :, 0:N_EXP], -1.0, None, ALU.add)
            order(dve.tensor_reduce(most[:, 0:1], U[:, 0, 32:32 + N_EXP], AX.X, ALU.max))
            order(dve.tensor_scalar(most[:, 1:2], most[:, 0:1], SLOTS + 0.5, 1.0, ALU.is_gt, ALU.add))
            dve.tensor_copy(npass_i[:, :], most[:, 1:2]).then_inc(r_done, 1)
            dve.wait_ge(r_done, 1)
            npass = dve.value_load(npass_i[0:1, 0:1], min_val=1, max_val=2)

            def dispatch(e):
                for t in range(NT):
                    col = place[:, t, bass.ds(e, 1)]
                    dve.tensor_scalar(disp[:, t, :], iota, col, None, ALU.is_equal)
                    last = dve.tensor_scalar(dispg[:, t, :], iota, col, gates[:, t, bass.ds(e, 1)], ALU.is_equal, ALU.mult)
                last.then_inc(e_disp, 1)

            def gather_lo(b, buf, n):
                dve.wait_ge(e_ghi, n)
                sl = slice(buf * SLOTS, (buf + 1) * SLOTS)
                dve.tensor_tensor(x_lo[:, 4 * b:4 * b + 4, sl], Y[:, 3 - b, :].rearrange("p (k n) -> p k n", k=4),
                                  x_hi[:, 4 * b:4 * b + 4, sl].bitcast(F32), ALU.subtract).then_inc(e_glo, 1)

            def put_back(j, n, banks):
                dve.wait_ge(e_scat, n)
                hs = h[:, j // 2, j % 2 * BANK:(j % 2 + 1) * BANK]
                dve.tensor_tensor(hs, hs, banks[j], ALU.add).then_inc(e_add, 1)

            in_loop = [Y[:, 2, :], Y[:, 3, :], Y[:, 2, :], Y[:, 3, :]]
            with dve.Fori(0, npass) as ps:
                g0 = dve.snap(ps * (2 * (N_EXP + 1)))
                dispatch(0)
                for b in range(2):
                    gather_lo(b, 0, g0 + (b + 1))
                with dve.Fori(0, N_EXP // 2) as two:
                    n2 = dve.snap(ps * (N_EXP // 2) + two)
                    base = dve.snap(n2 * (2 * N_EU))
                    step0 = dve.snap(n2 * (2 * NS))
                    scat0 = dve.snap(n2 * (2 * E_SCAT))
                    turn0 = dve.snap(n2 * 2)
                    gath0 = dve.snap(g0 + two * 4)
                    for half in range(2):
                        k, u0 = 0, half * N_EU

                        def e_ahead(n):
                            nonlocal k
                            while k < min(n + AHEAD + 1, N_EU):
                                s = unit_slot(k)
                                dve.wait_ge(e_hi, base + (u0 + k + 1))
                                dve.tensor_tensor(w_lo[:, s, :], e_raw(k), w_hi[:, s, :].bitcast(F32), ALU.subtract).then_inc(e_lo, 1)
                                k += 1

                        e_ahead(-1)
                        for s in range(NS):
                            e_ahead(EU["up", s, 3])
                            dve.wait_ge(e_silu, step0 + (half * NS + s + 1))
                            dve.tensor_tensor(pr[:, 0, :], gu[:, 0, :], U[:, 1, :], ALU.mult).then_inc(e_hid, 1)
                            if s >= 1:
                                e_ahead(EU["dn", s - 1, 1])
                            dve.wait_ge(e_thi, step0 + (half * NS + s + 1))
                            sl = slice(4 * (s % 2), 4 * (s % 2) + 4)
                            dve.tensor_tensor(t_lo[:, sl, 0:SLOTS], T[:, s % 2, :].rearrange("p (k n) -> p k n", k=4),
                                              t_hi[:, sl, 0:SLOTS].bitcast(F32), ALU.subtract).then_inc(e_tlo, 1)
                            if s < 2:
                                for j in (2 * s, 2 * s + 1):
                                    put_back(j, scat0 + (half * E_SCAT + j + 1), in_loop)
                            if s == 2:
                                dve.wait_ge(e_turn, turn0 + (half + 1))
                                dve.tensor_copy(comb, Y[:, 2, 0:S]).then_inc(e_comb, 1)
                                dispatch(two * 2 + (half + 1))
                            if s in (3, 4):
                                gather_lo(s - 3, 1 - half, gath0 + (2 * half + 2 + s - 2))
                        e_ahead(N_EU)
                dve.tensor_scalar(place, place, -float(SLOTS), None, ALU.add).then_inc(e_pass, 1)
                dve.wait_ge(e_pass, ps + 1)
            for j in range(E_SCAT):
                put_back(j, npass * (N_EXP * E_SCAT) + (j + 1), [Y[:, 2, :], Y[:, 3, :], U[:, 0, :], U[:, 1, :]])
            dve.wait_ge(e_add, npass * (N_EXP * E_SCAT) + E_SCAT)
            dve.sem_inc(h_done, 1)
            first_steps = steps[0]
            with dve.Fori(0, DEPTH) as l:
                at[0] = N_FIRST
                steps[0], steps[1] = 0, dve.snap(l * V_STEPS_LAYER + first_steps)
                dve.tensor_copy(gcur[:, :], sml[:, bass.ds(l * (3 * KC) + G_L, 3 * KC)])
                norm("X", l)
                ahead(("in", 0, 0), l)
                split_rows("nX", x_hi, x_lo, gcur[:, 0:KC], l)
                dve.wait_ge(s_mem, l * 16 + 16)
                row_scale(memr, l, "Mem")
                for t in range(NT):
                    last = dve.tensor_scalar(memr[:, t, :], memr[:, t, :], rs[:, t:t + 1], None, ALU.mult)
                last.then_inc(xr_ready, 1)
                split_rows("nMem", t_hi, t_lo, gcur[:, KC:2 * KC], l)
                ahead(("mk", 0, 1), l)
                dve.wait_ge(proj_out, proj(("in", NQ - 1), l))
                for t in range(NT):
                    heads = qkv[:, t, 0:6 * W_A].rearrange("p (g z) -> p g z", g=2)[:, :, 0:2 * W_A]\
                        .rearrange("p g (h d) -> p g h d", d=HD)
                    x1, x2 = heads[:, :, :, 0:ROT], heads[:, :, :, ROT:2 * ROT]
                    shape = [P, 2, 12, ROT]
                    cs = cst[:, C_COS + t * ROT:C_COS + (t + 1) * ROT].unsqueeze(1).unsqueeze(1).to_broadcast(shape)
                    sn = cst[:, C_SIN + t * ROT:C_SIN + (t + 1) * ROT].unsqueeze(1).unsqueeze(1).to_broadcast(shape)
                    for f, (a, b) in enumerate(((x1, cs), (x2, sn), (x2, cs), (x1, sn))):
                        last = dve.tensor_tensor(rot[:, f], a, b, ALU.mult)
                    order(last)
                    dve.tensor_tensor(x1, rot[:, 0], rot[:, 1], ALU.subtract)
                    last = dve.tensor_tensor(x2, rot[:, 2], rot[:, 3], ALU.add)
                    if t == 0:
                        order(last)
                last.then_inc(v_ready, 1)
                ahead(("in", NQ + NG - 1, 1), l)
                for g in range(4):
                    dve.wait_ge(t_filled, filled(("qT2", g), l))
                    for half in range(2):
                        r = slice(half * HD, (half + 1) * HD)
                        last = dve.tensor_scalar(qz[r, 4 * g + half:4 * g + 4:2, :],
                                                 T[r, T_BANK["qT2", g], :].rearrange("p (k n) -> p k n", k=2),
                                                 HD ** -0.5, None, ALU.mult)
                    last.then_inc(t_done, 1)
                for g in range(4):
                    dve.wait_ge(t_filled, filled(("kT2", g), l))
                    dve.tensor_copy(kT[:, 2 * g:2 * g + 2, :].rearrange("p k n -> p (k n)"),
                                    T[:, T_BANK["kT2", g], :]).then_inc(t_done, 1)

                def finish2(t):
                    over_sums(t, H_A + H_B + H_M).then_inc(o_done, 1)

                softmax(ITEMS2, finish2, l)
                dve.wait_ge(o_done, o_no(1, l))
                dve.sem_inc(xr_ready, 1)
                split_rows("oT2", x_hi, x_lo, None, l, groups=3)
                ahead(("pj", 2), l)
                dve.wait_ge(proj_out, proj(("in", NQ + NG - 1), l))
                for br in range(3):
                    dve.wait_ge(unit_used, used(("pj", br), l))
                    for t in range(NT):
                        for n in range(2):
                            gs = gat[:, t, br * D + n * BANK:br * D + (n + 1) * BANK]
                            src = Y[:, 2 * t + n, :] if br != 1 else (U[:, n, :] if t == 0 else T[:, n, :])
                            last = dve.tensor_tensor(gs, gs, src, ALU.mult)
                    last.then_inc(branch, 1)
                dve.wait_ge(branch, l * 3 + 3)
                for t in range(NT):
                    last = dve.tensor_tensor(xr[:, t, :], gat[:, t, 0:D], gat[:, t, D:2 * D], ALU.add)
                order(last)
                for t in range(NT):
                    last = dve.tensor_tensor(xr[:, t, :], xr[:, t, :], gat[:, t, 2 * D:3 * D], ALU.add)
                last.then_inc(xr_ready, 1)
                split_rows("yT", x_hi, x_lo, None, l)
                add_residual(("wo", 3), l)
                after_h(l * 2 + 5)
                norm("U", l)
                split_rows("nU", x_hi, x_lo, gcur[:, 2 * KC:3 * KC], l)
                for c in range(NU):
                    gated(("mu", c), lambda t: gu[:, t, :], l)
                    split_hidden(("mu", c), 4, c % 2, ("mu", 0, 1) if c == 0 else ("md", c - 1, 1), l)
                add_residual(("md", NU - 1, 1), l)
                after_h(l * 2 + 6)
                assert steps[0] == V_STEPS_LAYER, steps
            steps[0], steps[1] = first_steps + DEPTH * V_STEPS_LAYER, None
            for t in range(NT):
                last = dve.scalar_tensor_tensor(xr[:, t, :], h[:, t, :], 1.0, h[:, t, :], ALU.mult, ALU.mult,
                                                accum_out=ss[:, t:t + 1])
            order(last)
            dve.tensor_scalar(var[:, 0:NT], ss[:, 0:NT], 1.0 / D, EPS, ALU.mult, ALU.add).then_inc(n_var, 1)
            dve.wait_ge(n_sd, norm_no("X") + DEPTH * 3)
            refine(NT)
            dve.wait_ge(s_gfin, 16)
            for t in range(NT):
                last = dve.scalar_tensor_tensor(xr[:, t, :], h[:, t, :], rs[:, t:t + 1], gfin, ALU.mult, ALU.mult)
            last.then_inc(xr_ready, 1)

        @block.tensor
        def _(pe):
            def products(acc, a_hi, a_lo, b_hi, b_lo, first, last):
                pe.matmul(acc, a_hi, b_hi, start=first, stop=False)
                pe.matmul(acc, a_lo, b_hi, start=False, stop=False)
                return pe.matmul(acc, a_hi, b_lo, start=False, stop=last)

            def up(key, banks, a_hi, a_lo, l=None):
                for hf in range(2):
                    u = UNITS[(*key, hf)]
                    s = unit_slot(u)
                    pe.wait_ge(lo_ready, used((*key, hf), l))
                    for t in range(NT):
                        for q in range(4):
                            kc = 4 * hf + q
                            w = slice(q * BANK, (q + 1) * BANK)
                            tok = slice(t * P, (t + 1) * P)
                            last = products(banks[t], a_hi[:, kc, tok], a_lo[:, kc, tok], w_hi[:, s, w], w_lo[:, s, w],
                                            kc == 0, kc == KC - 1)
                    last.then_inc(unit_used, 1)

            def down(key, a_hi, a_lo, first, final, l=None, banks=None):
                u = UNITS[key]
                s = unit_slot(u)
                pe.wait_ge(lo_ready, used(key, l))
                for q in range(2):
                    for t in range(NT):
                        for n in range(2):
                            w = slice(q * D + n * BANK, q * D + (n + 1) * BANK)
                            tok = slice(t * P, (t + 1) * P)
                            last = products(Y[:, 2 * t + n, :], a_hi[:, q, tok], a_lo[:, q, tok], w_hi[:, s, w], w_lo[:, s, w],
                                            first and q == 0, final and q == 1)
                last.then_inc(unit_used, 1)

            def fill(key, l=None):
                prev = T_PREV[key]
                if prev is not None:
                    pe.wait_ge(t_done, filled(prev, l))
                return T[:, T_BANK[key], :]

            def turn_rows(name, rows, l=None, groups=4, xr_key=None):
                pe.wait_ge(xr_ready, xr_no(xr_key, l))
                for g in range(groups):
                    bank = fill((name, g), l)
                    for i in range(2):
                        for t in range(NT):
                            c = (2 * g + i) * P
                            last = pe.transpose(bank[:, i * S + t * P:i * S + (t + 1) * P], rows[:, t, c:c + P], ident)
                    last.then_inc(t_filled, 1)

            def turn_hidden(key, chunks, l=None):
                pe.wait_ge(hid_ready, hid(key, l))
                for b in range(chunks // 2):
                    k = (*key, b) if chunks == 4 else key
                    bank = fill(k, l)
                    for i in range(2):
                        for t in range(NT):
                            c = (2 * b + i) * P
                            last = pe.transpose(bank[:, i * S + t * P:i * S + (t + 1) * P], pr[:, t, c:c + P], ident)
                    last.then_inc(t_filled, 1)

            def project(key, n, a_hi, a_lo, l=None):
                if n >= 2:
                    pe.wait_ge(proj_out, proj(key, l) - 2)
                up(key, pair(n), a_hi, a_lo, l)

            def mlp(name, dname, n_chunks, chunks, per, l=None):
                def downs(c):
                    last_fill = (name, c, chunks // 2 - 1) if chunks == 4 else (name, c)
                    pe.wait_ge(t_done, filled(last_fill, l))
                    for i in range(per):
                        sl = slice(4 * (c % 2) + 2 * i, 4 * (c % 2) + 2 * i + 2)
                        key = (dname, c, i) if per == 2 else (dname, c)
                        down(key, t_hi[:, sl, :], t_lo[:, sl, :], c == 0 and i == 0, c == n_chunks - 1 and i == per - 1, l)

                for c in range(n_chunks):
                    if c >= 1:
                        pe.wait_ge(hid_ready, hid((name, c - 1), l))
                    up((name, c), pair(0), x_hi, x_lo, l)
                    if name == "au" and c == 0:
                        spatial()
                    if c >= 1:
                        downs(c - 1)
                    turn_hidden((name, c), chunks, l)
                downs(n_chunks - 1)

            def spatial():
                for j in range(NT * A_GROUPS):
                    t, g = j // A_GROUPS, j % A_GROUPS
                    pe.wait_ge(v_ready, t + 1)
                    bank = fill(("sp", j))
                    pe.matmul(bank[:, 0:A_GD], wsT[:, g, :], v_a[:, t, g * A_GD:(g + 1) * A_GD], start=True, stop=True)\
                        .then_inc(t_filled, 1)

            def softmax(items, value, l=None):
                def logits(i):
                    if i >= 2:
                        pe.wait_ge(p_ready, item_no(i - 2, l))
                    c = 0
                    for o, tiles in items[i][1]:
                        for head, kp, kt, v, mask, forget in tiles:
                            dst = logit_bank(i)[:, c:c + P]
                            q = qz[:, head, items[i][0] * P:(items[i][0] + 1) * P]
                            keys = slice(kt * P, (kt + 1) * P)
                            last = pe.matmul(dst, q, kT[:, kp, keys], start=True, stop=forget is None and mask is None)
                            if forget is not None:
                                last = pe.matmul(dst, sel[:, forget, :], ncum[:, keys], start=False, stop=mask is None)
                            if mask is not None:
                                last = pe.matmul(dst, identb[:, :], maskb[:, mask, :], start=False, stop=True)
                            c += P
                    last.then_inc(l_filled, 1)

                logits(0)
                for i in range(len(items)):
                    t, outs = items[i]
                    if i + 1 < len(items):
                        logits(i + 1)
                    pe.wait_ge(p_ready, item_no(i, l))
                    n = sum(len(tiles) for _, tiles in outs)
                    for j in range(n):
                        last = pe.transpose(U[:, j // 4, j % 4 * P:(j % 4 + 1) * P], p_sb[:, j * P:(j + 1) * P], ident)
                    last.then_inc(p_turned, 1)
                    pe.wait_ge(pT_a, item_no(i, l))
                    pe.wait_ge(pT_v, item_no(i, l))
                    if i >= 1 and items[i - 1][0] != t:
                        pe.wait_ge(o_done, o_no(t - 1, l))
                    j = 0
                    for o, tiles in outs:
                        for m, tile in enumerate(tiles):
                            last = pe.matmul(o_bank[:, o * HD:(o + 1) * HD], pT_sb[:, j * P:(j + 1) * P], value(tile),
                                             start=m == 0, stop=m == len(tiles) - 1)
                            j += 1
                    last.then_inc(pv_done, 1)

            pe.wait_ge(s_const, 64)
            pe.wait_ge(s_wsp, 16)
            for i in range(2):
                bank = fill(("wsT", i))
                for q in range(4):
                    last = pe.transpose(bank[:, q * P:(q + 1) * P], ws[:, 4 * i + q, :], ident)
                last.then_inc(t_filled, 1)
            turn_rows("nA", xr, xr_key="A")
            pe.wait_ge(t_done, filled(("nA", 3)))
            for c in range(NA):
                project(("av", c), c, x_hi, x_lo)
            pe.wait_ge(proj_out, proj(("av", NA - 1)))
            mlp("au", "ad", NA, 4, 2)
            turn_rows("nF", xr, xr_key="F")
            pe.wait_ge(t_done, filled(("nF", 3)))
            mlp("fu", "fd", NF, 2, 1)
            turn_rows("nKV", xr, xr_key="KV")
            pe.wait_ge(t_done, filled(("nKV", 3)))
            for c in range(4):
                project(("kv", c), c, x_hi, x_lo)
            pe.wait_ge(s_wf, 16)
            bank = fill(("fT", 0))
            for n, part in enumerate((x_hi, x_lo)):
                for kc in range(KC):
                    last = pe.matmul(bank[0:HEADS, 0:S], wf[:, kc, :], part[:, kc, :].bitcast(F32),
                                     start=n == 0 and kc == 0, stop=n == 1 and kc == KC - 1)
            last.then_inc(t_filled, 1)
            for c in range(4):
                if c < 2:
                    pe.wait_ge(proj_out, proj(("kv", c + 2)))
                project(("bi", c), c, t_hi, t_lo)
            pe.wait_ge(v_ready, NT + 1)
            for name, rows, n in (("kT", k_t, 1), ("qT", q_t, 2)):
                pe.wait_ge(v_ready, NT + n)
                for g in range(4):
                    bank = fill((name, g))
                    for i in range(2):
                        for t in range(NT):
                            c = (2 * g + i) * P
                            last = pe.transpose(bank[:, i * S + t * P:i * S + (t + 1) * P], rows[:, t, c:c + P], ident)
                    last.then_inc(t_filled, 1)
            pe.wait_ge(t_done, filled(("qT", 3)))
            pe.wait_ge(proj_out, proj(("bi", 3)))
            pe.wait_ge(ncum_ready, 1)
            pe.wait_ge(s_bf, 2)
            softmax(ITEMS1, lambda tile: v_t[:, tile[2], tile[3][1] * HD:(tile[3][1] + 1) * HD])
            pe.wait_ge(o_done, o_no(1))
            turn_rows("oT", xr, xr_key="O")
            pe.wait_ge(t_done, filled(("oT", 3)))
            for i in range(4):
                down(("bo", i), x_hi[:, 2 * i:2 * i + 2, :], x_lo[:, 2 * i:2 * i + 2, :], i == 0, i == 3)
            turn_rows("nM", xr, xr_key="M")
            pe.wait_ge(t_done, filled(("nM", 3)))
            pe.wait_ge(s_wr, 16)
            for t in range(NT):
                for n, part in enumerate((x_hi, x_lo)):
                    for kc in range(KC):
                        last = pe.matmul(U[:, t, 0:N_EXP], part[:, kc, t * P:(t + 1) * P].bitcast(F32), wr[:, kc, :],
                                         start=n == 0 and kc == 0, stop=n == 1 and kc == KC - 1)
            last.then_inc(r_logits, 1)
            pe.wait_ge(r_chosen, 1)
            pe.matmul(U[:, 0, 16:16 + N_EXP], tri, chosen[:, 0, :], start=True, stop=True)
            pe.matmul(U[:, 1, 16:16 + N_EXP], ones, chosen[:, 0, :], start=True, stop=False)
            pe.matmul(U[:, 1, 16:16 + N_EXP], tri, chosen[:, 1, :], start=False, stop=True)
            pe.matmul(U[:, 0, 32:32 + N_EXP], ones, chosen[:, 0, :], start=True, stop=False)
            pe.matmul(U[:, 0, 32:32 + N_EXP], ones, chosen[:, 1, :], start=False, stop=True).then_inc(r_place, 1)
            pe.wait_ge(r_done, 1)
            npass = pe.value_load(npass_i[0:1, 0:1], min_val=1, max_val=2)

            def gather(b, disp_no):
                pe.wait_ge(e_disp, disp_no)
                for q in range(4):
                    kc = 4 * b + q
                    for t in range(NT):
                        last = pe.matmul(Y[:, 3 - b, q * SLOTS:(q + 1) * SLOTS], xr[:, t, kc * P:(kc + 1) * P], disp[:, t, :],
                                         start=t == 0, stop=t == NT - 1)
                last.then_inc(e_gath, 1)

            def put_back(j, bank):
                t, n = j // 2, j % 2
                pe.matmul(bank, comb[:, t * P:(t + 1) * P], ye[:, n * BANK:(n + 1) * BANK],
                          start=True, stop=True).then_inc(e_scat, 1)

            with pe.Fori(0, npass) as ps:
                g0 = pe.snap(ps * (2 * (N_EXP + 1)))
                d0 = pe.snap(ps * (N_EXP + 1))
                for b in range(2):
                    gather(b, d0 + 1)
                with pe.Fori(0, N_EXP // 2) as two:
                    n2 = pe.snap(ps * (N_EXP // 2) + two)
                    base = pe.snap(n2 * (2 * N_EU))
                    step0 = pe.snap(n2 * (2 * NS))
                    scat0 = pe.snap(n2 * (2 * E_SCAT))
                    turn0 = pe.snap(n2 * 2)
                    gath0 = pe.snap(g0 + two * 4)
                    disp0 = pe.snap(d0 + two * 2)

                    def e_up(half, s):
                        tok = slice(half * SLOTS, (half + 1) * SLOTS)
                        if s >= 1:
                            pe.wait_ge(e_hid, step0 + (half * NS + s))
                        for j in range(4):
                            k = EU["up", s, j]
                            r = unit_slot(k)
                            pe.wait_ge(e_lo, base + (half * N_EU + k + 1 + E_RAW))
                            for q in range(4):
                                kc = 4 * (j % 2) + q
                                w = slice(q * BANK, (q + 1) * BANK)
                                last = products(U[:, j // 2, :], x_hi[:, kc, tok], x_lo[:, kc, tok], w_hi[:, r, w], w_lo[:, r, w],
                                                kc == 0, kc == KC - 1)
                            last.then_inc(e_used, 1)

                    def e_down(half, s):
                        tok = slice(0, SLOTS)
                        pe.wait_ge(e_tlo, step0 + (half * NS + s + 1))
                        for i in range(2):
                            k = EU["dn", s, i]
                            r = unit_slot(k)
                            pe.wait_ge(e_lo, base + (half * N_EU + k + 1 + E_RAW))
                            for q in range(2):
                                c = 4 * (s % 2) + 2 * i + q
                                for n in range(2):
                                    w = slice(q * D + n * BANK, q * D + (n + 1) * BANK)
                                    last = products(Y[:, n, :], t_hi[:, c, tok], t_lo[:, c, tok], w_hi[:, r, w], w_lo[:, r, w],
                                                    s == 0 and i == 0 and q == 0, s == NS - 1 and i == 1 and q == 1)
                            last.then_inc(e_used, 1)

                    for half in range(2):
                        pe.wait_ge(e_glo, gath0 + (2 * half + 2))
                        for s in range(NS):
                            e_up(half, s)
                            if s == 0:
                                pe.wait_ge(e_y, turn0 + (half + 1))
                                pe.wait_ge(e_comb, turn0 + (half + 1))
                            if s >= 1:
                                e_down(half, s - 1)
                            if s < 2:
                                for j in (2 * s, 2 * s + 1):
                                    if s == 1:
                                        pe.wait_ge(e_add, scat0 + (half * E_SCAT + j - 1))
                                    put_back(j, Y[:, 2 + j % 2, :])
                            if s == 2:
                                pe.wait_ge(e_add, scat0 + (half * E_SCAT + 4))
                                for t in range(NT):
                                    last = pe.transpose(Y[:, 2, t * P:(t + 1) * P], dispg[:, t, :], ident)
                                last.then_inc(e_turn, 1)
                            if s == 4:
                                pe.wait_ge(e_comb, turn0 + (half + 2))
                            if s in (3, 4):
                                gather(s - 3, disp0 + (half + 2))
                            pe.wait_ge(e_hid, step0 + (half * NS + s + 1))
                            for q in range(4):
                                last = pe.transpose(T[:, s % 2, q * P:(q + 1) * P], pr[:, 0, q * P:(q + 1) * P], ident)
                            last.then_inc(e_tf, 1)
                        e_down(half, NS - 1)
            pe.wait_ge(e_y, npass * N_EXP + 1)
            pe.wait_ge(e_comb, npass * N_EXP + 1)
            pe.wait_ge(e_glo, npass * (2 * (N_EXP + 1)))
            for j in range(E_SCAT):
                put_back(j, Y[:, 2 + j, :] if j < 2 else U[:, j - 2, :])
            with pe.Fori(0, DEPTH) as l:
                turn_rows("nX", xr, l, xr_key="X")
                turn_rows("nMem", memr, l, xr_key="Mem")
                pe.wait_ge(t_done, filled(("nX", 3), l))
                for c in range(NQ):
                    project(("in", c), c, x_hi, x_lo, l)
                pe.wait_ge(t_done, filled(("nMem", 3), l))
                project(("mk", 0), NQ, t_hi, t_lo, l)
                for c in range(NG):
                    project(("in", NQ + c), NQ + 1 + c, x_hi, x_lo, l)
                pe.wait_ge(v_ready, l + (NT + 3))
                pe.wait_ge(proj_out, proj(("in", NQ + NG - 1), l))
                a0, b0, m0 = 0, 3 * W_A, 3 * W_A + 3 * W_B
                q_at = [(qkv, a0 + i * P) for i in range(3)] + [(qkv, b0 + i * P) for i in range(3)] + [(qkv, m0 + i * P) for i in range(2)]
                k_at = [(qkv, a0 + W_A + i * P) for i in range(3)] + [(qkv, b0 + W_B + i * P) for i in range(3)] + [(km, i * P) for i in range(2)]
                for name, cols in (("qT2", q_at), ("kT2", k_at)):
                    for g in range(4):
                        bank = fill((name, g), l)
                        for i in range(2):
                            rows, c = cols[2 * g + i]
                            for t in range(NT):
                                last = pe.transpose(bank[:, i * S + t * P:i * S + (t + 1) * P], rows[:, t, c:c + P], ident)
                        last.then_inc(t_filled, 1)
                pe.wait_ge(t_done, filled(("kT2", 3), l))

                def value(tile):
                    which, head = tile[3]
                    rows, c = {"a": (qkv, a0 + 2 * W_A), "b": (qkv, b0 + 2 * W_B), "m": (km, W_M)}[which]
                    return rows[:, tile[2], c + head * HD:c + (head + 1) * HD]

                softmax(ITEMS2, value, l)
                pe.wait_ge(o_done, o_no(1, l))
                turn_rows("oT2", xr, l, groups=3, xr_key="O2")
                pe.wait_ge(t_done, filled(("oT2", 2), l))
                for i in range(3):
                    s = unit_slot(UNITS["pj", i])
                    pe.wait_ge(lo_ready, used(("pj", i), l))
                    if i == 2:
                        pe.wait_ge(branch, l * 3 + 1)
                    for q in range(2):
                        kc = 2 * i + q
                        for t in range(NT):
                            for n in range(2):
                                w = slice(q * D + n * BANK, q * D + (n + 1) * BANK)
                                tok = slice(t * P, (t + 1) * P)
                                acc = Y[:, 2 * t + n, :] if kc == 0 or kc >= 4 else (U[:, n, :] if t == 0 else T[:, n, :])
                                last = products(acc, x_hi[:, kc, tok], x_lo[:, kc, tok], w_hi[:, s, w], w_lo[:, s, w],
                                                kc in (0, 1, 4), kc in (0, 3, 5))
                    last.then_inc(unit_used, 1)
                turn_rows("yT", xr, l, xr_key="Y")
                pe.wait_ge(t_done, filled(("yT", 3), l))
                for i in range(4):
                    down(("wo", i), x_hi[:, 2 * i:2 * i + 2, :], x_lo[:, 2 * i:2 * i + 2, :], i == 0, i == 3, l)
                turn_rows("nU", xr, l, xr_key="U")
                pe.wait_ge(t_done, filled(("nU", 3), l))
                mlp("mu", "md", NU, 4, 2, l)


def constants(np):
    i = np.arange(P)
    q, k = i[:, None], i[None, :]
    c = np.zeros((P, N_CST), np.float32)
    c[:, C_ID:C_ID + P] = np.eye(P)
    c[:, C_TRI:C_TRI + P] = q < k
    c[:, C_IOTA:C_IOTA + P] = k
    c[:, C_ONES:C_ONES + S] = 1.0
    allowed = [q >= k, k >= q, (q >= k) & ((q - k) % 4 == 0), (q - k) % 4 == 0,
               (q >= k) & ((q - k) % 16 == 0), (q - k) % 16 == 0]
    masks = np.concatenate([np.where(a, 0.0, -1e30) for a in allowed], axis=1).astype(np.float32)
    inv_freq = (1.0 / (np.float32(500000.0) ** (np.arange(0, 2 * ROT, 2, dtype=np.float32) / np.float32(2 * ROT)))).astype(np.float32)
    angle = np.arange(S, dtype=np.float32)[:, None] * inv_freq[None, :]
    for t in range(NT):
        c[:, C_COS + t * ROT:C_COS + (t + 1) * ROT] = np.cos(angle[t * P:(t + 1) * P])
        c[:, C_SIN + t * ROT:C_SIN + (t + 1) * ROT] = np.sin(angle[t * P:(t + 1) * P])
    return c, masks


_WEIGHTS = ["a_w_in", "a_w_spatial", "a_w_out", "f_w_in", "f_w_out", "kv_w", "b_w_in", "b_w_out", "m_w_router", "m_w_in",
            "m_w_out", "w_in_2", "w_proj_2", "w_out_2", "w_mem_kv_2", "w_up_2", "w_down_2"]


def kernel(**inputs):
    import numpy as np
    import concourse.bacc as bacc
    from concourse.bass_utils import run_bass_kernel_spmd

    a = {k: np.ascontiguousarray(v) for k, v in inputs.items()}
    f32 = np.float32
    sml = np.zeros((P, N_SML), f32)
    for at, name in ((G_A, "a_norm_g"), (G_F, "f_norm_g"), (G_KV, "kv_norm_g"), (G_B, "b_norm_g")):
        sml[:, at:at + KC] = a[name].reshape(KC, P).T
    sml[:, G_BT:G_BT + A_GROUPS] = a["a_b_spatial"][0].T
    sml[:, G_K] = np.tile(a["k_norm_g"], 2)
    sml[:, G_Q] = np.tile(a["q_norm_g"][0], 2)
    sml[0:HEADS, G_BF] = a["kv_b_f"]
    for l in range(DEPTH):
        for j, name in enumerate(("norm_mix_2", "norm_mem_2", "norm_mlp_2")):
            at = G_L + (l * 3 + j) * KC
            sml[:, at:at + KC] = a[name][l].reshape(KC, P).T
    a["w_proj_2"] = np.concatenate([a["w_proj_a_2"], a["w_proj_b_2"], a["w_proj_m_2"]], axis=1)
    cst, masks = constants(np)
    arrays = {"x": a["x"], "mem": a["mem_2"], "cst": cst, "masks": masks, "sml": sml, "gv": a["a_v_norm_g"].reshape(-1),
              "gm": a["m_norm_g"].reshape(-1), "gfin": a["norm_final_2"]}
    arrays.update({n: a[n] for n in _WEIGHTS})

    nc = bacc.Bacc("TRN2", target_bir_lowering=False, num_devices=1)
    args, feeds = [], {}
    for name, v in arrays.items():
        feeds[f"in_{name}"] = v
        args.append(nc.dram_tensor(f"in_{name}", v.shape, mybir.dt.from_np(v.dtype), kind="ExternalInput").ap())
    out = nc.dram_tensor("out", (1, S, D), F32, kind="ExternalOutput").ap()
    program(nc, *args, out)
    return run_bass_kernel_spmd(nc, [feeds], core_ids=[0]).results[0]["out"]
```

```python
from contextlib import ExitStack

import concourse.bass as bass
from concourse import mybir

F32 = mybir.dt.float32
F32R = mybir.dt.float32r
BF16 = mybir.dt.bfloat16
I32 = mybir.dt.int32
U32 = mybir.dt.uint32
ALU = mybir.AluOpType
ACT = mybir.ActivationFunctionType
AX = mybir.AxisListType

P = 128
S = 256
NT = S // P
D = 1024
KC = D // P
BANK = 512
EPS = 1e-6
DEPTH = 2
HD = 64
A_HALF = 3072
A_GROUPS = 8
A_GD = A_HALF // A_GROUPS
NA = A_HALF // BANK
D_FF = 2816
NF = D_FF // 256
HEADS = D // HD
N_EXP = 8
D_EXP = 3584
NS = D_EXP // BANK
SLOTS = P
D_FF2 = 4096
NU = D_FF2 // BANK
W_A, W_B, W_M = 384, 384, 256
NQ = (3 * W_A + 3 * W_B + W_M) // BANK
NG = 3 * D // BANK
H_A, H_B, H_M = 2, 6, 4
ROT = 8
UNIT = 2048
RING = 3
AHEAD = RING - 1
E_RAW = 7

C_ID, C_TRI, C_IOTA, C_ONES, C_COS = 0, 128, 256, 384, 640
N_MASK = 6
C_SIN = C_COS + NT * ROT
N_CST = C_SIN + NT * ROT
G_A, G_F, G_KV, G_B, G_BT = 0, 8, 16, 24, 32
G_K, G_Q, G_BF, G_L = 40, 41, 42, 43
N_SML = G_L + DEPTH * 3 * KC


QKVG = [("kv", 0), ("kv", 1), ("bi", 0), ("bi", 1), ("kv", 2), ("kv", 3), ("bi", 2), ("bi", 3)]


def unit_numbers():
    first, layer = [], []
    two = lambda *k: [(*k, 0), (*k, 1)]
    for c in range(NA):
        first += two("av", c)
    first += two("au", 0)
    for c in range(1, NA):
        first += two("au", c) + two("ad", c - 1)
    first += two("ad", NA - 1)
    first += two("fu", 0)
    for c in range(1, NF):
        first += two("fu", c) + [("fd", c - 1)]
    first += [("fd", NF - 1)]
    for name, c in QKVG:
        first += two(name, c)
    first += [("bo", i) for i in range(4)]
    for c in range(NQ):
        layer += two("in", c)
    layer += two("mk", 0)
    for c in range(NQ, NQ + NG):
        layer += two("in", c)
    layer += [("pj", i) for i in range(3)] + [("wo", i) for i in range(4)]
    layer += two("mu", 0)
    for c in range(1, NU):
        layer += two("mu", c) + two("md", c - 1)
    layer += two("md", NU - 1)
    return first, layer


FIRST, LAYER = unit_numbers()
N_FIRST, N_LAYER = len(FIRST), len(LAYER)
UNITS = {k: n for n, k in enumerate(FIRST)}
UNITS.update({k: N_FIRST + n for n, k in enumerate(LAYER)})
assert N_LAYER % RING == 0
LANDED = []
for n, k in enumerate(FIRST + LAYER):
    LANDED.append((LANDED[n - RING] if n >= RING else 0) + (32 if k[0] == "fu" else 16))

T_FIRST = ([("nA", g) for g in range(4)] + [("wsT", i) for i in range(2)] + [("sp", j) for j in range(2 * A_GROUPS)]
           + [("au", c, b) for c in range(NA) for b in range(2)]
           + [("nF", g) for g in range(4)] + [("fu", c) for c in range(NF)]
           + [("nKV", g) for g in range(4)] + [("fT", 0)]
           + [("kT", g) for g in range(4)] + [("qT", g) for g in range(4)]
           + [("oT", g) for g in range(4)] + [("nM", g) for g in range(4)])
T_LAYER = ([("nX", g) for g in range(4)] + [("nMem", g) for g in range(4)]
           + [("qT2", g) for g in range(4)] + [("kT2", g) for g in range(4)]
           + [("oT2", g) for g in range(3)] + [("yT", g) for g in range(4)] + [("nU", g) for g in range(4)]
           + [("mu", c, b) for c in range(NU) for b in range(2)])
NOT_SPLIT = ("wsT", "sp", "fT", "kT", "qT", "qT2", "kT2")
N_TL = len(T_LAYER)
T_NUM, T_BANK, T_PREV = {}, {}, {}


def number_fills():
    last = [None, None]
    for where, keys in (("first", T_FIRST), ("layer", T_LAYER)):
        if where == "layer":
            last = [None, None]
        for n, k in enumerate(keys):
            bank = k[-1] % 2
            T_NUM[k] = n + (len(T_FIRST) if where == "layer" else 0)
            T_BANK[k] = bank
            T_PREV[k] = last[bank]
            last[bank] = k


number_fills()
H_FIRST = [k for k in T_FIRST if k[0] not in NOT_SPLIT]
H_LAYER = [k for k in T_LAYER if k[0] not in NOT_SPLIT]
H_NUM = {k: n for n, k in enumerate(H_FIRST + H_LAYER)}
N_HL = len(H_LAYER)

PROJ = {k: n for n, k in enumerate([("av", c) for c in range(NA)] + QKVG + [("in", c) for c in range(NQ)] + [("mk", 0)]
                                   + [("in", c) for c in range(NQ, NQ + NG)])}
N_PL = NQ + NG + 1
HID = {k: n for n, k in enumerate([("au", c) for c in range(NA)] + [("fu", c) for c in range(NF)]
                                  + [("mu", c) for c in range(NU)])}
NORMS = {k: n for n, k in enumerate(["A", "V", "F", "KV", "K", "Q", "M", "X", "Mem", "U"])}
LATE = {k: n for n, k in enumerate(["A", "F", "KV", "X", "Mem", "U"])}
XRS = {k: n for n, k in enumerate(["O0", "O", "M", "O2", "Y0", "Y"])}


def expert_units():
    keys = [("up", 0, j) for j in range(4)]
    for s in range(1, NS):
        keys += [("up", s, j) for j in range(4)] + [("dn", s - 1, i) for i in range(2)]
    return keys + [("dn", NS - 1, i) for i in range(2)]


EXPERT = expert_units()
N_EU = len(EXPERT)
EU = {k: n for n, k in enumerate(EXPERT)}
assert N_EU % RING == 0 and N_EU % E_RAW == 0
E_SCAT = 4

CAUSAL, NEAR, D4, D4OFF, D16, D16OFF = range(N_MASK)


def items_first():
    out = []
    for t in range(NT):
        n = 8 // (t + 1)
        for h0 in range(0, HEADS, n):
            out.append((t, [(h, [(h, h // 2, kt, ("v", h), CAUSAL if kt == t else None, h) for kt in range(t + 1)])
                            for h in range(h0, h0 + n)]))
    return out


def items_layer():
    out = []
    for t in range(NT):
        a = []
        for hh in range(H_A):
            tiles = []
            for g, (diag, off) in enumerate(((CAUSAL, NEAR), (D4, D4OFF), (D16, D16OFF))):
                head = 2 * g + hh
                tiles += [(head, head // 2, kt, ("a", head), diag if kt == t else off, None) for kt in range(t + 1)]
            a.append((hh, tiles))
        b = [(H_A + h, [(6 + h, 3 + h // 2, kt, ("b", h), CAUSAL if kt == t else None, None) for kt in range(t + 1)])
             for h in range(H_B)]
        m = [(H_A + H_B + h, [(12 + h, 6 + h // 2, kt, ("m", h), None, None) for kt in range(NT)])
             for h in range(H_M)]
        if t == 0:
            out += [(t, a), (t, b)]
        else:
            out += [(t, a[0:1]), (t, a[1:2]), (t, b[0:3]), (t, b[3:6])]
        out.append((t, m))
    return out


ITEMS1, ITEMS2 = items_first(), items_layer()
N_I1, N_I2 = len(ITEMS1), len(ITEMS2)
V_STEPS_LAYER = 21


def program(nc, x, mem, cst_d, masks_d, sml_d, gv_d, gm_d, gfin_d, a_w_in, a_w_spatial, a_w_out, f_w_in, f_w_out, kv_w,
            b_w_in, b_w_out, m_w_router, m_w_in, m_w_out, w_in_2, w_proj_2, w_out_2, w_mem_kv_2, w_up_2, w_down_2,
            out):
    ctx = ExitStack()
    with ctx:
        def sb(name, shape, dt=F32):
            return ctx.enter_context(nc.sbuf_tensor(name, shape, dt))

        def sem(name):
            return ctx.enter_context(nc.semaphore(name))

        raw = sb("raw", [P, RING, UNIT])
        w_hi = sb("w_hi", [P, RING, UNIT], F32R)
        w_lo = sb("w_lo", [P, RING, UNIT], F32R)
        h = sb("h", [P, NT, D])
        xr = sb("xr", [P, NT, D])
        x_hi = sb("x_hi", [P, KC, S], F32R)
        x_lo = sb("x_lo", [P, KC, S], F32R)
        t_hi = sb("t_hi", [P, KC, S], F32R)
        t_lo = sb("t_lo", [P, KC, S], F32R)
        gu = sb("gu", [P, NT, BANK])
        pr = sb("pr", [P, NT, BANK])
        arena = sb("arena", [P, 6 * NT * D])
        qz = sb("qz", [P, HEADS, S])
        kT = sb("kT", [P, KC, S])
        cst = sb("cst", [P, N_CST])
        sml = sb("sml", [P, N_SML])
        gcur = sb("gcur", [P, 3 * KC])
        identb = sb("identb", [P, P], BF16)
        maskb = sb("maskb", [P, N_MASK, P], BF16)
        wf = sb("wf", [P, KC, HEADS])
        wr = sb("wr", [P, KC, N_EXP])
        ss = sb("ss", [P, NT])
        var = sb("var", [P, 2 * HEADS])
        sd = sb("sd", [P, 2 * HEADS])
        rs = sb("rs", [P, 2 * HEADS])
        rsn = sb("rsn", [P, len(LATE), NT])
        ssv = sb("ssv", [P, NT, NA])
        nmx = sb("nmx", [P, 2, 8])
        sums = sb("sums", [P, NT, HEADS])
        rsum = sb("rsum", [P, NT, HEADS])
        npass_i = sb("npass_i", [P, 1], I32)

        ident = cst[:, C_ID:C_ID + P]
        tri = cst[:, C_TRI:C_TRI + P]
        iota = cst[:, C_IOTA:C_IOTA + P]
        iota8 = cst[:, C_IOTA:C_IOTA + N_EXP]
        ones = cst[:, C_ONES:C_ONES + P]
        ones2 = cst[:, C_ONES:C_ONES + S]

        mask_f = pr[:, :, :].rearrange("p t n -> p (t n)")[:, 0:N_MASK * P]

        def slab(n, width=NT * D, at=0):
            return arena[:, n * NT * D + at:n * NT * D + at + width]

        v_a = slab(0, NT * A_HALF).rearrange("p (t n) -> p t n", t=NT)
        gv_b = slab(3, A_HALF)
        wsT = slab(4, A_GROUPS * P, at=D).rearrange("p (g i) -> p g i", g=A_GROUPS)
        ws = slab(5, A_GROUPS * P).rearrange("p (g j) -> p g j", g=A_GROUPS)
        wsr = slab(5).rearrange("p (t g i) -> p t g i", t=NT, g=A_GROUPS)
        k_t = slab(0).rearrange("p (t n) -> p t n", t=NT)
        v_t = slab(1).rearrange("p (t n) -> p t n", t=NT)
        q_t = slab(2).rearrange("p (t n) -> p t n", t=NT)
        gate_t = slab(3).rearrange("p (t n) -> p t n", t=NT)
        sq_t = slab(4).rearrange("p (t n) -> p t n", t=NT)
        sel = slab(5).rearrange("p (h j) -> p h j", h=HEADS)
        fz = sq_t[:, 0, 0:S]
        fa = sq_t[:, 0, S:2 * S]
        fe = sq_t[:, 0, 2 * S:3 * S]
        ncum = sq_t[:, 1, 0:S]
        diag = pr[:, :, 0:P]
        gm_b = slab(0, D)
        disp = slab(0, NT * SLOTS, at=D).rearrange("p (t n) -> p t n", t=NT)
        dispg = slab(0, NT * SLOTS, at=D + 256).rearrange("p (t n) -> p t n", t=NT)
        comb = slab(0, S, at=D + 512)
        ye = slab(1, D)
        lg = slab(1, NT * 8, at=D).rearrange("p (t n) -> p t n", t=NT)
        mx8 = slab(1, NT * 8, at=D + 16).rearrange("p (t n) -> p t n", t=NT)
        mi8 = slab(1, NT * 8, at=D + 32).bitcast(U32).rearrange("p (t n) -> p t n", t=NT)
        mif = slab(1, NT * 8, at=D + 48).rearrange("p (t n) -> p t n", t=NT)
        gw = slab(1, NT * 4, at=D + 64).rearrange("p (t n) -> p t n", t=NT)
        one1 = slab(1, NT * 8, at=D + 80).rearrange("p (t n) -> p t n", t=NT)
        chosen = slab(1, NT * 8, at=D + 96).rearrange("p (t n) -> p t n", t=NT)
        gate1 = slab(1, NT * 8, at=D + 112).rearrange("p (t n) -> p t n", t=NT)
        gate2 = slab(1, NT * 8, at=D + 128).rearrange("p (t n) -> p t n", t=NT)
        gates = slab(1, NT * 16, at=D + 144).rearrange("p (t n) -> p t n", t=NT)
        place = slab(1, NT * 16, at=D + 176).rearrange("p (t n) -> p t n", t=NT)
        most = slab(1, 2, at=D + 208)
        qkv = slab(0, NT * 3 * D).rearrange("p (t n) -> p t n", t=NT)
        km = qkv[:, :, NQ * BANK:NQ * BANK + 2 * W_M]
        memr = slab(3).rearrange("p (t n) -> p t n", t=NT)
        gat = slab(3, NT * 3 * D).rearrange("p (t n) -> p t n", t=NT)
        rot = pr[:, :, :].rearrange("p t n -> p (t n)")[:, 0:768].rearrange("p (f g h r) -> p f g h r", f=4, g=2, h=12)
        gfin = slab(0, D)

        Y = ctx.enter_context(nc.psum_tensor("Y", [P, 4, BANK], F32))
        U = ctx.enter_context(nc.psum_tensor("U", [P, 2, BANK], F32))
        T = ctx.enter_context(nc.psum_tensor("T", [P, 2, BANK], F32))

        logit_bank = Y[:, 0:2, :].rearrange("p a n -> p (a n)")
        o_bank = T[:, :, :].rearrange("p a n -> p (a n)")
        p_sb = gu[:, :, :].rearrange("p a n -> p (a n)")
        pT_sb = pr[:, :, :].rearrange("p a n -> p (a n)")

        def pair(n):
            return [U[:, t, :] for t in range(NT)] if n % 2 == 0 else [Y[:, t, :] for t in range(NT)]

        side = [Y[:, NT + t, :] for t in range(NT)]

        def gate_unit(b):
            return ("in", NQ + b // 2), b % 2

        s_const = sem("s_const")
        s_x = sem("s_x")
        s_mask = sem("s_mask")
        s_wsp = sem("s_wsp")
        s_gv = sem("s_gv")
        s_wf = sem("s_wf")
        s_wr = sem("s_wr")
        s_gm = sem("s_gm")
        s_mem = sem("s_mem")
        s_gfin = sem("s_gfin")
        s_zero = sem("s_zero")
        s_bf = sem("s_bf")
        loaded = [sem(f"loaded{i}") for i in range(RING)]
        hi_ready = sem("hi_ready")
        lo_ready = sem("lo_ready")
        unit_used = sem("unit_used")
        t_filled = sem("t_filled")
        t_split = sem("t_split")
        t_done = sem("t_done")
        g_cur = sem("g_cur")
        n_var = sem("n_var")
        n_sd = sem("n_sd")
        rs_ready = sem("rs_ready")
        y_tile = sem("y_tile")
        xr_ready = sem("xr_ready")
        proj_out = sem("proj_out")
        hid_act = sem("hid_act")
        hid_ready = sem("hid_ready")
        v_ready = sem("v_ready")
        h_done = sem("h_done")
        v_step = sem("v_step")
        f_diag = sem("f_diag")
        f_z = sem("f_z")
        f_e = sem("f_e")
        ncum_ready = sem("ncum_ready")
        l_filled = sem("l_filled")
        mx_ready = sem("mx_ready")
        p_ready = sem("p_ready")
        p_turned = sem("p_turned")
        pT_a = sem("pT_a")
        pT_v = sem("pT_v")
        pv_done = sem("pv_done")
        o_done = sem("o_done")
        m_tile = sem("m_tile")
        branch = sem("branch")
        r_logits = sem("r_logits")
        r_diff = sem("r_diff")
        r_exp = sem("r_exp")
        r_chosen = sem("r_chosen")
        r_place = sem("r_place")
        r_done = sem("r_done")
        e_loaded = [sem(f"e_loaded{i}") for i in range(E_RAW)]
        e_hi = sem("e_hi")
        e_lo = sem("e_lo")
        e_used = sem("e_used")
        e_disp = sem("e_disp")
        e_gath = sem("e_gath")
        e_ghi = sem("e_ghi")
        e_glo = sem("e_glo")
        e_turn = sem("e_turn")
        e_comb = sem("e_comb")
        e_silu = sem("e_silu")
        e_hid = sem("e_hid")
        e_tf = sem("e_tf")
        e_thi = sem("e_thi")
        e_tlo = sem("e_tlo")
        e_y = sem("e_y")
        e_scat = sem("e_scat")
        e_add = sem("e_add")
        e_pass = sem("e_pass")
        s_out = sem("s_out")

        block = ctx.enter_context(nc.Block())

        def used(key, l=None):
            n = UNITS[key] + 1
            return n if l is None else l * N_LAYER + n

        def filled(key, l=None):
            n = T_NUM[key] + 1
            return n if l is None else l * N_TL + n

        def split(key, l=None):
            n = H_NUM[key] + 1
            return n if l is None else l * N_HL + n

        def proj(key, l=None):
            n = PROJ[key] + 1
            return n if l is None else l * N_PL + n

        def hid(key, l=None):
            n = HID[key] + 1
            return n if l is None else l * NU + n

        def norm_no(key, l=None):
            n = NORMS[key] + 1
            return n if l is None else l * 3 + n

        def xr_no(key, l=None):
            n = XRS[key] + 1
            return n if l is None else l * 3 + n

        def rs_no(key, l=None):
            n = LATE[key] + 1
            return n if l is None else l * 3 + n

        def late(key, t):
            return rsn[:, LATE[key], t:t + 1]

        def sums_no(key, l=None):
            n = ["ad", "fd", "bo", "wo", "md"].index(key) + 1
            return n if l is None else l * 2 + n

        def item_no(i, l=None):
            return i + 1 if l is None else l * N_I2 + N_I1 + i + 1

        def o_no(t, l=None):
            return t + 1 if l is None else l * NT + NT + t + 1

        def unit_slot(u):
            return u % RING

        def e_raw(k):
            i = k % E_RAW
            return raw[:, i, :] if i < RING else slab(2 + i - RING)


        @block.sync
        def _(sp):
            col = "(hf kc p) (c n) -> c hf p kc n"
            colf = dict(hf=2, kc=4, p=P, n=BANK)
            row2 = dict(i=2, kc=2, p=P)
            a_in = a_w_in[0].rearrange(col, **colf)
            a_out = a_w_out[0].rearrange("(c i kc p) n -> c i p kc n", **row2)
            f_in = f_w_in[0].rearrange("(hf kc p) (ab c n) -> c hf ab p kc n", hf=2, kc=4, p=P, ab=2, n=256)
            f_out = f_w_out[0].rearrange("(c kc p) n -> c p kc n", kc=2, p=P)
            kv_in = kv_w[:, 0:2 * D].rearrange(col, **colf)
            b_in = b_w_in[0].rearrange(col, **colf)
            b_out = b_w_out[0].rearrange("(i kc p) n -> i p kc n", kc=2, p=P)
            lcol = "l (hf kc p) (c n) -> l c hf p kc n"
            in2 = w_in_2.rearrange(lcol, **colf)
            mkv2 = w_mem_kv_2.rearrange(lcol, **colf)
            pj2 = w_proj_2.rearrange("l (i kc p) n -> l i p kc n", kc=2, p=P)
            wo2 = w_out_2.rearrange("l (i kc p) n -> l i p kc n", kc=2, p=P)
            up2 = w_up_2.rearrange(lcol, **colf)
            dn2 = w_down_2.rearrange("l (c i kc p) n -> l c i p kc n", **row2)
            first_src = {"av": lambda c, i: a_in[NA + c, i], "au": lambda c, i: a_in[c, i],
                         "ad": lambda c, i: a_out[c, i], "fd": lambda c: f_out[c],
                         "kv": lambda c, i: kv_in[c, i], "bi": lambda c, i: b_in[c, i], "bo": lambda i: b_out[i]}
            layer_src = {"in": lambda l, c, i: in2[l, c, i], "mk": lambda l, c, i: mkv2[l, c, i],
                         "pj": lambda l, i: pj2[l, i], "wo": lambda l, i: wo2[l, i],
                         "mu": lambda l, c, i: up2[l, c, i], "md": lambda l, c, i: dn2[l, c, i]}

            def dst(u, source):
                d = raw[:, unit_slot(u), :]
                return d.rearrange("p (kc n) -> p kc n", kc=source.shape[1])

            sp.dma_start(h[:, :, :], x.rearrange("b (t p) d -> p (b t) d", p=P)).then_inc(s_x, 16)
            sp.dma_start(cst[:, :], cst_d).then_inc(s_const, 16)
            for u, key in enumerate(FIRST):
                if u == 1:
                    sp.dma_start(sml[:, :], sml_d).then_inc(s_const, 16)
                if u >= RING:
                    sp.wait_ge(lo_ready, u + 1 - RING)
                if key[0] == "fu":
                    both = raw[:, unit_slot(u), :].rearrange("p (kc ab n) -> p ab kc n", kc=4, ab=2)
                    for ab in range(2):
                        sp.dma_start(both[:, ab], f_in[key[1], key[2], ab]).then_inc(loaded[unit_slot(u)], 16)
                    continue
                source = first_src[key[0]](*key[1:])
                sp.dma_start(dst(u, source), source).then_inc(loaded[unit_slot(u)], 16)

            up_src = m_w_in[0].rearrange("e (hf kc p) (ab s n) -> e s ab hf p kc n", hf=2, kc=4, p=P, ab=2, n=BANK)
            dn_src = m_w_out[0].rearrange("e (s i kc p) n -> e s i p kc n", i=2, kc=2, p=P)
            sp.wait_ge(lo_ready, N_FIRST)
            sp.wait_ge(r_done, 1)
            sp.sem_inc(e_lo, E_RAW)
            npass = sp.value_load(npass_i[0:1, 0:1], min_val=1, max_val=2)
            with sp.Fori(0, npass) as ps:
                with sp.Fori(0, N_EXP) as e:
                    base = sp.snap((ps * N_EXP + e) * N_EU)
                    for k, key in enumerate(EXPERT):
                        sp.wait_ge(e_lo, base + (k + 1))
                        if key[0] == "up":
                            source = up_src[e, key[1], key[2] // 2, key[2] % 2]
                        else:
                            source = dn_src[e, key[1], key[2]]
                        d = e_raw(k).rearrange("p (kc n) -> p kc n", kc=source.shape[1])
                        sp.dma_start(d, source).then_inc(e_loaded[k % E_RAW], 16)
            with sp.Fori(0, DEPTH) as l:
                sp.wait_ge(e_lo, npass * (N_EXP * N_EU) + E_RAW)
                for key in LAYER:
                    u = UNITS[key]
                    if u == N_FIRST + RING:
                        sp.wait_ge(h_done, l * 2 + 4)
                        sp.dma_start(memr, mem.rearrange("b (t p) d -> p (b t) d", p=P)).then_inc(s_mem, 16)
                    sp.wait_ge(lo_ready, l * N_LAYER + (u + 1 - RING))
                    source = layer_src[key[0]](l, *key[1:])
                    sp.dma_start(dst(u, source), source).then_inc(loaded[unit_slot(u)], 16)
            sp.wait_ge(xr_ready, xr_no("M") + DEPTH * 3 + 1)
            sp.dma_start(out.rearrange("b (t p) d -> p (b t) d", p=P), xr[:, :, :]).then_inc(s_out, 16)
            sp.wait_ge(s_out, 16)

        @block.gpsimd
        def _(pool):
            pool.dma_start(mask_f, masks_d).then_inc(s_mask, 16)
            pool.dma_start(ws, a_w_spatial[0].rearrange("g i j -> i g j")).then_inc(s_wsp, 16)
            pool.dma_start(gv_b, gv_d.partition_broadcast(P)).then_inc(s_gv, 16)
            pool.dma_start(wf[:, :, :], kv_w[:, 2 * D:2 * D + HEADS].rearrange("(kc p) n -> p kc n", p=P)).then_inc(s_wf, 16)
            pool.dma_start(wr[:, :, :], m_w_router[0].rearrange("(kc p) n -> p kc n", p=P)).then_inc(s_wr, 16)
            pool.memset(qz[:, :, :], 0.0).then_inc(s_zero, 1)
            pool.wait_ge(h_done, 3)
            pool.dma_start(gm_b, gm_d.partition_broadcast(P)).then_inc(s_gm, 16)
            pool.wait_ge(h_done, DEPTH * 2 + 4)
            pool.dma_start(gfin, gfin_d.partition_broadcast(P)).then_inc(s_gfin, 16)

        @block.scalar
        def _(act):
            at = [0]

            def hi(u, l=None):
                s = unit_slot(u)
                n = LANDED[u]
                act.wait_ge(loaded[s], n if l is None else l * (N_LAYER // RING * 16) + n)
                if u >= RING:
                    n = u + 1 - RING
                    act.wait_ge(unit_used, n if l is None else l * N_LAYER + n)
                act.activation(w_hi[:, s, :], raw[:, s, :], ACT.Copy).then_inc(hi_ready, 1)

            def ahead(key, l=None):
                end = N_FIRST if l is None else N_FIRST + N_LAYER
                while at[0] < min(UNITS[key] + AHEAD + 1, end):
                    hi(at[0], l)
                    at[0] += 1

            def root(key, n, l=None):
                act.wait_ge(n_var, norm_no(key, l))
                act.activation(sd[:, 0:n], var[:, 0:n], ACT.Sqrt).then_inc(n_sd, 1)
                if key in LATE:
                    act.wait_ge(rs_ready, rs_no(key, l))

            def split_rows(name, dest, gain, l=None, groups=4, also=None):
                for g in range(groups):
                    act.wait_ge(t_filled, filled((name, g), l))
                    b = T_BANK[name, g]
                    if gain is None:
                        last = act.activation(dest[:, 2 * g:2 * g + 2, :].rearrange("p k n -> p (k n)"), T[:, b, :], ACT.Copy)
                    else:
                        for d, gn in ((dest, gain),) + (also or ()):
                            for i in range(2):
                                kc = 2 * g + i
                                last = act.activation(d[:, kc, :], T[:, b, i * S:(i + 1) * S], ACT.Copy,
                                                      scale=gn[:, kc:kc + 1])
                    last.then_inc(t_split, 1)

            def gains(c):
                return sml[:, c:c + KC]

            def evac(key, dest, func, banks, norm, l=None):
                ahead((*key, 1), l)
                act.wait_ge(unit_used, used((*key, 1), l))
                for t in range(NT):
                    last = act.activation(dest(t), banks[t], func, scale=late(norm, t))
                last.then_inc(proj_out, 1)

            def hidden(key, func, norm, l=None, width=BANK):
                ahead((*key, 1), l)
                act.wait_ge(unit_used, used((*key, 1), l))
                n = hid(key, l)
                if key != ("au", 0):
                    act.wait_ge(hid_ready, n - 1)
                for t in range(NT):
                    last = act.activation(gu[:, t, 0:width], U[:, t, 0:width], func, scale=late(norm, t))
                last.then_inc(hid_act, 1)

            def split_hidden(key, chunks, buf, after, l=None):
                ahead(after, l)
                for b in range(chunks // 2):
                    k = (*key, b) if chunks == 4 else key
                    act.wait_ge(t_filled, filled(k, l))
                    d = t_hi[:, 4 * buf + 2 * b:4 * buf + 2 * b + 2, :]
                    act.activation(d.rearrange("p k n -> p (k n)"), T[:, T_BANK[k], :], ACT.Copy).then_inc(t_split, 1)

            def softmax(items, beside, l=None):
                beside(-1)
                for i in range(-1, len(items)):
                    if i >= 0:
                        beside(i)
                        pT_copy(i, l)
                    if i + 1 == len(items):
                        break
                    t, outs = items[i + 1]
                    act.wait_ge(mx_ready, item_no(i + 1, l))
                    at_col = 0
                    for j, (o, tiles) in enumerate(outs):
                        w = len(tiles) * P
                        last = act.activation(p_sb[:, at_col:at_col + w], logit_bank[:, at_col:at_col + w], ACT.Exp,
                                              bias=nmx[:, (i + 1) % 2, j:j + 1], accum_out=sums[:, t, o:o + 1])
                        at_col += w
                    last.then_inc(p_ready, 1)

            def pT_copy(i, l):
                act.wait_ge(p_turned, item_no(i, l))
                act.activation(pT_sb[:, 0:BANK], U[:, 0, :], ACT.Copy).then_inc(pT_a, 1)

            act.wait_ge(s_const, 32)
            hi(0)
            at[0] = 1
            split_rows("nA", x_hi, gains(G_A))
            ahead(("av", 0, 0))
            root("A", NT)
            for c in range(NA):
                evac(("av", c), lambda t: v_a[:, t, c * BANK:(c + 1) * BANK], ACT.Gelu, pair(c), "A")
            root("V", NT)
            for c in range(NA):
                hidden(("au", c), ACT.Gelu, "A")
                split_hidden(("au", c), 4, c % 2, ("au", 0, 1) if c == 0 else ("ad", c - 1, 1))
            ahead(("ad", NA - 1, 1))
            split_rows("nF", x_hi, gains(G_F))
            root("F", NT)
            for c in range(NF):
                hidden(("fu", c), ACT.Silu, "F", width=256)
                split_hidden(("fu", c), 2, c % 2, ("fu", 0, 1) if c == 0 else ("fd", c - 1))
            ahead(("fd", NF - 1))
            split_rows("nKV", x_hi, gains(G_KV), also=((t_hi, gains(G_B)),))
            root("KV", NT)
            def evac_part(key, banks):
                name, c = key
                dest = {"kv": (k_t, v_t), "bi": (q_t, gate_t)}[name][c // 2]
                evac(key, lambda t: dest[:, t, c % 2 * BANK:(c % 2 + 1) * BANK],
                     ACT.Sigmoid if name == "bi" and c >= 2 else ACT.Copy, banks, "KV")

            for n in range(2):
                evac_part(QKVG[n], pair(n))
            ahead(("bi", 0, 0))
            root("K", 2 * HEADS)
            for n in range(2, 4):
                evac_part(QKVG[n], pair(n))
            ahead(("kv", 2, 0))
            root("Q", 2 * HEADS)
            ahead(("kv", 2, 1))
            act.wait_ge(f_z, 1)
            act.activation(fe[0:HEADS, :], fa[0:HEADS, :], ACT.Exp).then_inc(f_e, 1)
            evac_part(("kv", 2), side)
            act.wait_ge(f_z, 2)
            act.activation(fe[0:HEADS, :], fa[0:HEADS, :], ACT.Ln).then_inc(f_e, 1)

            def beside1(i):
                if i in (-1, 1, 3):
                    evac_part(QKVG[5 + (i + 1) // 2], side)
                if i < 3:
                    ahead(("bi", 2 + (i + 1) // 2, (i + 1) % 2))

            softmax(ITEMS1, beside1)
            split_rows("oT", x_hi, None)
            ahead(("bo", 3))
            root("M", NT)
            split_rows("nM", x_hi, None)
            act.wait_ge(r_diff, 1)
            act.activation(gw[:, :, 1:2], gw[:, :, 0:1], ACT.Exp).then_inc(r_exp, 1)
            act.wait_ge(unit_used, N_FIRST)
            act.sem_inc(e_used, RING)
            act.wait_ge(r_done, 1)
            npass = act.value_load(npass_i[0:1, 0:1], min_val=1, max_val=2)
            def gather_hi(b, buf, n):
                act.wait_ge(e_gath, n)
                act.activation(x_hi[:, 4 * b:4 * b + 4, buf * SLOTS:(buf + 1) * SLOTS],
                               Y[:, 3 - b, :].rearrange("p (k n) -> p k n", k=4), ACT.Copy).then_inc(e_ghi, 1)

            def output():
                for n in range(2):
                    last = act.activation(ye[:, n * BANK:(n + 1) * BANK], Y[:, n, :], ACT.Copy)
                last.then_inc(e_y, 1)

            with act.Fori(0, npass) as ps:
                g0 = act.snap(ps * (2 * (N_EXP + 1)))
                for b in range(2):
                    gather_hi(b, 0, g0 + (b + 1))
                with act.Fori(0, N_EXP // 2) as two:
                    n2 = act.snap(ps * (N_EXP // 2) + two)
                    base = act.snap(n2 * (2 * N_EU))
                    ld = act.snap(n2 * (2 * N_EU // E_RAW * 16))
                    step0 = act.snap(n2 * (2 * NS))
                    gath0 = act.snap(g0 + two * 4)
                    for half in range(2):
                        k, u0 = 0, half * N_EU

                        def e_ahead(n):
                            nonlocal k
                            while k < min(n + AHEAD + 1, N_EU):
                                s = unit_slot(k)
                                act.wait_ge(e_loaded[k % E_RAW], ld + ((u0 + k) // E_RAW + 1) * 16)
                                act.wait_ge(e_used, base + (u0 + k + 1))
                                act.activation(w_hi[:, s, :], e_raw(k), ACT.Copy).then_inc(e_hi, 1)
                                k += 1

                        e_ahead(-1)
                        act.wait_ge(e_used, base + (u0 + RING))
                        output()
                        for s in range(NS):
                            e_ahead(EU["up", s, 3])
                            act.wait_ge(e_used, base + (u0 + EU["up", s, 3] + 1 + RING))
                            if s >= 1:
                                act.wait_ge(e_hid, step0 + (half * NS + s))
                            act.activation(gu[:, 0, :], U[:, 0, :], ACT.Silu).then_inc(e_silu, 1)
                            if s >= 1:
                                e_ahead(EU["dn", s - 1, 1])
                            act.wait_ge(e_tf, step0 + (half * NS + s + 1))
                            act.activation(t_hi[:, 4 * (s % 2):4 * (s % 2) + 4, 0:SLOTS],
                                           T[:, s % 2, :].rearrange("p (k n) -> p k n", k=4), ACT.Copy).then_inc(e_thi, 1)
                            if s in (3, 4):
                                gather_hi(s - 3, 1 - half, gath0 + (2 * half + 2 + s - 2))
                        e_ahead(N_EU)
            act.wait_ge(e_used, npass * (N_EXP * N_EU) + RING)
            output()
            with act.Fori(0, DEPTH) as l:
                at[0] = N_FIRST
                for u in range(N_FIRST, N_FIRST + AHEAD):
                    hi(u, l)
                    at[0] += 1
                act.wait_ge(g_cur, l + 1)
                split_rows("nX", x_hi, gcur[:, 0:KC], l)
                ahead(("in", 0, 0), l)
                root("X", NT, l)
                for c in range(NQ):
                    evac(("in", c), lambda t: qkv[:, t, c * BANK:(c + 1) * BANK], ACT.Copy, pair(c), "X", l)
                    if c == 1:
                        split_rows("nMem", t_hi, gcur[:, KC:2 * KC], l)
                        root("Mem", NT, l)
                evac(("mk", 0), lambda t: km[:, t, :], ACT.Copy, pair(NQ), "Mem", l)

                def evac_gate(c):
                    evac(("in", NQ + c), lambda t: gat[:, t, c * BANK:(c + 1) * BANK], ACT.Sigmoid, side, "X", l)

                def ahead_gate(b):
                    key, hf = gate_unit(b)
                    ahead((*key, hf), l)

                ahead_gate(0)
                evac_gate(0)
                ahead_gate(2)

                def beside2(i):
                    if i >= 0 and i % 2 == 0:
                        evac_gate(1 + i // 2)
                    ahead_gate(4 + i)

                softmax(ITEMS2, beside2, l)
                evac_gate(NG - 1)
                split_rows("oT2", x_hi, None, l, groups=3)
                ahead(("pj", 2), l)
                split_rows("yT", x_hi, None, l)
                ahead(("wo", 3), l)
                split_rows("nU", x_hi, gcur[:, 2 * KC:3 * KC], l)
                root("U", NT, l)
                for c in range(NU):
                    hidden(("mu", c), ACT.Relu, "U", l)
                    split_hidden(("mu", c), 4, c % 2, ("mu", 0, 1) if c == 0 else ("md", c - 1, 1), l)
                ahead(("md", NU - 1, 1), l)
            act.wait_ge(n_var, norm_no("X") + DEPTH * 3)
            act.activation(sd[:, 0:NT], var[:, 0:NT], ACT.Sqrt).then_inc(n_sd, 1)

        @block.vector
        def _(dve):
            at = [0]
            steps = [0, None]

            def order(ins):
                steps[0] += 1
                ins.then_inc(v_step, 1)
                dve.wait_ge(v_step, steps[0] if steps[1] is None else steps[1] + steps[0])

            def lo(u, l=None):
                s = unit_slot(u)
                dve.wait_ge(hi_ready, u + 1 if l is None else l * N_LAYER + (u + 1))
                dve.tensor_tensor(w_lo[:, s, :], raw[:, s, :], w_hi[:, s, :].bitcast(F32), ALU.subtract).then_inc(lo_ready, 1)

            def ahead(key, l=None):
                end = N_FIRST if l is None else N_FIRST + N_LAYER
                while at[0] < min(UNITS[key] + AHEAD + 1, end):
                    lo(at[0], l)
                    at[0] += 1

            def row_scale(src, key, l=None):
                for t in range(NT):
                    last = dve.scalar_tensor_tensor(xr[:, t, :], src[:, t, :], 1.0, src[:, t, :], ALU.mult, ALU.mult,
                                                    accum_out=ss[:, t:t + 1])
                order(last)
                dve.tensor_scalar(var[:, 0:NT], ss[:, 0:NT], 1.0 / D, EPS, ALU.mult, ALU.add).then_inc(n_var, 1)
                if key not in LATE:
                    return inverse(NT, key, l)
                dve.wait_ge(n_sd, norm_no(key, l))
                refine(NT, rsn[:, LATE[key], :]).then_inc(rs_ready, 1)

            def inverse(n, key, l=None):
                dve.wait_ge(n_sd, norm_no(key, l))
                order(refine(n, rs[:, 0:n]))

            def refine(n, dest):
                order(dve.reciprocal(rs[:, 0:n], sd[:, 0:n]))
                order(dve.tensor_tensor(sd[:, 0:n], rs[:, 0:n], rs[:, 0:n], ALU.mult))
                order(dve.tensor_tensor(sd[:, 0:n], sd[:, 0:n], var[:, 0:n], ALU.mult))
                order(dve.tensor_scalar(sd[:, 0:n], sd[:, 0:n], -0.5, 1.5, ALU.mult, ALU.add))
                return dve.tensor_tensor(dest, rs[:, 0:n], sd[:, 0:n], ALU.mult)

            def split_rows(name, hi_d, lo_d, gain, l=None, groups=4, also=None):
                for g in range(groups):
                    dve.wait_ge(t_split, split((name, g), l))
                    b = T_BANK[name, g]
                    if gain is None:
                        sl = slice(2 * g, 2 * g + 2)
                        last = dve.tensor_tensor(lo_d[:, sl, :].rearrange("p k n -> p (k n)"), T[:, b, :],
                                                 hi_d[:, sl, :].rearrange("p k n -> p (k n)").bitcast(F32), ALU.subtract)
                    else:
                        for hd, ld, gn in ((hi_d, lo_d, gain),) + (also or ()):
                            for i in range(2):
                                kc = 2 * g + i
                                last = dve.scalar_tensor_tensor(ld[:, kc, :], T[:, b, i * S:(i + 1) * S], gn[:, kc:kc + 1],
                                                                hd[:, kc, :].bitcast(F32), ALU.mult, ALU.subtract)
                    last.then_inc(t_done, 1)

            def gains(c):
                return sml[:, c:c + KC]

            def gated(key, other, l=None):
                ahead((*key, 1), l)
                dve.wait_ge(hid_act, hid(key, l))
                for t in range(NT):
                    last = dve.tensor_tensor(pr[:, t, :], gu[:, t, :], other(t), ALU.mult)
                last.then_inc(hid_ready, 1)

            def split_hidden(key, chunks, buf, after, l=None):
                ahead(after, l)
                for b in range(chunks // 2):
                    k = (*key, b) if chunks == 4 else key
                    dve.wait_ge(t_split, split(k, l))
                    sl = slice(4 * buf + 2 * b, 4 * buf + 2 * b + 2)
                    dve.tensor_tensor(t_lo[:, sl, :].rearrange("p k n -> p (k n)"), T[:, T_BANK[k], :],
                                      t_hi[:, sl, :].rearrange("p k n -> p (k n)").bitcast(F32),
                                      ALU.subtract).then_inc(t_done, 1)

            def add_residual(key, l=None):
                ahead(key, l)
                dve.wait_ge(y_tile, sums_no(key[0], l))
                add_tile(0)
                dve.wait_ge(unit_used, used(key, l))
                add_tile(1).then_inc(h_done, 1)

            def add_tile(t):
                for n in range(2):
                    hs = h[:, t, n * BANK:(n + 1) * BANK]
                    last = dve.tensor_tensor(hs, hs, Y[:, 2 * t + n, :], ALU.add)
                return last

            def after_h(n):
                dve.wait_ge(h_done, n)

            def softmax(items, beside, finish, l=None):
                for i in range(-1, len(items)):
                    if i >= 0:
                        n = sum(len(o[1]) for o in items[i][1]) * P
                        dve.wait_ge(p_turned, item_no(i, l))
                        dve.tensor_copy(pT_sb[:, BANK:n], U[:, 1, 0:n - BANK]).then_inc(pT_v, 1)
                    if i + 1 < len(items):
                        outs = items[i + 1][1]
                        w = len(outs[0][1]) * P
                        dve.wait_ge(l_filled, item_no(i + 1, l))
                        dve.tensor_reduce(nmx[:, (i + 1) % 2, 0:len(outs)],
                                          logit_bank[:, 0:len(outs) * w].rearrange("p (o w) -> p o w", w=w),
                                          AX.X, ALU.max, negate=True).then_inc(mx_ready, 1)
                    beside(i)
                    if i >= 0 and (i + 1 == len(items) or items[i + 1][0] != items[i][0]):
                        dve.wait_ge(pv_done, item_no(i, l))
                        finish(items[i][0])

            def over_sums(t, n):
                order(dve.reciprocal(rsum[:, t, 0:n], sums[:, t, 0:n]))
                return dve.tensor_tensor(xr[:, t, 0:n * HD].rearrange("p (o d) -> p o d", d=HD),
                                         o_bank[:, 0:n * HD].rearrange("p (o d) -> p o d", d=HD),
                                         rsum[:, t, 0:n].unsqueeze(2).to_broadcast([P, n, HD]), ALU.mult)

            dve.wait_ge(s_const, 32)
            dve.wait_ge(s_x, 16)
            lo(0)
            at[0] = 1
            split_rows("nA", x_hi, x_lo, gains(G_A))
            ahead(("av", 0, 0))
            row_scale(h, "A")
            dve.wait_ge(s_mask, 16)
            dve.tensor_copy(identb[:, :], ident).then_inc(s_bf, 1)
            dve.tensor_copy(maskb[:, :, :].rearrange("p m n -> p (m n)"), mask_f).then_inc(s_bf, 1)
            dve.wait_ge(s_bf, 2)
            for c in range(NA):
                ahead(("av", c, 1))
                if c == 1:
                    for i in range(2):
                        dve.wait_ge(t_filled, filled(("wsT", i)))
                        dve.tensor_copy(wsT[:, 4 * i:4 * i + 4, :].rearrange("p g n -> p (g n)"),
                                        T[:, T_BANK["wsT", i], :]).then_inc(t_done, 1)
                    dve.wait_ge(t_done, filled(("wsT", 1)))
                    dve.memset(wsT[HD:P, :, 0:HD], 0.0)
                dve.wait_ge(proj_out, proj(("av", c)))
                for t in range(NT):
                    vs = v_a[:, t, c * BANK:(c + 1) * BANK]
                    last = dve.scalar_tensor_tensor(pr[:, t, :], vs, 1.0, vs, ALU.mult, ALU.mult,
                                                    accum_out=ssv[:, t, c:c + 1])
                order(last)
                if c == 0:
                    dve.wait_ge(s_gv, 16)
                for t in range(NT):
                    vs = v_a[:, t, c * BANK:(c + 1) * BANK]
                    last = dve.tensor_tensor(vs, vs, gv_b[:, c * BANK:(c + 1) * BANK], ALU.mult)
            order(dve.tensor_reduce(ss[:, :], ssv[:, :, :], AX.X, ALU.add))
            dve.tensor_scalar(var[:, 0:NT], ss[:, :], 1.0 / A_HALF, EPS, ALU.mult, ALU.add).then_inc(n_var, 1)
            inverse(NT, "V")
            for t in range(NT):
                dve.tensor_scalar(wsr[:, t, :, :].rearrange("p g i -> p (g i)"), wsT[:, :, :].rearrange("p g i -> p (g i)"),
                                  rs[:, t:t + 1], None, ALU.mult).then_inc(v_ready, 1)
            for j in range(NT * A_GROUPS):
                t, g = j // A_GROUPS, j % A_GROUPS
                dve.wait_ge(t_filled, filled(("sp", j)))
                last = dve.tensor_scalar(v_a[:, t, g * A_GD:(g + 1) * A_GD], T[:, T_BANK["sp", j], 0:A_GD],
                                         sml[:, G_BT + g:G_BT + g + 1], None, ALU.add)
                last.then_inc(t_done, 1)
            dve.wait_ge(t_done, filled(("sp", NT * A_GROUPS - 1)))
            for c in range(NA):
                gated(("au", c), lambda t: v_a[:, t, c * BANK:(c + 1) * BANK])
                split_hidden(("au", c), 4, c % 2, ("au", 0, 1) if c == 0 else ("ad", c - 1, 1))
            add_residual(("ad", NA - 1, 1))
            after_h(1)
            split_rows("nF", x_hi, x_lo, gains(G_F))
            row_scale(h, "F")
            dve.wait_ge(rs_ready, rs_no("F"))
            for c in range(NF):
                ahead(("fu", c, 1))
                dve.wait_ge(hid_act, hid(("fu", c)))
                for t in range(NT):
                    last = dve.scalar_tensor_tensor(pr[:, t, 0:256], U[:, t, 256:512], late("F", t), gu[:, t, 0:256],
                                                    ALU.mult, ALU.mult)
                last.then_inc(hid_ready, 1)
                split_hidden(("fu", c), 2, c % 2, ("fu", 0, 1) if c == 0 else ("fd", c - 1))
            add_residual(("fd", NF - 1))
            after_h(2)
            split_rows("nKV", x_hi, x_lo, gains(G_KV), also=((t_hi, t_lo, gains(G_B)),))
            row_scale(h, "KV")
            dve.wait_ge(rs_ready, rs_no("KV"))
            for t in range(NT):
                last = dve.tensor_scalar(diag[:, t, :], ident, late("KV", t), None, ALU.mult)
            last.then_inc(f_diag, 1)
            dve.tensor_copy(sel, ident[:, 0:HEADS].unsqueeze(2).to_broadcast([P, HEADS, P]))

            def head_norm(rows, key, after):
                for t in range(NT):
                    order(dve.tensor_tensor(sq_t[:, t, :], rows[:, t, :], rows[:, t, :], ALU.mult))
                    last = dve.tensor_reduce(var[:, t * HEADS:(t + 1) * HEADS],
                                             sq_t[:, t, :].rearrange("p (o d) -> p o d", d=HD), AX.X, ALU.add)
                order(last)
                dve.tensor_scalar(var[:, :], var[:, :], 1.0 / HD, EPS, ALU.mult, ALU.add).then_inc(n_var, 1)
                ahead(after)
                inverse(2 * HEADS, key)
                for t in range(NT):
                    r3 = rows[:, t, :].rearrange("p (o d) -> p o d", d=HD)
                    last = dve.tensor_tensor(r3, r3, rs[:, t * HEADS:(t + 1) * HEADS].unsqueeze(2).to_broadcast([P, HEADS, HD]),
                                             ALU.mult)
                last.then_inc(v_ready, 1)

            ahead(("kv", 1, 1))
            dve.wait_ge(proj_out, proj(("kv", 1)))
            head_norm(k_t, "K", ("bi", 0, 0))
            ahead(("bi", 1, 1))
            dve.wait_ge(proj_out, proj(("bi", 1)))
            head_norm(q_t, "Q", ("kv", 2, 0))
            order(dve.memset(sq_t[:, :, :], 0.0))
            dve.wait_ge(t_filled, filled(("fT", 0)))
            order(dve.tensor_copy(fe[0:HEADS, :], T[0:HEADS, 0, S:2 * S]))
            dve.tensor_tensor(fz[0:HEADS, :], T[0:HEADS, 0, 0:S], fe[0:HEADS, :], ALU.mult).then_inc(t_done, 1)
            dve.wait_ge(t_done, filled(("fT", 0)))
            order(dve.tensor_scalar(fz[0:HEADS, :], fz[0:HEADS, :], sml[0:HEADS, G_BF:G_BF + 1], None, ALU.add))
            order(dve.tensor_scalar(fe[0:HEADS, :], fz[0:HEADS, :], -1.0, None, ALU.mult))
            dve.tensor_tensor(fa[0:HEADS, :], fe[0:HEADS, :], fz[0:HEADS, :], ALU.min).then_inc(f_z, 1)
            ahead(("kv", 2, 1))
            dve.wait_ge(f_e, 1)
            dve.tensor_scalar(fa[0:HEADS, :], fe[0:HEADS, :], 1.0, None, ALU.add).then_inc(f_z, 1)
            for g in range(4):
                dve.wait_ge(t_filled, filled(("kT", g)))
                dve.tensor_scalar(kT[:, 2 * g:2 * g + 2, :].rearrange("p k n -> p (k n)"), T[:, T_BANK["kT", g], :],
                                  sml[:, G_K:G_K + 1], None, ALU.mult).then_inc(t_done, 1)
            dve.wait_ge(f_e, 2)
            order(dve.scalar_tensor_tensor(fa[0:HEADS, :], fz[0:HEADS, :], 0.0, fe[0:HEADS, :], ALU.min, ALU.subtract))
            dve.tensor_tensor_scan(ncum[0:HEADS, :], ones2[0:HEADS, :], fa[0:HEADS, :], 0.0, ALU.mult, ALU.subtract).then_inc(ncum_ready, 1)
            ahead(("kv", 3, 0))
            dve.wait_ge(s_zero, 1)
            for g in range(4):
                dve.wait_ge(t_filled, filled(("qT", g)))
                for half in range(2):
                    r = slice(half * HD, (half + 1) * HD)
                    last = dve.tensor_scalar(qz[r, 4 * g + half:4 * g + 4:2, :],
                                             T[r, T_BANK["qT", g], :].rearrange("p (k n) -> p k n", k=2),
                                             sml[r, G_Q:G_Q + 1], HD ** -0.5, ALU.mult, ALU.mult)
                last.then_inc(t_done, 1)

            ahead(("kv", 3, 1))

            def output_gate(t):
                dve.tensor_tensor(xr[:, t, :], xr[:, t, :], gate_t[:, t, :], ALU.mult).then_inc(xr_ready, 1)

            def finish1(t):
                if t == NT - 1:
                    dve.wait_ge(o_done, o_no(0))
                    dve.wait_ge(proj_out, proj(("bi", 3)))
                    output_gate(0)
                over_sums(t, HEADS).then_inc(o_done, 1)

            def beside1(i):
                if i < 3:
                    ahead(("bi", 2 + (i + 1) // 2, (i + 1) % 2))

            softmax(ITEMS1, beside1, finish1)
            dve.wait_ge(o_done, o_no(1))
            output_gate(1)
            split_rows("oT", x_hi, x_lo, None)
            add_residual(("bo", 3))
            after_h(3)
            row_scale(h, "M")
            dve.wait_ge(s_gm, 16)
            for t in range(NT):
                last = dve.scalar_tensor_tensor(xr[:, t, :], h[:, t, :], rs[:, t:t + 1], gm_b, ALU.mult, ALU.mult)
            last.then_inc(xr_ready, 1)
            split_rows("nM", x_hi, x_lo, None)
            dve.wait_ge(r_logits, 1)
            order(dve.tensor_copy(lg, U[:, :, 0:N_EXP]))
            for t in range(NT):
                last = dve.max(mx8[:, t, :], lg[:, t, :])
            order(last)
            for t in range(NT):
                last = dve.max_index(mi8[:, t, :], mx8[:, t, :], lg[:, t, :])
            order(last)
            dve.tensor_tensor(gw[:, :, 0:1], mx8[:, :, 1:2], mx8[:, :, 0:1], ALU.subtract).then_inc(r_diff, 1)
            order(dve.tensor_copy(mif, mi8))
            for t in range(NT):
                last = dve.tensor_scalar(one1[:, t, :], iota8, mif[:, t, 0:1], None, ALU.is_equal)
            order(last)
            for t in range(NT):
                last = dve.scalar_tensor_tensor(chosen[:, t, :], iota8, mif[:, t, 1:2], one1[:, t, :], ALU.is_equal, ALU.add)
            last.then_inc(r_chosen, 1)
            dve.wait_ge(r_exp, 1)
            order(dve.tensor_scalar(gw[:, :, 2:3], gw[:, :, 1:2], 1.0, None, ALU.add))
            order(dve.reciprocal(gw[:, :, 2:3], gw[:, :, 2:3]))
            order(dve.tensor_tensor(gw[:, :, 3:4], gw[:, :, 1:2], gw[:, :, 2:3], ALU.mult))
            for t in range(NT):
                dve.tensor_scalar(gate1[:, t, :], iota8, mif[:, t, 0:1], gw[:, t, 2:3], ALU.is_equal, ALU.mult)
                last = dve.tensor_scalar(gate2[:, t, :], iota8, mif[:, t, 1:2], gw[:, t, 3:4], ALU.is_equal, ALU.mult)
            order(last)
            order(dve.memset(gates, 0.0))
            dve.memset(place, -1.0)
            dve.memset(comb, 0.0).then_inc(e_comb, 1)
            order(dve.tensor_tensor(gates[:, :, 0:N_EXP], gate1, gate2, ALU.add))
            dve.wait_ge(r_place, 1)
            order(dve.scalar_tensor_tensor(place[:, :, 0:N_EXP], U[:, :, 16:16 + N_EXP], 1.0, chosen, ALU.add, ALU.mult))
            dve.tensor_scalar(place[:, :, 0:N_EXP], place[:, :, 0:N_EXP], -1.0, None, ALU.add)
            order(dve.tensor_reduce(most[:, 0:1], U[:, 0, 32:32 + N_EXP], AX.X, ALU.max))
            order(dve.tensor_scalar(most[:, 1:2], most[:, 0:1], SLOTS + 0.5, 1.0, ALU.is_gt, ALU.add))
            dve.tensor_copy(npass_i[:, :], most[:, 1:2]).then_inc(r_done, 1)
            dve.wait_ge(r_done, 1)
            npass = dve.value_load(npass_i[0:1, 0:1], min_val=1, max_val=2)

            def dispatch(e):
                for t in range(NT):
                    col = place[:, t, bass.ds(e, 1)]
                    dve.tensor_scalar(disp[:, t, :], iota, col, None, ALU.is_equal)
                    last = dve.tensor_scalar(dispg[:, t, :], iota, col, gates[:, t, bass.ds(e, 1)], ALU.is_equal, ALU.mult)
                last.then_inc(e_disp, 1)

            def gather_lo(b, buf, n):
                dve.wait_ge(e_ghi, n)
                sl = slice(buf * SLOTS, (buf + 1) * SLOTS)
                dve.tensor_tensor(x_lo[:, 4 * b:4 * b + 4, sl], Y[:, 3 - b, :].rearrange("p (k n) -> p k n", k=4),
                                  x_hi[:, 4 * b:4 * b + 4, sl].bitcast(F32), ALU.subtract).then_inc(e_glo, 1)

            def put_back(j, n, banks):
                dve.wait_ge(e_scat, n)
                hs = h[:, j // 2, j % 2 * BANK:(j % 2 + 1) * BANK]
                dve.tensor_tensor(hs, hs, banks[j], ALU.add).then_inc(e_add, 1)

            in_loop = [Y[:, 2, :], Y[:, 3, :], Y[:, 2, :], Y[:, 3, :]]
            with dve.Fori(0, npass) as ps:
                g0 = dve.snap(ps * (2 * (N_EXP + 1)))
                dispatch(0)
                for b in range(2):
                    gather_lo(b, 0, g0 + (b + 1))
                with dve.Fori(0, N_EXP // 2) as two:
                    n2 = dve.snap(ps * (N_EXP // 2) + two)
                    base = dve.snap(n2 * (2 * N_EU))
                    step0 = dve.snap(n2 * (2 * NS))
                    scat0 = dve.snap(n2 * (2 * E_SCAT))
                    turn0 = dve.snap(n2 * 2)
                    gath0 = dve.snap(g0 + two * 4)
                    for half in range(2):
                        k, u0 = 0, half * N_EU

                        def e_ahead(n):
                            nonlocal k
                            while k < min(n + AHEAD + 1, N_EU):
                                s = unit_slot(k)
                                dve.wait_ge(e_hi, base + (u0 + k + 1))
                                dve.tensor_tensor(w_lo[:, s, :], e_raw(k), w_hi[:, s, :].bitcast(F32), ALU.subtract).then_inc(e_lo, 1)
                                k += 1

                        e_ahead(-1)
                        for s in range(NS):
                            e_ahead(EU["up", s, 3])
                            dve.wait_ge(e_silu, step0 + (half * NS + s + 1))
                            dve.tensor_tensor(pr[:, 0, :], gu[:, 0, :], U[:, 1, :], ALU.mult).then_inc(e_hid, 1)
                            if s >= 1:
                                e_ahead(EU["dn", s - 1, 1])
                            dve.wait_ge(e_thi, step0 + (half * NS + s + 1))
                            sl = slice(4 * (s % 2), 4 * (s % 2) + 4)
                            dve.tensor_tensor(t_lo[:, sl, 0:SLOTS], T[:, s % 2, :].rearrange("p (k n) -> p k n", k=4),
                                              t_hi[:, sl, 0:SLOTS].bitcast(F32), ALU.subtract).then_inc(e_tlo, 1)
                            if s < 2:
                                for j in (2 * s, 2 * s + 1):
                                    put_back(j, scat0 + (half * E_SCAT + j + 1), in_loop)
                            if s == 2:
                                dve.wait_ge(e_turn, turn0 + (half + 1))
                                dve.tensor_copy(comb, Y[:, 2, 0:S]).then_inc(e_comb, 1)
                                dispatch(two * 2 + (half + 1))
                            if s in (3, 4):
                                gather_lo(s - 3, 1 - half, gath0 + (2 * half + 2 + s - 2))
                        e_ahead(N_EU)
                dve.tensor_scalar(place, place, -float(SLOTS), None, ALU.add).then_inc(e_pass, 1)
                dve.wait_ge(e_pass, ps + 1)
            first_steps = steps[0]
            with dve.Fori(0, DEPTH) as l:
                at[0] = N_FIRST
                steps[0], steps[1] = 0, dve.snap(l * V_STEPS_LAYER + first_steps)
                dve.tensor_copy(gcur[:, :], sml[:, bass.ds(l * (3 * KC) + G_L, 3 * KC)]).then_inc(g_cur, 1)
                for u in range(N_FIRST, N_FIRST + AHEAD):
                    lo(u, l)
                    at[0] += 1
                dve.wait_ge(e_scat, npass * (N_EXP * E_SCAT) + E_SCAT)
                dve.wait_ge(y_tile, l * 2 + sums_no("bo"))
                add_tile(0)
                dve.wait_ge(unit_used, l * N_LAYER + N_FIRST)
                add_tile(1).then_inc(h_done, 1)
                after_h(l * 2 + 4)
                dve.wait_ge(g_cur, l + 1)
                split_rows("nX", x_hi, x_lo, gcur[:, 0:KC], l)
                ahead(("in", 0, 0), l)
                row_scale(h, "X", l)
                ahead(("in", 1, 1), l)
                split_rows("nMem", t_hi, t_lo, gcur[:, KC:2 * KC], l)
                dve.wait_ge(s_mem, l * 16 + 16)
                row_scale(memr, "Mem", l)
                ahead(("mk", 0, 1), l)
                dve.wait_ge(proj_out, proj(("in", NQ - 1), l))
                for t in range(NT):
                    heads = qkv[:, t, 0:6 * W_A].rearrange("p (g z) -> p g z", g=2)[:, :, 0:2 * W_A]\
                        .rearrange("p g (h d) -> p g h d", d=HD)
                    x1, x2 = heads[:, :, :, 0:ROT], heads[:, :, :, ROT:2 * ROT]
                    shape = [P, 2, 12, ROT]
                    cs = cst[:, C_COS + t * ROT:C_COS + (t + 1) * ROT].unsqueeze(1).unsqueeze(1).to_broadcast(shape)
                    sn = cst[:, C_SIN + t * ROT:C_SIN + (t + 1) * ROT].unsqueeze(1).unsqueeze(1).to_broadcast(shape)
                    for f, (a, b) in enumerate(((x1, cs), (x2, sn), (x2, cs), (x1, sn))):
                        last = dve.tensor_tensor(rot[:, f], a, b, ALU.mult)
                    order(last)
                    dve.tensor_tensor(x1, rot[:, 0], rot[:, 1], ALU.subtract)
                    last = dve.tensor_tensor(x2, rot[:, 2], rot[:, 3], ALU.add)
                    if t == 0:
                        order(last)
                last.then_inc(v_ready, 1)

                def ahead_gate(b):
                    key, hf = gate_unit(b)
                    ahead((*key, hf), l)

                ahead_gate(0)
                for g in range(4):
                    dve.wait_ge(t_filled, filled(("qT2", g), l))
                    for half in range(2):
                        r = slice(half * HD, (half + 1) * HD)
                        last = dve.tensor_scalar(qz[r, 4 * g + half:4 * g + 4:2, :],
                                                 T[r, T_BANK["qT2", g], :].rearrange("p (k n) -> p k n", k=2),
                                                 HD ** -0.5, None, ALU.mult)
                    last.then_inc(t_done, 1)
                ahead_gate(1)
                for g in range(4):
                    dve.wait_ge(t_filled, filled(("kT2", g), l))
                    dve.tensor_copy(kT[:, 2 * g:2 * g + 2, :].rearrange("p k n -> p (k n)"),
                                    T[:, T_BANK["kT2", g], :]).then_inc(t_done, 1)

                ahead_gate(2)

                def finish2(t):
                    over_sums(t, H_A + H_B + H_M).then_inc(o_done, 1)

                softmax(ITEMS2, lambda i: ahead_gate(4 + i), finish2, l)
                dve.wait_ge(o_done, o_no(1, l))
                dve.sem_inc(xr_ready, 1)
                split_rows("oT2", x_hi, x_lo, None, l, groups=3)
                ahead(("pj", 2), l)
                dve.wait_ge(proj_out, proj(("in", NQ + NG - 1), l))
                for br in range(2):
                    dve.wait_ge(unit_used, used(("pj", br), l))
                    for t in range(NT):
                        for n in range(2):
                            gs = gat[:, t, br * D + n * BANK:br * D + (n + 1) * BANK]
                            src = Y[:, 2 * t + n, :] if br == 0 else (U[:, n, :] if t == 0 else T[:, n, :])
                            last = dve.tensor_tensor(gs, gs, src, ALU.mult)
                    last.then_inc(branch, 1)
                dve.wait_ge(branch, l * 4 + 2)
                for t in range(NT):
                    last = dve.tensor_tensor(xr[:, t, :], gat[:, t, 0:D], gat[:, t, D:2 * D], ALU.add)
                order(last)
                for t in range(NT):
                    if t == 0:
                        dve.wait_ge(m_tile, l + 1)
                    else:
                        dve.wait_ge(unit_used, used(("pj", 2), l))
                    for n in range(2):
                        gs = gat[:, t, 2 * D + n * BANK:2 * D + (n + 1) * BANK]
                        last = dve.tensor_tensor(gs, gs, Y[:, 2 * t + n, :], ALU.mult)
                    last.then_inc(branch, 1)
                    dve.wait_ge(branch, l * 4 + 3 + t)
                    dve.tensor_tensor(xr[:, t, :], xr[:, t, :], gat[:, t, 2 * D:3 * D], ALU.add).then_inc(xr_ready, 1)
                split_rows("yT", x_hi, x_lo, None, l)
                add_residual(("wo", 3), l)
                after_h(l * 2 + 5)
                split_rows("nU", x_hi, x_lo, gcur[:, 2 * KC:3 * KC], l)
                row_scale(h, "U", l)
                for c in range(NU):
                    gated(("mu", c), lambda t: gu[:, t, :], l)
                    split_hidden(("mu", c), 4, c % 2, ("mu", 0, 1) if c == 0 else ("md", c - 1, 1), l)
                ahead(("md", NU - 1, 1), l)
                assert steps[0] == V_STEPS_LAYER, steps
            steps[0], steps[1] = first_steps + DEPTH * V_STEPS_LAYER, None
            dve.wait_ge(y_tile, DEPTH * 2 + sums_no("bo"))
            add_tile(0)
            dve.wait_ge(unit_used, N_FIRST + DEPTH * N_LAYER)
            add_tile(1).then_inc(h_done, 1)
            after_h(DEPTH * 2 + 4)
            for t in range(NT):
                last = dve.scalar_tensor_tensor(xr[:, t, :], h[:, t, :], 1.0, h[:, t, :], ALU.mult, ALU.mult,
                                                accum_out=ss[:, t:t + 1])
            order(last)
            dve.tensor_scalar(var[:, 0:NT], ss[:, 0:NT], 1.0 / D, EPS, ALU.mult, ALU.add).then_inc(n_var, 1)
            dve.wait_ge(n_sd, norm_no("X") + DEPTH * 3)
            order(refine(NT, rs[:, 0:NT]))
            dve.wait_ge(s_gfin, 16)
            for t in range(NT):
                last = dve.scalar_tensor_tensor(xr[:, t, :], h[:, t, :], rs[:, t:t + 1], gfin, ALU.mult, ALU.mult)
            last.then_inc(xr_ready, 1)

        @block.tensor
        def _(pe):
            def products(acc, a_hi, a_lo, b_hi, b_lo, first, last):
                pe.matmul(acc, a_hi, b_hi, start=first, stop=False)
                pe.matmul(acc, a_lo, b_hi, start=False, stop=False)
                return pe.matmul(acc, a_hi, b_lo, start=False, stop=last)

            def up_unit(key, hf, banks, a_hi, a_lo, l=None, fresh=None):
                s = unit_slot(UNITS[(*key, hf)])
                if fresh:
                    pe.wait_ge(t_done, filled((fresh, 2 * hf + 1), l))
                pe.wait_ge(lo_ready, used((*key, hf), l))
                for t in range(NT):
                    for q in range(4):
                        kc = 4 * hf + q
                        w = slice(q * BANK, (q + 1) * BANK)
                        tok = slice(t * P, (t + 1) * P)
                        last = products(banks[t], a_hi[:, kc, tok], a_lo[:, kc, tok], w_hi[:, s, w], w_lo[:, s, w],
                                        kc == 0, kc == KC - 1)
                last.then_inc(unit_used, 1)

            def up(key, banks, a_hi, a_lo, l=None, fresh=None):
                for hf in range(2):
                    up_unit(key, hf, banks, a_hi, a_lo, l, fresh)

            def beside_unit(key, hf, first, a_hi, a_lo, l=None):
                if hf == 0 and not first:
                    pe.wait_ge(proj_out, proj(key, l) - 1)
                up_unit(key, hf, side, a_hi, a_lo, l)

            def down(key, a_hi, a_lo, first, final, l=None, banks=None):
                u = UNITS[key]
                s = unit_slot(u)
                pe.wait_ge(lo_ready, used(key, l))
                for t in range(NT):
                    for q in range(2):
                        for n in range(2):
                            w = slice(q * D + n * BANK, q * D + (n + 1) * BANK)
                            tok = slice(t * P, (t + 1) * P)
                            last = products(Y[:, 2 * t + n, :], a_hi[:, q, tok], a_lo[:, q, tok], w_hi[:, s, w], w_lo[:, s, w],
                                            first and q == 0, final and q == 1)
                    if final and t == 0:
                        last.then_inc(y_tile, 1)
                last.then_inc(unit_used, 1)

            def fill(key, l=None):
                prev = T_PREV[key]
                if prev is not None:
                    pe.wait_ge(t_done, filled(prev, l))
                return T[:, T_BANK[key], :]

            def turn_rows(name, rows, l=None, groups=4):
                for g in range(groups):
                    bank = fill((name, g), l)
                    for i in range(2):
                        for t in range(NT):
                            c = (2 * g + i) * P
                            last = pe.transpose(bank[:, i * S + t * P:i * S + (t + 1) * P], rows[:, t, c:c + P], ident)
                    last.then_inc(t_filled, 1)

            def turn_hidden(key, chunks, l=None):
                pe.wait_ge(hid_ready, hid(key, l))
                for b in range(chunks // 2):
                    k = (*key, b) if chunks == 4 else key
                    bank = fill(k, l)
                    for i in range(2):
                        for t in range(NT):
                            c = (2 * b + i) * P
                            last = pe.transpose(bank[:, i * S + t * P:i * S + (t + 1) * P], pr[:, t, c:c + P], ident)
                    last.then_inc(t_filled, 1)

            def project(key, n, a_hi, a_lo, l=None, fresh=None):
                if n >= 2:
                    pe.wait_ge(proj_out, proj(key, l) - 2)
                up(key, pair(n), a_hi, a_lo, l, fresh)

            def mlp(name, dname, n_chunks, chunks, per, l=None, fresh=None):
                def downs(c):
                    last_fill = (name, c, chunks // 2 - 1) if chunks == 4 else (name, c)
                    pe.wait_ge(t_done, filled(last_fill, l))
                    for i in range(per):
                        sl = slice(4 * (c % 2) + 2 * i, 4 * (c % 2) + 2 * i + 2)
                        key = (dname, c, i) if per == 2 else (dname, c)
                        down(key, t_hi[:, sl, :], t_lo[:, sl, :], c == 0 and i == 0, c == n_chunks - 1 and i == per - 1, l)

                for c in range(n_chunks):
                    if c >= 1:
                        pe.wait_ge(hid_ready, hid((name, c - 1), l))
                    up((name, c), pair(0), x_hi, x_lo, l, fresh if c == 0 else None)
                    if name == "au" and c == 0:
                        spatial()
                    if c >= 1:
                        downs(c - 1)
                    turn_hidden((name, c), chunks, l)
                downs(n_chunks - 1)

            def spatial():
                for j in range(NT * A_GROUPS):
                    t, g = j // A_GROUPS, j % A_GROUPS
                    pe.wait_ge(v_ready, t + 1)
                    bank = fill(("sp", j))
                    pe.matmul(bank[:, 0:A_GD], wsr[:, t, g, :], v_a[:, t, g * A_GD:(g + 1) * A_GD], start=True, stop=True)\
                        .then_inc(t_filled, 1)

            def softmax(items, value, beside, l=None):
                def logits(i):
                    if i >= 1:
                        pe.wait_ge(p_ready, item_no(i - 1, l))
                    c = 0
                    for o, tiles in items[i][1]:
                        for head, kp, kt, v, mask, forget in tiles:
                            dst = logit_bank[:, c:c + P]
                            q = qz[:, head, items[i][0] * P:(items[i][0] + 1) * P]
                            keys = slice(kt * P, (kt + 1) * P)
                            last = pe.matmul(dst, q, kT[:, kp, keys], start=True, stop=forget is None and mask is None)
                            if forget is not None:
                                last = pe.matmul(dst, sel[:, forget, :], ncum[:, keys], start=False, stop=mask is None)
                            if mask is not None:
                                last = pe.matmul(dst, identb[:, :], maskb[:, mask, :], start=False, stop=True)
                            c += P
                    last.then_inc(l_filled, 1)

                logits(0)
                beside(-1)
                for i in range(len(items)):
                    t, outs = items[i]
                    pe.wait_ge(p_ready, item_no(i, l))
                    n = sum(len(tiles) for _, tiles in outs)
                    for j in range(n):
                        last = pe.transpose(U[:, j // 4, j % 4 * P:(j % 4 + 1) * P], p_sb[:, j * P:(j + 1) * P], ident)
                    last.then_inc(p_turned, 1)
                    if i + 1 < len(items):
                        logits(i + 1)
                    beside(i)
                    pe.wait_ge(pT_a, item_no(i, l))
                    pe.wait_ge(pT_v, item_no(i, l))
                    if i >= 1 and items[i - 1][0] != t:
                        pe.wait_ge(o_done, o_no(t - 1, l))
                    j = 0
                    for o, tiles in outs:
                        for m, tile in enumerate(tiles):
                            last = pe.matmul(o_bank[:, o * HD:(o + 1) * HD], pT_sb[:, j * P:(j + 1) * P], value(tile),
                                             start=m == 0, stop=m == len(tiles) - 1)
                            j += 1
                    last.then_inc(pv_done, 1)

            pe.wait_ge(s_const, 32)
            pe.wait_ge(s_x, 16)
            turn_rows("nA", h)
            for c in range(NA):
                project(("av", c), c, x_hi, x_lo, fresh="nA" if c == 0 else None)
                if c == 0:
                    pe.wait_ge(s_wsp, 16)
                    for i in range(2):
                        bank = fill(("wsT", i))
                        for q in range(4):
                            last = pe.transpose(bank[:, q * P:(q + 1) * P], ws[:, 4 * i + q, :], ident)
                        last.then_inc(t_filled, 1)
            pe.wait_ge(proj_out, proj(("av", NA - 1)))
            mlp("au", "ad", NA, 4, 2)
            pe.wait_ge(h_done, 1)
            turn_rows("nF", h)
            mlp("fu", "fd", NF, 2, 1, fresh="nF")
            pe.wait_ge(h_done, 2)
            turn_rows("nKV", h)
            for n in range(4):
                project(QKVG[n], n, *((x_hi, x_lo) if QKVG[n][0] == "kv" else (t_hi, t_lo)), fresh="nKV" if n == 0 else None)
            pe.wait_ge(s_wf, 16)
            bank = fill(("fT", 0))
            for n, part in enumerate((x_hi, x_lo)):
                for kc in range(KC):
                    last = pe.matmul(bank[0:HEADS, 0:S], wf[:, kc, :], part[:, kc, :].bitcast(F32),
                                     start=n == 0 and kc == 0, stop=n == 1 and kc == KC - 1)
            pe.wait_ge(f_diag, 1)
            for t in range(NT):
                last = pe.matmul(bank[0:HEADS, S + t * P:S + (t + 1) * P], ones[:, 0:HEADS], diag[:, t, :], start=True, stop=True)
            last.then_inc(t_filled, 1)
            def turn_heads(name, rows):
                for g in range(4):
                    bank = fill((name, g))
                    for i in range(2):
                        for t in range(NT):
                            c = (2 * g + i) * P
                            last = pe.transpose(bank[:, i * S + t * P:i * S + (t + 1) * P], rows[:, t, c:c + P], ident)
                    last.then_inc(t_filled, 1)

            for hf in range(2):
                beside_unit(("kv", 2), hf, True, x_hi, x_lo)
            pe.wait_ge(v_ready, NT + 1)
            turn_heads("kT", k_t)
            beside_unit(("kv", 3), 0, False, x_hi, x_lo)
            pe.wait_ge(v_ready, NT + 2)
            turn_heads("qT", q_t)
            beside_unit(("kv", 3), 1, False, x_hi, x_lo)
            pe.wait_ge(t_done, filled(("qT", 3)))
            pe.wait_ge(proj_out, proj(("bi", 1)))
            pe.wait_ge(ncum_ready, 1)
            pe.wait_ge(s_bf, 2)

            def beside1(i):
                if i < 3:
                    beside_unit(("bi", 2 + (i + 1) // 2), (i + 1) % 2, False, t_hi, t_lo)

            softmax(ITEMS1, lambda tile: v_t[:, tile[2], tile[3][1] * HD:(tile[3][1] + 1) * HD], beside1)
            pe.wait_ge(xr_ready, xr_no("O"))
            turn_rows("oT", xr)
            pe.wait_ge(t_done, filled(("oT", 3)))
            for i in range(4):
                down(("bo", i), x_hi[:, 2 * i:2 * i + 2, :], x_lo[:, 2 * i:2 * i + 2, :], i == 0, i == 3)
            pe.wait_ge(xr_ready, xr_no("M"))
            turn_rows("nM", xr)
            pe.wait_ge(t_done, filled(("nM", 3)))
            pe.wait_ge(s_wr, 16)
            for t in range(NT):
                for n, part in enumerate((x_hi, x_lo)):
                    for kc in range(KC):
                        last = pe.matmul(U[:, t, 0:N_EXP], part[:, kc, t * P:(t + 1) * P].bitcast(F32), wr[:, kc, :],
                                         start=n == 0 and kc == 0, stop=n == 1 and kc == KC - 1)
            last.then_inc(r_logits, 1)
            pe.wait_ge(r_chosen, 1)
            pe.matmul(U[:, 0, 16:16 + N_EXP], tri, chosen[:, 0, :], start=True, stop=True)
            pe.matmul(U[:, 1, 16:16 + N_EXP], ones, chosen[:, 0, :], start=True, stop=False)
            pe.matmul(U[:, 1, 16:16 + N_EXP], tri, chosen[:, 1, :], start=False, stop=True)
            pe.matmul(U[:, 0, 32:32 + N_EXP], ones, chosen[:, 0, :], start=True, stop=False)
            pe.matmul(U[:, 0, 32:32 + N_EXP], ones, chosen[:, 1, :], start=False, stop=True).then_inc(r_place, 1)
            pe.wait_ge(r_done, 1)
            npass = pe.value_load(npass_i[0:1, 0:1], min_val=1, max_val=2)

            def gather(b, disp_no):
                pe.wait_ge(e_disp, disp_no)
                for q in range(4):
                    kc = 4 * b + q
                    for t in range(NT):
                        last = pe.matmul(Y[:, 3 - b, q * SLOTS:(q + 1) * SLOTS], xr[:, t, kc * P:(kc + 1) * P], disp[:, t, :],
                                         start=t == 0, stop=t == NT - 1)
                last.then_inc(e_gath, 1)

            def put_back(j, bank):
                t, n = j // 2, j % 2
                pe.matmul(bank, comb[:, t * P:(t + 1) * P], ye[:, n * BANK:(n + 1) * BANK],
                          start=True, stop=True).then_inc(e_scat, 1)

            with pe.Fori(0, npass) as ps:
                g0 = pe.snap(ps * (2 * (N_EXP + 1)))
                d0 = pe.snap(ps * (N_EXP + 1))
                for b in range(2):
                    gather(b, d0 + 1)
                with pe.Fori(0, N_EXP // 2) as two:
                    n2 = pe.snap(ps * (N_EXP // 2) + two)
                    base = pe.snap(n2 * (2 * N_EU))
                    step0 = pe.snap(n2 * (2 * NS))
                    scat0 = pe.snap(n2 * (2 * E_SCAT))
                    turn0 = pe.snap(n2 * 2)
                    gath0 = pe.snap(g0 + two * 4)
                    disp0 = pe.snap(d0 + two * 2)

                    def e_up(half, s):
                        tok = slice(half * SLOTS, (half + 1) * SLOTS)
                        if s >= 1:
                            pe.wait_ge(e_hid, step0 + (half * NS + s))
                        for j in range(4):
                            k = EU["up", s, j]
                            r = unit_slot(k)
                            pe.wait_ge(e_lo, base + (half * N_EU + k + 1 + E_RAW))
                            for q in range(4):
                                kc = 4 * (j % 2) + q
                                w = slice(q * BANK, (q + 1) * BANK)
                                last = products(U[:, j // 2, :], x_hi[:, kc, tok], x_lo[:, kc, tok], w_hi[:, r, w], w_lo[:, r, w],
                                                kc == 0, kc == KC - 1)
                            last.then_inc(e_used, 1)

                    def e_down(half, s):
                        tok = slice(0, SLOTS)
                        pe.wait_ge(e_tlo, step0 + (half * NS + s + 1))
                        for i in range(2):
                            k = EU["dn", s, i]
                            r = unit_slot(k)
                            pe.wait_ge(e_lo, base + (half * N_EU + k + 1 + E_RAW))
                            for q in range(2):
                                c = 4 * (s % 2) + 2 * i + q
                                for n in range(2):
                                    w = slice(q * D + n * BANK, q * D + (n + 1) * BANK)
                                    last = products(Y[:, n, :], t_hi[:, c, tok], t_lo[:, c, tok], w_hi[:, r, w], w_lo[:, r, w],
                                                    s == 0 and i == 0 and q == 0, s == NS - 1 and i == 1 and q == 1)
                            last.then_inc(e_used, 1)

                    for half in range(2):
                        pe.wait_ge(e_glo, gath0 + (2 * half + 2))
                        for s in range(NS):
                            e_up(half, s)
                            if s == 0:
                                pe.wait_ge(e_y, turn0 + (half + 1))
                                pe.wait_ge(e_comb, turn0 + (half + 1))
                            if s >= 1:
                                e_down(half, s - 1)
                            if s < 2:
                                for j in (2 * s, 2 * s + 1):
                                    if s == 1:
                                        pe.wait_ge(e_add, scat0 + (half * E_SCAT + j - 1))
                                    put_back(j, Y[:, 2 + j % 2, :])
                            if s == 2:
                                pe.wait_ge(e_add, scat0 + (half * E_SCAT + 4))
                                for t in range(NT):
                                    last = pe.transpose(Y[:, 2, t * P:(t + 1) * P], dispg[:, t, :], ident)
                                last.then_inc(e_turn, 1)
                            if s == 4:
                                pe.wait_ge(e_comb, turn0 + (half + 2))
                            if s in (3, 4):
                                gather(s - 3, disp0 + (half + 2))
                            pe.wait_ge(e_hid, step0 + (half * NS + s + 1))
                            for q in range(4):
                                last = pe.transpose(T[:, s % 2, q * P:(q + 1) * P], pr[:, 0, q * P:(q + 1) * P], ident)
                            last.then_inc(e_tf, 1)
                        e_down(half, NS - 1)
            pe.wait_ge(e_y, npass * N_EXP + 1)
            pe.wait_ge(e_comb, npass * N_EXP + 1)
            pe.wait_ge(e_glo, npass * (2 * (N_EXP + 1)))
            for j in range(E_SCAT):
                put_back(j, Y[:, j, :])
            with pe.Fori(0, DEPTH) as l:
                pe.wait_ge(h_done, l * 2 + 4)
                turn_rows("nX", h, l)
                for c in range(NQ):
                    project(("in", c), c, x_hi, x_lo, l, fresh="nX" if c == 0 else None)
                    if c == 1:
                        pe.wait_ge(s_mem, l * 16 + 16)
                        turn_rows("nMem", memr, l)
                pe.wait_ge(t_done, filled(("nMem", 3), l))
                project(("mk", 0), NQ, t_hi, t_lo, l)

                def gates(b):
                    key, hf = gate_unit(b)
                    beside_unit(key, hf, b == 0, x_hi, x_lo, l)

                gates(0)
                pe.wait_ge(v_ready, l + (NT + 3))
                pe.wait_ge(proj_out, proj(("mk", 0), l))
                a0, b0, m0 = 0, 3 * W_A, 3 * W_A + 3 * W_B
                q_at = [(qkv, a0 + i * P) for i in range(3)] + [(qkv, b0 + i * P) for i in range(3)] + [(qkv, m0 + i * P) for i in range(2)]
                k_at = [(qkv, a0 + W_A + i * P) for i in range(3)] + [(qkv, b0 + W_B + i * P) for i in range(3)] + [(km, i * P) for i in range(2)]
                for name, cols in (("qT2", q_at), ("kT2", k_at)):
                    for g in range(4):
                        bank = fill((name, g), l)
                        for i in range(2):
                            rows, c = cols[2 * g + i]
                            for t in range(NT):
                                last = pe.transpose(bank[:, i * S + t * P:i * S + (t + 1) * P], rows[:, t, c:c + P], ident)
                        last.then_inc(t_filled, 1)
                    gates(1 if name == "qT2" else 2)
                pe.wait_ge(t_done, filled(("kT2", 3), l))

                def value(tile):
                    which, head = tile[3]
                    rows, c = {"a": (qkv, a0 + 2 * W_A), "b": (qkv, b0 + 2 * W_B), "m": (km, W_M)}[which]
                    return rows[:, tile[2], c + head * HD:c + (head + 1) * HD]

                softmax(ITEMS2, value, lambda i: gates(4 + i), l)
                pe.wait_ge(o_done, o_no(1, l))
                pe.wait_ge(xr_ready, xr_no("O2", l))
                turn_rows("oT2", xr, l, groups=3)
                pe.wait_ge(t_done, filled(("oT2", 2), l))
                for i in range(3):
                    s = unit_slot(UNITS["pj", i])
                    pe.wait_ge(lo_ready, used(("pj", i), l))
                    if i == 2:
                        pe.wait_ge(branch, l * 4 + 1)
                    for t in range(NT):
                        for q in range(2):
                            kc = 2 * i + q
                            for n in range(2):
                                w = slice(q * D + n * BANK, q * D + (n + 1) * BANK)
                                tok = slice(t * P, (t + 1) * P)
                                acc = Y[:, 2 * t + n, :] if kc == 0 or kc >= 4 else (U[:, n, :] if t == 0 else T[:, n, :])
                                last = products(acc, x_hi[:, kc, tok], x_lo[:, kc, tok], w_hi[:, s, w], w_lo[:, s, w],
                                                kc in (0, 1, 4), kc in (0, 3, 5))
                        if i == 2 and t == 0:
                            last.then_inc(m_tile, 1)
                    last.then_inc(unit_used, 1)
                pe.wait_ge(xr_ready, xr_no("Y", l))
                turn_rows("yT", xr, l)
                pe.wait_ge(t_done, filled(("yT", 3), l))
                for i in range(4):
                    down(("wo", i), x_hi[:, 2 * i:2 * i + 2, :], x_lo[:, 2 * i:2 * i + 2, :], i == 0, i == 3, l)
                pe.wait_ge(h_done, l * 2 + 5)
                turn_rows("nU", h, l)
                mlp("mu", "md", NU, 4, 2, l, fresh="nU")


def constants(np):
    i = np.arange(P)
    q, k = i[:, None], i[None, :]
    c = np.zeros((P, N_CST), np.float32)
    c[:, C_ID:C_ID + P] = np.eye(P)
    c[:, C_TRI:C_TRI + P] = q < k
    c[:, C_IOTA:C_IOTA + P] = k
    c[:, C_ONES:C_ONES + S] = 1.0
    allowed = [q >= k, k >= q, (q >= k) & ((q - k) % 4 == 0), (q - k) % 4 == 0,
               (q >= k) & ((q - k) % 16 == 0), (q - k) % 16 == 0]
    masks = np.concatenate([np.where(a, 0.0, -1e30) for a in allowed], axis=1).astype(np.float32)
    inv_freq = (1.0 / (np.float32(500000.0) ** (np.arange(0, 2 * ROT, 2, dtype=np.float32) / np.float32(2 * ROT)))).astype(np.float32)
    angle = np.arange(S, dtype=np.float32)[:, None] * inv_freq[None, :]
    for t in range(NT):
        c[:, C_COS + t * ROT:C_COS + (t + 1) * ROT] = np.cos(angle[t * P:(t + 1) * P])
        c[:, C_SIN + t * ROT:C_SIN + (t + 1) * ROT] = np.sin(angle[t * P:(t + 1) * P])
    return c, masks


_WEIGHTS = ["a_w_in", "a_w_spatial", "a_w_out", "f_w_in", "f_w_out", "kv_w", "b_w_in", "b_w_out", "m_w_router", "m_w_in",
            "m_w_out", "w_in_2", "w_proj_2", "w_out_2", "w_mem_kv_2", "w_up_2", "w_down_2"]


def kernel(**inputs):
    import numpy as np
    import concourse.bacc as bacc
    from concourse.bass_utils import run_bass_kernel_spmd

    a = {k: np.ascontiguousarray(v) for k, v in inputs.items()}
    f32 = np.float32
    sml = np.zeros((P, N_SML), f32)
    for at, name in ((G_A, "a_norm_g"), (G_F, "f_norm_g"), (G_KV, "kv_norm_g"), (G_B, "b_norm_g")):
        sml[:, at:at + KC] = a[name].reshape(KC, P).T
    sml[:, G_BT:G_BT + A_GROUPS] = a["a_b_spatial"][0].T
    sml[:, G_K] = np.tile(a["k_norm_g"], 2)
    sml[:, G_Q] = np.tile(a["q_norm_g"][0], 2)
    sml[0:HEADS, G_BF] = a["kv_b_f"]
    for l in range(DEPTH):
        for j, name in enumerate(("norm_mix_2", "norm_mem_2", "norm_mlp_2")):
            at = G_L + (l * 3 + j) * KC
            sml[:, at:at + KC] = a[name][l].reshape(KC, P).T
    a["w_proj_2"] = np.concatenate([a["w_proj_a_2"], a["w_proj_b_2"], a["w_proj_m_2"]], axis=1)
    cst, masks = constants(np)
    arrays = {"x": a["x"], "mem": a["mem_2"], "cst": cst, "masks": masks, "sml": sml, "gv": a["a_v_norm_g"].reshape(-1),
              "gm": a["m_norm_g"].reshape(-1), "gfin": a["norm_final_2"]}
    arrays.update({n: a[n] for n in _WEIGHTS})

    nc = bacc.Bacc("TRN2", target_bir_lowering=False, num_devices=1)
    args, feeds = [], {}
    for name, v in arrays.items():
        feeds[f"in_{name}"] = v
        args.append(nc.dram_tensor(f"in_{name}", v.shape, mybir.dt.from_np(v.dtype), kind="ExternalInput").ap())
    out = nc.dram_tensor("out", (1, S, D), F32, kind="ExternalOutput").ap()
    program(nc, *args, out)
    return run_bass_kernel_spmd(nc, [feeds], core_ids=[0]).results[0]["out"]
```

```python
from contextlib import ExitStack

import concourse.bass as bass
from concourse import mybir

F32 = mybir.dt.float32
F32R = mybir.dt.float32r
BF16 = mybir.dt.bfloat16
I32 = mybir.dt.int32
U32 = mybir.dt.uint32
ALU = mybir.AluOpType
ACT = mybir.ActivationFunctionType
AX = mybir.AxisListType

P = 128
S = 256
NT = S // P
D = 1024
KC = D // P
BANK = 512
EPS = 1e-6
DEPTH = 2
HD = 64
A_HALF = 3072
A_GROUPS = 8
A_GD = A_HALF // A_GROUPS
NA = A_HALF // BANK
D_FF = 2816
NF = D_FF // 256
HEADS = D // HD
N_EXP = 8
D_EXP = 3584
NS = D_EXP // BANK
SLOTS = P
D_FF2 = 4096
NU = D_FF2 // BANK
W_A, W_B, W_M = 384, 384, 256
NQ = (3 * W_A + 3 * W_B + W_M) // BANK
NG = 3 * D // BANK
H_A, H_B, H_M = 2, 6, 4
ROT = 8
UNIT = 2048
RING = 3
AHEAD = RING - 1
E_RAW = 7

C_ID, C_TRI, C_IOTA, C_ONES, C_COS = 0, 128, 256, 384, 640
N_MASK = 6
C_SIN = C_COS + NT * ROT
N_CST = C_SIN + NT * ROT
G_A, G_F, G_KV, G_B, G_BT = 0, 8, 16, 24, 32
G_M = 40
G_K, G_Q, G_BF, G_L = 48, 49, 50, 51
N_SML = G_L + DEPTH * 3 * KC


GATES = [0, 1, 4, 5, 2, 3]
QKVG = [("kv", 0), ("kv", 1), ("bi", 0), ("bi", 1), ("kv", 2), ("kv", 3), ("bi", 2), ("bi", 3)]


def unit_numbers():
    first, layer = [], []
    two = lambda *k: [(*k, 0), (*k, 1)]
    for c in range(NA):
        first += two("av", c)
    first += two("au", 0)
    for c in range(1, NA):
        first += two("au", c) + two("ad", c - 1)
    first += two("ad", NA - 1)
    first += two("fu", 0)
    for c in range(1, NF):
        first += two("fu", c) + [("fd", c - 1)]
    first += [("fd", NF - 1)]
    for name, c in QKVG:
        first += two(name, c)
    first += [("bo", i) for i in range(4)]
    for c in range(NQ):
        layer += two("in", c)
    layer += two("mk", 0)
    for c in GATES:
        layer += two("in", NQ + c)
    layer += [("pj", i) for i in range(3)] + [("wo", i) for i in range(4)]
    layer += two("mu", 0)
    for c in range(1, NU):
        layer += two("mu", c) + two("md", c - 1)
    layer += two("md", NU - 1)
    return first, layer


FIRST, LAYER = unit_numbers()
N_FIRST, N_LAYER = len(FIRST), len(LAYER)
UNITS = {k: n for n, k in enumerate(FIRST)}
UNITS.update({k: N_FIRST + n for n, k in enumerate(LAYER)})
assert N_LAYER % RING == 0
LANDED = []
for n, k in enumerate(FIRST + LAYER):
    LANDED.append((LANDED[n - RING] if n >= RING else 0) + (32 if k[0] == "fu" else 16))

T_FIRST = ([("nA", g) for g in range(4)] + [("wsT", i) for i in range(2)] + [("sp", j) for j in range(2 * A_GROUPS)]
           + [("au", c, b) for c in range(NA) for b in range(2)]
           + [("nF", g) for g in range(4)] + [("fu", c) for c in range(NF)]
           + [("nKV", g) for g in range(4)] + [("nB", g) for g in range(4)] + [("fT", 0)]
           + [("kT", g) for g in range(4)] + [("qT", g) for g in range(4)]
           + [("oT", g) for g in range(4)] + [("nM", g) for g in range(4)])
T_LAYER = ([("nX", g) for g in range(4)] + [("nMem", g) for g in range(4)]
           + [("qT2", g) for g in range(4)] + [("kT2", g) for g in range(4)]
           + [("oT2", g) for g in range(3)] + [("yT", g) for g in range(4)] + [("nU", g) for g in range(4)]
           + [("mu", c, b) for c in range(NU) for b in range(2)])
NOT_SPLIT = ("wsT", "sp", "fT", "kT", "qT", "qT2", "kT2")
N_TL = len(T_LAYER)
T_NUM, T_BANK, T_PREV = {}, {}, {}


def number_fills():
    last = [None, None]
    for where, keys in (("first", T_FIRST), ("layer", T_LAYER)):
        if where == "layer":
            last = [None, None]
        for n, k in enumerate(keys):
            bank = k[-1] % 2
            T_NUM[k] = n + (len(T_FIRST) if where == "layer" else 0)
            T_BANK[k] = bank
            T_PREV[k] = last[bank]
            last[bank] = k


number_fills()
H_FIRST = [k for k in T_FIRST if k[0] not in NOT_SPLIT]
H_LAYER = [k for k in T_LAYER if k[0] not in NOT_SPLIT]
H_NUM = {k: n for n, k in enumerate(H_FIRST + H_LAYER)}
N_HL = len(H_LAYER)

PROJ = {k: n for n, k in enumerate([("av", c) for c in range(NA)] + QKVG + [("in", c) for c in range(NQ)] + [("mk", 0)]
                                   + [("in", NQ + c) for c in GATES])}
N_PL = NQ + NG + 1
HID = {k: n for n, k in enumerate([("au", c) for c in range(NA)] + [("fu", c) for c in range(NF)]
                                  + [("mu", c) for c in range(NU)])}
NORMS = {k: n for n, k in enumerate(["A", "V", "F", "KV", "K", "Q", "M", "X", "Mem", "U"])}
LATE = {k: n for n, k in enumerate(["A", "F", "KV", "M", "X", "Mem", "U"])}
XRS = {k: n for n, k in enumerate(["O0", "O", "M", "O2", "Y0", "Y"])}


def expert_units():
    keys = [("up", 0, j) for j in range(4)]
    for s in range(1, NS):
        keys += [("up", s, j) for j in range(4)] + [("dn", s - 1, i) for i in range(2)]
    return keys + [("dn", NS - 1, i) for i in range(2)]


EXPERT = expert_units()
N_EU = len(EXPERT)
EU = {k: n for n, k in enumerate(EXPERT)}
assert N_EU % RING == 0 and N_EU % E_RAW == 0
E_SCAT = 4

CAUSAL, NEAR, D4, D4OFF, D16, D16OFF = range(N_MASK)


def items_first():
    out = []
    for t in range(NT):
        n = 8 // (t + 1)
        for h0 in range(0, HEADS, n):
            out.append((t, [(h, [(h, h // 2, kt, ("v", h), CAUSAL if kt == t else None, h) for kt in range(t + 1)])
                            for h in range(h0, h0 + n)]))
    return out


def items_layer():
    out = []
    for t in range(NT):
        a = []
        for hh in range(H_A):
            tiles = []
            for g, (diag, off) in enumerate(((CAUSAL, NEAR), (D4, D4OFF), (D16, D16OFF))):
                head = 2 * g + hh
                tiles += [(head, head // 2, kt, ("a", head), diag if kt == t else off, None) for kt in range(t + 1)]
            a.append((hh, tiles))
        b = [(H_A + H_M + h, [(6 + h, 3 + h // 2, kt, ("b", h), CAUSAL if kt == t else None, None) for kt in range(t + 1)])
             for h in range(H_B)]
        m = [(H_A + h, [(12 + h, 6 + h // 2, kt, ("m", h), None, None) for kt in range(NT)])
             for h in range(H_M)]
        if t == 0:
            out += [(t, a), (t, b)]
        else:
            out += [(t, a[0:1]), (t, a[1:2]), (t, b[0:3]), (t, b[3:6])]
        out.append((t, m))
    return out


ITEMS1, ITEMS2 = items_first(), items_layer()
BESIDE1 = [[0], [1], [2], [3], [4, 5], [6, 7], []]
BESIDE2 = [[6, 7], [8, 9], [10, 11], [12, 13], [14, 15], [16, 17], [18, 19], [20], [21]]
N_I1, N_I2 = len(ITEMS1), len(ITEMS2)
V_STEPS_LAYER = 21


def program(nc, x, mem, cst_d, masks_d, sml_d, gv_d, gm_d, gfin_d, a_w_in, a_w_spatial, a_w_out, f_w_in, f_w_out, kv_w,
            b_w_in, b_w_out, m_w_router, m_w_in, m_w_out, w_in_2, w_proj_2, w_out_2, w_mem_kv_2, w_up_2, w_down_2,
            out):
    ctx = ExitStack()
    with ctx:
        def sb(name, shape, dt=F32):
            return ctx.enter_context(nc.sbuf_tensor(name, shape, dt))

        def sem(name):
            return ctx.enter_context(nc.semaphore(name))

        raw = sb("raw", [P, RING, UNIT])
        w_hi = sb("w_hi", [P, RING, UNIT], F32R)
        w_lo = sb("w_lo", [P, RING, UNIT], F32R)
        h = sb("h", [P, NT, D])
        xr = sb("xr", [P, NT, D])
        x_hi = sb("x_hi", [P, KC, S], F32R)
        x_lo = sb("x_lo", [P, KC, S], F32R)
        t_hi = sb("t_hi", [P, KC, S], F32R)
        t_lo = sb("t_lo", [P, KC, S], F32R)
        gu = sb("gu", [P, NT, BANK])
        pr = sb("pr", [P, NT, BANK])
        arena = sb("arena", [P, 6 * NT * D])
        qz = sb("qz", [P, HEADS, S])
        kT = sb("kT", [P, KC, S])
        cst = sb("cst", [P, N_CST])
        sml = sb("sml", [P, N_SML])
        gcur = sb("gcur", [P, 3 * KC])
        identb = sb("identb", [P, P], BF16)
        maskb = sb("maskb", [P, N_MASK, P], BF16)
        wf = sb("wf", [P, KC, HEADS])
        wr = sb("wr", [P, KC, N_EXP])
        wr2 = sb("wr2", [P, KC, 2 * N_EXP], F32R)
        ss = sb("ss", [P, NT])
        var = sb("var", [P, 2 * HEADS])
        sd = sb("sd", [P, 2 * HEADS])
        rs = sb("rs", [P, 2 * HEADS])
        rsn = sb("rsn", [P, len(LATE), NT])
        ssv = sb("ssv", [P, NT, NA])
        nmx = sb("nmx", [P, 2, 8])
        sums = sb("sums", [P, NT, HEADS])
        rsum = sb("rsum", [P, NT, HEADS])
        npass_i = sb("npass_i", [P, 1], I32)

        ident = cst[:, C_ID:C_ID + P]
        tri = cst[:, C_TRI:C_TRI + P]
        iota = cst[:, C_IOTA:C_IOTA + P]
        iota8 = cst[:, C_IOTA:C_IOTA + N_EXP]
        ones = cst[:, C_ONES:C_ONES + P]
        ones2 = cst[:, C_ONES:C_ONES + S]

        mask_f = pr[:, :, :].rearrange("p t n -> p (t n)")[:, 0:N_MASK * P]

        def slab(n, width=NT * D, at=0):
            return arena[:, n * NT * D + at:n * NT * D + at + width]

        v_a = slab(0, NT * A_HALF).rearrange("p (t n) -> p t n", t=NT)
        gv_b = slab(3, A_HALF)
        wsT = slab(4, A_GROUPS * P, at=D).rearrange("p (g i) -> p g i", g=A_GROUPS)
        ws = slab(5, A_GROUPS * P).rearrange("p (g j) -> p g j", g=A_GROUPS)
        wsr = slab(5).rearrange("p (t g i) -> p t g i", t=NT, g=A_GROUPS)
        k_t = slab(0).rearrange("p (t n) -> p t n", t=NT)
        v_t = slab(1).rearrange("p (t n) -> p t n", t=NT)
        q_t = slab(2).rearrange("p (t n) -> p t n", t=NT)
        gate_t = slab(3).rearrange("p (t n) -> p t n", t=NT)
        sq_t = slab(4).rearrange("p (t n) -> p t n", t=NT)
        sel = slab(5).rearrange("p (h j) -> p h j", h=HEADS)
        fz = sq_t[:, 0, 0:S]
        fa = sq_t[:, 0, S:2 * S]
        fe = sq_t[:, 0, 2 * S:3 * S]
        ncum = sq_t[:, 1, 0:S]
        diag = pr[:, :, 0:P]
        gm_b = slab(0, D)
        disp = slab(0, NT * SLOTS, at=D).rearrange("p (t n) -> p t n", t=NT)
        dispg = slab(0, NT * SLOTS, at=D + 256).rearrange("p (t n) -> p t n", t=NT)
        comb = slab(0, S, at=D + 512)
        ye = slab(1, D)
        lg = slab(1, NT * 8, at=D).rearrange("p (t n) -> p t n", t=NT)
        mx8 = slab(1, NT * 8, at=D + 16).rearrange("p (t n) -> p t n", t=NT)
        mi8 = slab(1, NT * 8, at=D + 32).bitcast(U32).rearrange("p (t n) -> p t n", t=NT)
        mif = slab(1, NT * 8, at=D + 48).rearrange("p (t n) -> p t n", t=NT)
        gw = slab(1, NT * 4, at=D + 64).rearrange("p (t n) -> p t n", t=NT)
        one1 = slab(1, NT * 8, at=D + 80).rearrange("p (t n) -> p t n", t=NT)
        chosen = slab(1, NT * 8, at=D + 96).rearrange("p (t n) -> p t n", t=NT)
        gate1 = slab(1, NT * 8, at=D + 112).rearrange("p (t n) -> p t n", t=NT)
        gate2 = slab(1, NT * 8, at=D + 128).rearrange("p (t n) -> p t n", t=NT)
        gates = slab(1, NT * 16, at=D + 144).rearrange("p (t n) -> p t n", t=NT)
        place = slab(1, NT * 16, at=D + 176).rearrange("p (t n) -> p t n", t=NT)
        most = slab(1, 2, at=D + 208)
        qkv = slab(0, NT * 3 * D).rearrange("p (t n) -> p t n", t=NT)
        km = qkv[:, :, NQ * BANK:NQ * BANK + 2 * W_M]
        memr = slab(3).rearrange("p (t n) -> p t n", t=NT)
        gat = slab(3, NT * 3 * D).rearrange("p (t n) -> p t n", t=NT)
        rot = pr[:, :, :].rearrange("p t n -> p (t n)")[:, 0:768].rearrange("p (f g h r) -> p f g h r", f=4, g=2, h=12)
        gfin = slab(0, D)

        Y = ctx.enter_context(nc.psum_tensor("Y", [P, 4, BANK], F32))
        U = ctx.enter_context(nc.psum_tensor("U", [P, 2, BANK], F32))
        T = ctx.enter_context(nc.psum_tensor("T", [P, 2, BANK], F32))

        logit_bank = Y[:, 0:2, :].rearrange("p a n -> p (a n)")
        o_bank = T[:, :, :].rearrange("p a n -> p (a n)")
        p_sb = gu[:, :, :].rearrange("p a n -> p (a n)")
        pT_sb = pr[:, :, :].rearrange("p a n -> p (a n)")

        def pair(n):
            return [U[:, t, :] for t in range(NT)] if n % 2 == 0 else [Y[:, t, :] for t in range(NT)]

        side = [Y[:, NT + t, :] for t in range(NT)]

        def gate_unit(b):
            return ("in", NQ + GATES[b // 2]), b % 2

        s_const = sem("s_const")
        s_x = sem("s_x")
        s_mask = sem("s_mask")
        s_wsp = sem("s_wsp")
        s_gv = sem("s_gv")
        s_wf = sem("s_wf")
        s_wr = sem("s_wr")
        s_gm = sem("s_gm")
        s_mem = sem("s_mem")
        s_gfin = sem("s_gfin")
        s_zero = sem("s_zero")
        s_bf = sem("s_bf")
        loaded = [sem(f"loaded{i}") for i in range(RING)]
        hi_ready = sem("hi_ready")
        lo_ready = sem("lo_ready")
        unit_used = sem("unit_used")
        t_filled = sem("t_filled")
        t_split = sem("t_split")
        t_done = sem("t_done")
        g_cur = sem("g_cur")
        n_var = sem("n_var")
        n_sd = sem("n_sd")
        rs_ready = sem("rs_ready")
        y_tile = sem("y_tile")
        xr_ready = sem("xr_ready")
        proj_out = sem("proj_out")
        up_tile0 = sem("up_tile0")
        act_tile0 = sem("act_tile0")
        hid_act = sem("hid_act")
        hid_ready = sem("hid_ready")
        v_ready = sem("v_ready")
        sp_v = sem("sp_v")
        sp_a = sem("sp_a")
        h_done = sem("h_done")
        v_step = sem("v_step")
        f_diag = sem("f_diag")
        f_z = sem("f_z")
        f_e = sem("f_e")
        ncum_ready = sem("ncum_ready")
        l_filled = sem("l_filled")
        mx_ready = sem("mx_ready")
        p_ready = sem("p_ready")
        p_turned = sem("p_turned")
        pT_a = sem("pT_a")
        pT_v = sem("pT_v")
        pv_done = sem("pv_done")
        o_done = sem("o_done")
        pj_sums = sem("pj_sums")
        branch = sem("branch")
        r_wr = sem("r_wr")
        r_logits = sem("r_logits")
        r_diff = sem("r_diff")
        r_exp = sem("r_exp")
        r_chosen = sem("r_chosen")
        r_place = sem("r_place")
        r_done = sem("r_done")
        e_loaded = [sem(f"e_loaded{i}") for i in range(E_RAW)]
        e_hi = sem("e_hi")
        e_lo = sem("e_lo")
        e_used = sem("e_used")
        e_disp = sem("e_disp")
        e_gath = sem("e_gath")
        e_ghi = sem("e_ghi")
        e_glo = sem("e_glo")
        e_turn = sem("e_turn")
        e_comb = sem("e_comb")
        e_silu = sem("e_silu")
        e_hid = sem("e_hid")
        e_tf = sem("e_tf")
        e_thi = sem("e_thi")
        e_tlo = sem("e_tlo")
        e_y = sem("e_y")
        e_scat = sem("e_scat")
        e_add = sem("e_add")
        e_pass = sem("e_pass")
        s_out = sem("s_out")

        block = ctx.enter_context(nc.Block())

        def used(key, l=None):
            n = UNITS[key] + 1
            return n if l is None else l * N_LAYER + n

        def filled(key, l=None):
            n = T_NUM[key] + 1
            return n if l is None else l * N_TL + n

        def split(key, l=None):
            n = H_NUM[key] + 1
            return n if l is None else l * N_HL + n

        def proj(key, l=None):
            n = PROJ[key] + 1
            return n if l is None else l * N_PL + n

        def hid(key, l=None):
            n = HID[key] + 1
            return n if l is None else l * NU + n

        def norm_no(key, l=None):
            n = NORMS[key] + 1
            return n if l is None else l * 3 + n

        def xr_no(key, l=None):
            n = XRS[key] + 1
            return n if l is None else l * 3 + n

        def rs_no(key, l=None):
            n = LATE[key] + 1
            return n if l is None else l * 3 + n

        def late(key, t):
            return rsn[:, LATE[key], t:t + 1]

        def mlp_no(name, l=None):
            n = ["au", "fu", "mu"].index(name) + 1
            return n if l is None else l + n

        def sums_no(key, l=None):
            n = ["ad", "fd", "bo", "wo", "md"].index(key) + 1
            return n if l is None else l * 2 + n

        def item_no(i, l=None):
            return i + 1 if l is None else l * N_I2 + N_I1 + i + 1

        def o_no(t, l=None):
            return t + 1 if l is None else l * NT + NT + t + 1

        def unit_slot(u):
            return u % RING

        def e_raw(k):
            i = k % E_RAW
            return slab(2 + i) if i < E_RAW - RING else raw[:, i - (E_RAW - RING), :]


        @block.sync
        def _(sp):
            col = "(hf kc p) (c n) -> c hf p kc n"
            colf = dict(hf=2, kc=4, p=P, n=BANK)
            row2 = dict(i=2, kc=2, p=P)
            a_in = a_w_in[0].rearrange(col, **colf)
            a_out = a_w_out[0].rearrange("(c i kc p) n -> c i p kc n", **row2)
            f_in = f_w_in[0].rearrange("(hf kc p) (ab c n) -> c hf ab p kc n", hf=2, kc=4, p=P, ab=2, n=256)
            f_out = f_w_out[0].rearrange("(c kc p) n -> c p kc n", kc=2, p=P)
            kv_in = kv_w[:, 0:2 * D].rearrange(col, **colf)
            b_in = b_w_in[0].rearrange(col, **colf)
            b_out = b_w_out[0].rearrange("(i kc p) n -> i p kc n", kc=2, p=P)
            lcol = "l (hf kc p) (c n) -> l c hf p kc n"
            in2 = w_in_2.rearrange(lcol, **colf)
            mkv2 = w_mem_kv_2.rearrange(lcol, **colf)
            pj2 = w_proj_2.rearrange("l (i kc p) n -> l i p kc n", kc=2, p=P)
            wo2 = w_out_2.rearrange("l (i kc p) n -> l i p kc n", kc=2, p=P)
            up2 = w_up_2.rearrange(lcol, **colf)
            dn2 = w_down_2.rearrange("l (c i kc p) n -> l c i p kc n", **row2)
            first_src = {"av": lambda c, i: a_in[NA + c, i], "au": lambda c, i: a_in[c, i],
                         "ad": lambda c, i: a_out[c, i], "fd": lambda c: f_out[c],
                         "kv": lambda c, i: kv_in[c, i], "bi": lambda c, i: b_in[c, i], "bo": lambda i: b_out[i]}
            layer_src = {"in": lambda l, c, i: in2[l, c, i], "mk": lambda l, c, i: mkv2[l, c, i],
                         "pj": lambda l, i: pj2[l, i], "wo": lambda l, i: wo2[l, i],
                         "mu": lambda l, c, i: up2[l, c, i], "md": lambda l, c, i: dn2[l, c, i]}

            def dst(u, source):
                d = raw[:, unit_slot(u), :]
                return d.rearrange("p (kc n) -> p kc n", kc=source.shape[1])

            sp.dma_start(h[:, :, :], x.rearrange("b (t p) d -> p (b t) d", p=P)).then_inc(s_x, 16)
            sp.dma_start(cst[:, :], cst_d).then_inc(s_const, 16)
            sp.dma_start(sml[:, :], sml_d).then_inc(s_const, 16)
            for u, key in enumerate(FIRST):
                if u >= RING:
                    sp.wait_ge(lo_ready, u + 1 - RING)
                if key[0] == "fu":
                    both = raw[:, unit_slot(u), :].rearrange("p (kc ab n) -> p ab kc n", kc=4, ab=2)
                    for ab in range(2):
                        sp.dma_start(both[:, ab], f_in[key[1], key[2], ab]).then_inc(loaded[unit_slot(u)], 16)
                    continue
                source = first_src[key[0]](*key[1:])
                sp.dma_start(dst(u, source), source).then_inc(loaded[unit_slot(u)], 16)

            up_src = m_w_in[0].rearrange("e (hf kc p) (ab s n) -> e s ab hf p kc n", hf=2, kc=4, p=P, ab=2, n=BANK)
            dn_src = m_w_out[0].rearrange("e (s i kc p) n -> e s i p kc n", i=2, kc=2, p=P)
            sp.wait_ge(xr_ready, xr_no("O"))
            sp.sem_inc(e_lo, E_RAW)
            npass = sp.alloc_register("npass")
            with sp.Fori(0, npass) as ps:
                with sp.Fori(0, N_EXP) as e:
                    base = sp.snap((ps * N_EXP + e) * N_EU)
                    for k, key in enumerate(EXPERT):
                        if k == E_RAW - RING:
                            sp.wait_ge(lo_ready, N_FIRST)
                        sp.wait_ge(e_lo, base + (k + 1))
                        if key[0] == "up":
                            source = up_src[e, key[1], key[2] // 2, key[2] % 2]
                        else:
                            source = dn_src[e, key[1], key[2]]
                        d = e_raw(k).rearrange("p (kc n) -> p kc n", kc=source.shape[1])
                        sp.dma_start(d, source).then_inc(e_loaded[k % E_RAW], 16)
                sp.wait_ge(r_done, 1)
                sp.reg_load(npass, npass_i[0:1, 0:1])
            passes = sp.value_load(npass_i[0:1, 0:1], min_val=1, max_val=2)
            units = sp.snap(passes * (N_EXP * N_EU) + E_RAW)
            with sp.Fori(0, DEPTH) as l:
                sp.wait_ge(e_lo, units)
                for key in LAYER:
                    u = UNITS[key]
                    if u == N_FIRST + RING:
                        sp.wait_ge(h_done, l * 2 + 4)
                        sp.dma_start(memr, mem.rearrange("b (t p) d -> p (b t) d", p=P)).then_inc(s_mem, 16)
                    sp.wait_ge(lo_ready, l * N_LAYER + (u + 1 - RING))
                    source = layer_src[key[0]](l, *key[1:])
                    sp.dma_start(dst(u, source), source).then_inc(loaded[unit_slot(u)], 16)
            sp.wait_ge(xr_ready, xr_no("M") + DEPTH * 3 + 1)
            sp.dma_start(out.rearrange("b (t p) d -> p (b t) d", p=P), xr[:, :, :]).then_inc(s_out, 16)
            sp.wait_ge(s_out, 16)

        @block.gpsimd
        def _(pool):
            pool.dma_start(mask_f, masks_d).then_inc(s_mask, 16)
            pool.dma_start(ws, a_w_spatial[0].rearrange("g i j -> i g j")).then_inc(s_wsp, 16)
            pool.dma_start(gv_b, gv_d.partition_broadcast(P)).then_inc(s_gv, 16)
            pool.dma_start(wf[:, :, :], kv_w[:, 2 * D:2 * D + HEADS].rearrange("(kc p) n -> p kc n", p=P)).then_inc(s_wf, 16)
            pool.dma_start(wr[:, :, :], m_w_router[0].rearrange("(kc p) n -> p kc n", p=P)).then_inc(s_wr, 16)
            pool.memset(qz[:, :, :], 0.0).then_inc(s_zero, 1)
            pool.wait_ge(xr_ready, xr_no("O"))
            pool.dma_start(gm_b, gm_d.partition_broadcast(P)).then_inc(s_gm, 16)
            pool.wait_ge(h_done, DEPTH * 2 + 4)
            pool.dma_start(gfin, gfin_d.partition_broadcast(P)).then_inc(s_gfin, 16)

        @block.scalar
        def _(act):
            at = [0]

            def hi(u, l=None):
                s = unit_slot(u)
                n = LANDED[u]
                act.wait_ge(loaded[s], n if l is None else l * (N_LAYER // RING * 16) + n)
                if u >= RING:
                    n = u + 1 - RING
                    act.wait_ge(unit_used, n if l is None else l * N_LAYER + n)
                act.activation(w_hi[:, s, :], raw[:, s, :], ACT.Copy).then_inc(hi_ready, 1)

            def ahead(key, l=None):
                end = N_FIRST if l is None else N_FIRST + N_LAYER
                while at[0] < min(UNITS[key] + AHEAD + 1, end):
                    hi(at[0], l)
                    at[0] += 1

            def root(key, n, l=None):
                act.wait_ge(n_var, norm_no(key, l))
                act.activation(sd[:, 0:n], var[:, 0:n], ACT.Sqrt).then_inc(n_sd, 1)
                if key in LATE:
                    act.wait_ge(rs_ready, rs_no(key, l))

            def split_rows(name, dest, gain, l=None, groups=4, start=0):
                for g in range(start, groups):
                    act.wait_ge(t_filled, filled((name, g), l))
                    b = T_BANK[name, g]
                    if gain is None:
                        last = act.activation(dest[:, 2 * g:2 * g + 2, :].rearrange("p k n -> p (k n)"), T[:, b, :], ACT.Copy)
                    else:
                        for i in range(2):
                            kc = 2 * g + i
                            last = act.activation(dest[:, kc, :], T[:, b, i * S:(i + 1) * S], ACT.Copy,
                                                  scale=gain[:, kc:kc + 1])
                    last.then_inc(t_split, 1)

            def gains(c):
                return sml[:, c:c + KC]

            def evac(key, dest, func, banks, norm, l=None):
                ahead((*key, 1), l)
                act.wait_ge(unit_used, used((*key, 1), l))
                for t in range(NT):
                    last = act.activation(dest(t), banks[t], func, scale=late(norm, t))
                last.then_inc(proj_out, 1)

            def hidden(key, func, norm, l=None, width=BANK):
                ahead((*key, 0 if key[1] == 0 else 1), l)
                n = hid(key, l)
                if key != ("au", 0):
                    act.wait_ge(hid_ready, n - 1)
                for t in range(NT):
                    if key[1] == 0 and t == 0:
                        act.wait_ge(up_tile0, mlp_no(key[0], l))
                    else:
                        act.wait_ge(unit_used, used((*key, 1), l))
                    last = act.activation(gu[:, t, 0:width], U[:, t, 0:width], func, scale=late(norm, t))
                    if key[1] == 0 and t == 0:
                        last.then_inc(act_tile0, 1)
                last.then_inc(hid_act, 1)

            def split_hidden(key, chunks, buf, after, l=None):
                ahead(after, l)
                for b in range(chunks // 2):
                    k = (*key, b) if chunks == 4 else key
                    act.wait_ge(t_filled, filled(k, l))
                    d = t_hi[:, 4 * buf + 2 * b:4 * buf + 2 * b + 2, :]
                    act.activation(d.rearrange("p k n -> p (k n)"), T[:, T_BANK[k], :], ACT.Copy).then_inc(t_split, 1)

            def softmax(items, beside, l=None):
                beside(-1)
                for i in range(-1, len(items)):
                    if i >= 0:
                        beside(i)
                        pT_copy(i, l)
                    if i + 1 == len(items):
                        break
                    t, outs = items[i + 1]
                    act.wait_ge(mx_ready, item_no(i + 1, l))
                    at_col = 0
                    for j, (o, tiles) in enumerate(outs):
                        w = len(tiles) * P
                        last = act.activation(p_sb[:, at_col:at_col + w], logit_bank[:, at_col:at_col + w], ACT.Exp,
                                              bias=nmx[:, (i + 1) % 2, j:j + 1], accum_out=sums[:, t, o:o + 1])
                        at_col += w
                    last.then_inc(p_ready, 1)

            def pT_copy(i, l):
                act.wait_ge(p_turned, item_no(i, l))
                act.activation(pT_sb[:, 0:BANK], U[:, 0, :], ACT.Copy).then_inc(pT_a, 1)

            act.wait_ge(s_const, 32)
            split_rows("nA", x_hi, gains(G_A), groups=2)
            hi(0)
            at[0] = 1
            split_rows("nA", x_hi, gains(G_A), start=2)
            ahead(("av", 0, 0))
            root("A", NT)
            for c in range(NA):
                evac(("av", c), lambda t: v_a[:, t, c * BANK:(c + 1) * BANK], ACT.Gelu, pair(c), "A")
            root("V", NT)
            for c in range(NA):
                hidden(("au", c), ACT.Gelu, "A")
                if c == 0:
                    for j in range(1, NT * A_GROUPS, 2):
                        t, g = j // A_GROUPS, j % A_GROUPS
                        act.wait_ge(t_filled, filled(("sp", j)))
                        act.activation(v_a[:, t, g * A_GD:(g + 1) * A_GD], T[:, T_BANK["sp", j], 0:A_GD], ACT.Identity,
                                       bias=sml[:, G_BT + g:G_BT + g + 1]).then_inc(sp_a, 1)
                split_hidden(("au", c), 4, c % 2, ("au", 0, 1) if c == 0 else ("ad", c - 1, 1))
            ahead(("ad", NA - 1, 1))
            split_rows("nF", x_hi, gains(G_F))
            root("F", NT)
            for c in range(NF):
                hidden(("fu", c), ACT.Silu, "F", width=256)
                split_hidden(("fu", c), 2, c % 2, ("fu", 0, 1) if c == 0 else ("fd", c - 1))
            ahead(("fd", NF - 1))
            split_rows("nKV", x_hi, gains(G_KV))
            root("KV", NT)
            def evac_part(key, banks):
                name, c = key
                dest = {"kv": (k_t, v_t), "bi": (q_t, gate_t)}[name][c // 2]
                evac(key, lambda t: dest[:, t, c % 2 * BANK:(c % 2 + 1) * BANK],
                     ACT.Sigmoid if name == "bi" and c >= 2 else ACT.Copy, banks, "KV")

            evac_part(QKVG[0], pair(0))
            split_rows("nB", t_hi, gains(G_B), groups=2)
            evac_part(QKVG[1], pair(1))
            split_rows("nB", t_hi, gains(G_B), start=2)
            ahead(("bi", 0, 0))
            root("K", 2 * HEADS)
            for n in range(2, 4):
                evac_part(QKVG[n], pair(n))
            ahead(("kv", 2, 0))
            root("Q", 2 * HEADS)
            ahead(("kv", 2, 1))
            act.wait_ge(f_z, 1)
            act.activation(fe[0:HEADS, :], fa[0:HEADS, :], ACT.Exp).then_inc(f_e, 1)
            evac_part(("kv", 2), side)
            act.wait_ge(f_z, 2)
            act.activation(fe[0:HEADS, :], fa[0:HEADS, :], ACT.Ln).then_inc(f_e, 1)

            def beside1(i):
                if i in (-1, 3, 5):
                    evac_part(QKVG[{-1: 5, 3: 6, 5: 7}[i]], side)
                if BESIDE1[i + 1]:
                    u = BESIDE1[i + 1][-1] // 2
                    ahead(("bi", 2 + u // 2, u % 2))

            softmax(ITEMS1, beside1)
            split_rows("oT", x_hi, None)
            ahead(("bo", 3))
            split_rows("nM", x_hi, gains(G_M))
            root("M", NT)
            act.wait_ge(r_diff, 1)
            act.activation(gw[:, :, 1:2], gw[:, :, 0:1], ACT.Exp).then_inc(r_exp, 1)
            act.wait_ge(unit_used, N_FIRST)
            act.sem_inc(e_used, RING)
            def gather_hi(b, n):
                act.wait_ge(e_gath, n)
                act.activation(x_hi[:, 4 * b:4 * b + 4, 0:SLOTS], Y[:, 3 - b, :].rearrange("p (k n) -> p k n", k=4),
                               ACT.Copy).then_inc(e_ghi, 1)

            def output():
                for n in range(2):
                    last = act.activation(ye[:, n * BANK:(n + 1) * BANK], Y[:, n, :], ACT.Copy)
                last.then_inc(e_y, 1)

            npass = act.alloc_register("npass")
            with act.Fori(0, npass) as ps:
                g0 = act.snap(ps * (2 * (N_EXP + 1)))
                with act.Fori(0, N_EXP) as e:
                    n = act.snap(ps * N_EXP + e)
                    base = act.snap(n * N_EU)
                    ld = act.snap(n * (N_EU // E_RAW * 16))
                    step0 = act.snap(n * NS)
                    gath0 = act.snap(g0 + e * 2)
                    k = 0

                    def e_hi_next():
                        nonlocal k
                        s = unit_slot(k)
                        act.wait_ge(e_loaded[k % E_RAW], ld + (k // E_RAW + 1) * 16)
                        act.wait_ge(e_used, base + (k + 1))
                        act.activation(w_hi[:, s, :], e_raw(k), ACT.Copy).then_inc(e_hi, 1)
                        k += 1

                    def e_ahead(n):
                        while k < min(n + AHEAD + 1, N_EU):
                            e_hi_next()

                    e_hi_next()
                    for b in range(2):
                        gather_hi(b, gath0 + (b + 1))
                    e_ahead(-1)
                    act.wait_ge(e_used, base + RING)
                    output()
                    for s in range(NS):
                        e_ahead(EU["up", s, 3])
                        act.wait_ge(e_used, base + (EU["up", s, 3] + 1 + RING))
                        if s >= 1:
                            act.wait_ge(e_hid, step0 + s)
                        act.activation(gu[:, 0, :], U[:, 0, :], ACT.Silu).then_inc(e_silu, 1)
                        if s >= 1:
                            e_ahead(EU["dn", s - 1, 1])
                        act.wait_ge(e_tf, step0 + (s + 1))
                        act.activation(t_hi[:, 4 * (s % 2):4 * (s % 2) + 4, 0:SLOTS],
                                       T[:, s % 2, :].rearrange("p (k n) -> p k n", k=4), ACT.Copy).then_inc(e_thi, 1)
                    e_ahead(N_EU)
                act.wait_ge(r_done, 1)
                act.reg_load(npass, npass_i[0:1, 0:1])
            passes = act.value_load(npass_i[0:1, 0:1], min_val=1, max_val=2)
            act.wait_ge(e_used, passes * (N_EXP * N_EU) + RING)
            output()
            with act.Fori(0, DEPTH) as l:
                at[0] = N_FIRST
                for u in range(N_FIRST, N_FIRST + AHEAD):
                    hi(u, l)
                    at[0] += 1
                act.wait_ge(g_cur, l + 1)
                split_rows("nX", x_hi, gcur[:, 0:KC], l)
                ahead(("in", 0, 0), l)
                root("X", NT, l)
                for c in range(NQ):
                    evac(("in", c), lambda t: qkv[:, t, c * BANK:(c + 1) * BANK], ACT.Copy, pair(c), "X", l)
                    if c in (1, 2):
                        split_rows("nMem", t_hi, gcur[:, KC:2 * KC], l, groups=2 * c, start=2 * c - 2)
                    if c == 2:
                        root("Mem", NT, l)
                evac(("mk", 0), lambda t: km[:, t, :], ACT.Copy, pair(NQ), "Mem", l)

                def evac_gate(n):
                    c = GATES[n]
                    evac(("in", NQ + c), lambda t: gat[:, t, c * BANK:(c + 1) * BANK], ACT.Sigmoid, side, "X", l)

                def ahead_gate(b):
                    key, hf = gate_unit(b)
                    ahead((*key, hf), l)

                ahead_gate(0)
                evac_gate(0)
                ahead_gate(2)

                def beside2(i):
                    if i >= 0 and i % 2 == 0:
                        evac_gate(1 + i // 2)
                    ahead_gate(min(4 + i, 10))

                softmax(ITEMS2, beside2, l)
                ahead_gate(11)
                split_rows("oT2", t_hi, None, l, groups=3)
                evac_gate(NG - 1)
                ahead(("pj", 2), l)
                split_rows("yT", x_hi, None, l)
                ahead(("wo", 3), l)
                split_rows("nU", x_hi, gcur[:, 2 * KC:3 * KC], l)
                root("U", NT, l)
                for c in range(NU):
                    hidden(("mu", c), ACT.Relu, "U", l)
                    split_hidden(("mu", c), 4, c % 2, ("mu", 0, 1) if c == 0 else ("md", c - 1, 1), l)
                ahead(("md", NU - 1, 1), l)
            act.wait_ge(n_var, norm_no("X") + DEPTH * 3)
            act.activation(sd[:, 0:NT], var[:, 0:NT], ACT.Sqrt).then_inc(n_sd, 1)

        @block.vector
        def _(dve):
            at = [0]
            steps = [0, None]

            def order(ins):
                steps[0] += 1
                ins.then_inc(v_step, 1)
                dve.wait_ge(v_step, steps[0] if steps[1] is None else steps[1] + steps[0])

            def lo(u, l=None):
                s = unit_slot(u)
                dve.wait_ge(hi_ready, u + 1 if l is None else l * N_LAYER + (u + 1))
                dve.tensor_tensor(w_lo[:, s, :], raw[:, s, :], w_hi[:, s, :].bitcast(F32), ALU.subtract).then_inc(lo_ready, 1)

            def ahead(key, l=None):
                end = N_FIRST if l is None else N_FIRST + N_LAYER
                while at[0] < min(UNITS[key] + AHEAD + 1, end):
                    lo(at[0], l)
                    at[0] += 1

            def row_scale(src, key, l=None):
                for t in range(NT):
                    last = dve.scalar_tensor_tensor(xr[:, t, :], src[:, t, :], 1.0, src[:, t, :], ALU.mult, ALU.mult,
                                                    accum_out=ss[:, t:t + 1])
                order(last)
                dve.tensor_scalar(var[:, 0:NT], ss[:, 0:NT], 1.0 / D, EPS, ALU.mult, ALU.add).then_inc(n_var, 1)
                if key not in LATE:
                    return inverse(NT, key, l)
                dve.wait_ge(n_sd, norm_no(key, l))
                refine(NT, rsn[:, LATE[key], :]).then_inc(rs_ready, 1)

            def inverse(n, key, l=None):
                dve.wait_ge(n_sd, norm_no(key, l))
                order(refine(n, rs[:, 0:n]))

            def refine(n, dest):
                order(dve.reciprocal(rs[:, 0:n], sd[:, 0:n]))
                order(dve.tensor_tensor(sd[:, 0:n], rs[:, 0:n], rs[:, 0:n], ALU.mult))
                order(dve.tensor_tensor(sd[:, 0:n], sd[:, 0:n], var[:, 0:n], ALU.mult))
                order(dve.tensor_scalar(sd[:, 0:n], sd[:, 0:n], -0.5, 1.5, ALU.mult, ALU.add))
                return dve.tensor_tensor(dest, rs[:, 0:n], sd[:, 0:n], ALU.mult)

            def split_rows(name, hi_d, lo_d, gain, l=None, groups=4, start=0):
                for g in range(start, groups):
                    dve.wait_ge(t_split, split((name, g), l))
                    b = T_BANK[name, g]
                    if gain is None:
                        sl = slice(2 * g, 2 * g + 2)
                        last = dve.tensor_tensor(lo_d[:, sl, :].rearrange("p k n -> p (k n)"), T[:, b, :],
                                                 hi_d[:, sl, :].rearrange("p k n -> p (k n)").bitcast(F32), ALU.subtract)
                    else:
                        for i in range(2):
                            kc = 2 * g + i
                            last = dve.scalar_tensor_tensor(lo_d[:, kc, :], T[:, b, i * S:(i + 1) * S], gain[:, kc:kc + 1],
                                                            hi_d[:, kc, :].bitcast(F32), ALU.mult, ALU.subtract)
                    last.then_inc(t_done, 1)

            def gains(c):
                return sml[:, c:c + KC]

            def wait_act(key, t, l=None):
                if key[1] == 0 and t == 0:
                    dve.wait_ge(act_tile0, mlp_no(key[0], l))
                else:
                    dve.wait_ge(hid_act, hid(key, l))

            def gated(key, other, l=None):
                if key != ("au", 0):
                    ahead((*key, 0 if key[1] == 0 else 1), l)
                for t in range(NT):
                    wait_act(key, t, l)
                    last = dve.tensor_tensor(pr[:, t, :], gu[:, t, :], other(t), ALU.mult)
                last.then_inc(hid_ready, 1)

            def split_hidden(key, chunks, buf, after, l=None):
                ahead(after, l)
                for b in range(chunks // 2):
                    k = (*key, b) if chunks == 4 else key
                    dve.wait_ge(t_split, split(k, l))
                    sl = slice(4 * buf + 2 * b, 4 * buf + 2 * b + 2)
                    dve.tensor_tensor(t_lo[:, sl, :].rearrange("p k n -> p (k n)"), T[:, T_BANK[k], :],
                                      t_hi[:, sl, :].rearrange("p k n -> p (k n)").bitcast(F32),
                                      ALU.subtract).then_inc(t_done, 1)

            def add_residual(key, l=None):
                ahead(key, l)
                dve.wait_ge(y_tile, sums_no(key[0], l))
                add_tile(0)
                dve.wait_ge(unit_used, used(key, l))
                add_tile(1).then_inc(h_done, 1)

            def add_tile(t):
                for n in range(2):
                    hs = h[:, t, n * BANK:(n + 1) * BANK]
                    last = dve.tensor_tensor(hs, hs, Y[:, 2 * t + n, :], ALU.add)
                return last

            def after_h(n):
                dve.wait_ge(h_done, n)

            def softmax(items, beside, finish, l=None):
                for i in range(-1, len(items)):
                    if i >= 0:
                        n = sum(len(o[1]) for o in items[i][1]) * P
                        dve.wait_ge(p_turned, item_no(i, l))
                        dve.tensor_copy(pT_sb[:, BANK:n], U[:, 1, 0:n - BANK]).then_inc(pT_v, 1)
                    if i + 1 < len(items):
                        outs = items[i + 1][1]
                        w = len(outs[0][1]) * P
                        dve.wait_ge(l_filled, item_no(i + 1, l))
                        dve.tensor_reduce(nmx[:, (i + 1) % 2, 0:len(outs)],
                                          logit_bank[:, 0:len(outs) * w].rearrange("p (o w) -> p o w", w=w),
                                          AX.X, ALU.max, negate=True).then_inc(mx_ready, 1)
                    beside(i)
                    if i >= 0 and (i + 1 == len(items) or items[i + 1][0] != items[i][0]):
                        dve.wait_ge(pv_done, item_no(i, l))
                        finish(items[i][0])

            def over_sums(t, n):
                order(dve.reciprocal(rsum[:, t, 0:n], sums[:, t, 0:n]))
                return dve.tensor_tensor(xr[:, t, 0:n * HD].rearrange("p (o d) -> p o d", d=HD),
                                         o_bank[:, 0:n * HD].rearrange("p (o d) -> p o d", d=HD),
                                         rsum[:, t, 0:n].unsqueeze(2).to_broadcast([P, n, HD]), ALU.mult)

            dve.wait_ge(s_const, 32)
            dve.wait_ge(s_x, 16)
            split_rows("nA", x_hi, x_lo, gains(G_A), groups=2)
            lo(0)
            at[0] = 1
            split_rows("nA", x_hi, x_lo, gains(G_A), start=2)
            ahead(("av", 0, 0))
            row_scale(h, "A")
            dve.wait_ge(s_mask, 16)
            dve.tensor_copy(identb[:, :], ident).then_inc(s_bf, 1)
            dve.tensor_copy(maskb[:, :, :].rearrange("p m n -> p (m n)"), mask_f).then_inc(s_bf, 1)
            dve.wait_ge(s_bf, 2)
            for c in range(NA):
                ahead(("av", c, 1))
                if c == 1:
                    for i in range(2):
                        dve.wait_ge(t_filled, filled(("wsT", i)))
                        dve.tensor_copy(wsT[:, 4 * i:4 * i + 4, :].rearrange("p g n -> p (g n)"),
                                        T[:, T_BANK["wsT", i], :]).then_inc(t_done, 1)
                    dve.wait_ge(t_done, filled(("wsT", 1)))
                    dve.memset(wsT[HD:P, :, 0:HD], 0.0)
                dve.wait_ge(proj_out, proj(("av", c)))
                for t in range(NT):
                    vs = v_a[:, t, c * BANK:(c + 1) * BANK]
                    last = dve.scalar_tensor_tensor(pr[:, t, :], vs, 1.0, vs, ALU.mult, ALU.mult,
                                                    accum_out=ssv[:, t, c:c + 1])
                order(last)
                if c == 0:
                    dve.wait_ge(s_gv, 16)
                for t in range(NT):
                    vs = v_a[:, t, c * BANK:(c + 1) * BANK]
                    last = dve.tensor_tensor(vs, vs, gv_b[:, c * BANK:(c + 1) * BANK], ALU.mult)
            order(dve.tensor_reduce(ss[:, :], ssv[:, :, :], AX.X, ALU.add))
            dve.tensor_scalar(var[:, 0:NT], ss[:, :], 1.0 / A_HALF, EPS, ALU.mult, ALU.add).then_inc(n_var, 1)
            inverse(NT, "V")
            for t in range(NT):
                dve.tensor_scalar(wsr[:, t, :, :].rearrange("p g i -> p (g i)"), wsT[:, :, :].rearrange("p g i -> p (g i)"),
                                  rs[:, t:t + 1], None, ALU.mult).then_inc(v_ready, 1)
            for j in range(0, NT * A_GROUPS, 2):
                t, g = j // A_GROUPS, j % A_GROUPS
                dve.wait_ge(t_filled, filled(("sp", j)))
                dve.tensor_scalar(v_a[:, t, g * A_GD:(g + 1) * A_GD], T[:, T_BANK["sp", j], 0:A_GD],
                                  sml[:, G_BT + g:G_BT + g + 1], None, ALU.add).then_inc(sp_v, 1)
            dve.wait_ge(sp_v, A_GROUPS * NT // 2)
            dve.wait_ge(sp_a, A_GROUPS * NT // 2)
            dve.sem_inc(t_done, NT * A_GROUPS)
            for c in range(NA):
                gated(("au", c), lambda t: v_a[:, t, c * BANK:(c + 1) * BANK])
                split_hidden(("au", c), 4, c % 2, ("au", 0, 1) if c == 0 else ("ad", c - 1, 1))
            add_residual(("ad", NA - 1, 1))
            after_h(1)
            split_rows("nF", x_hi, x_lo, gains(G_F))
            row_scale(h, "F")
            dve.wait_ge(rs_ready, rs_no("F"))
            for c in range(NF):
                ahead(("fu", c, 0 if c == 0 else 1))
                for t in range(NT):
                    wait_act(("fu", c), t)
                    last = dve.scalar_tensor_tensor(pr[:, t, 0:256], U[:, t, 256:512], late("F", t), gu[:, t, 0:256],
                                                    ALU.mult, ALU.mult)
                last.then_inc(hid_ready, 1)
                split_hidden(("fu", c), 2, c % 2, ("fu", 0, 1) if c == 0 else ("fd", c - 1))
            add_residual(("fd", NF - 1))
            dve.wait_ge(s_wr, 16)
            order(dve.tensor_copy(wr2[:, :, 0:N_EXP], wr[:, :, :]))
            dve.tensor_tensor(wr2[:, :, N_EXP:2 * N_EXP], wr[:, :, :], wr2[:, :, 0:N_EXP].bitcast(F32),
                              ALU.subtract).then_inc(r_wr, 1)
            after_h(2)
            split_rows("nKV", x_hi, x_lo, gains(G_KV))
            row_scale(h, "KV")
            dve.wait_ge(rs_ready, rs_no("KV"))
            for t in range(NT):
                last = dve.tensor_scalar(diag[:, t, :], ident, late("KV", t), None, ALU.mult)
            last.then_inc(f_diag, 1)
            dve.tensor_copy(sel, ident[:, 0:HEADS].unsqueeze(2).to_broadcast([P, HEADS, P]))

            def head_norm(rows, key, after):
                for t in range(NT):
                    order(dve.tensor_tensor(sq_t[:, t, :], rows[:, t, :], rows[:, t, :], ALU.mult))
                    last = dve.tensor_reduce(var[:, t * HEADS:(t + 1) * HEADS],
                                             sq_t[:, t, :].rearrange("p (o d) -> p o d", d=HD), AX.X, ALU.add)
                order(last)
                dve.tensor_scalar(var[:, :], var[:, :], 1.0 / HD, EPS, ALU.mult, ALU.add).then_inc(n_var, 1)
                ahead(after)
                inverse(2 * HEADS, key)
                for t in range(NT):
                    r3 = rows[:, t, :].rearrange("p (o d) -> p o d", d=HD)
                    last = dve.tensor_tensor(r3, r3, rs[:, t * HEADS:(t + 1) * HEADS].unsqueeze(2).to_broadcast([P, HEADS, HD]),
                                             ALU.mult)
                last.then_inc(v_ready, 1)

            ahead(("kv", 0, 1))
            split_rows("nB", t_hi, t_lo, gains(G_B), groups=2)
            ahead(("kv", 1, 1))
            split_rows("nB", t_hi, t_lo, gains(G_B), start=2)
            dve.wait_ge(proj_out, proj(("kv", 1)))
            head_norm(k_t, "K", ("bi", 0, 0))
            ahead(("bi", 1, 1))
            dve.wait_ge(proj_out, proj(("bi", 1)))
            head_norm(q_t, "Q", ("kv", 2, 0))
            order(dve.memset(sq_t[:, :, :], 0.0))
            dve.wait_ge(t_filled, filled(("fT", 0)))
            order(dve.tensor_copy(fe[0:HEADS, :], T[0:HEADS, 0, S:2 * S]))
            dve.tensor_tensor(fz[0:HEADS, :], T[0:HEADS, 0, 0:S], fe[0:HEADS, :], ALU.mult).then_inc(t_done, 1)
            dve.wait_ge(t_done, filled(("fT", 0)))
            order(dve.tensor_scalar(fz[0:HEADS, :], fz[0:HEADS, :], sml[0:HEADS, G_BF:G_BF + 1], None, ALU.add))
            order(dve.tensor_scalar(fe[0:HEADS, :], fz[0:HEADS, :], -1.0, None, ALU.mult))
            dve.tensor_tensor(fa[0:HEADS, :], fe[0:HEADS, :], fz[0:HEADS, :], ALU.min).then_inc(f_z, 1)
            ahead(("kv", 2, 1))
            dve.wait_ge(f_e, 1)
            dve.tensor_scalar(fa[0:HEADS, :], fe[0:HEADS, :], 1.0, None, ALU.add).then_inc(f_z, 1)
            for g in range(4):
                dve.wait_ge(t_filled, filled(("kT", g)))
                dve.tensor_scalar(kT[:, 2 * g:2 * g + 2, :].rearrange("p k n -> p (k n)"), T[:, T_BANK["kT", g], :],
                                  sml[:, G_K:G_K + 1], None, ALU.mult).then_inc(t_done, 1)
            dve.wait_ge(f_e, 2)
            order(dve.scalar_tensor_tensor(fa[0:HEADS, :], fz[0:HEADS, :], 0.0, fe[0:HEADS, :], ALU.min, ALU.subtract))
            dve.tensor_tensor_scan(ncum[0:HEADS, :], ones2[0:HEADS, :], fa[0:HEADS, :], 0.0, ALU.mult, ALU.subtract).then_inc(ncum_ready, 1)
            ahead(("kv", 3, 0))
            dve.wait_ge(s_zero, 1)
            for g in range(4):
                dve.wait_ge(t_filled, filled(("qT", g)))
                for half in range(2):
                    r = slice(half * HD, (half + 1) * HD)
                    last = dve.tensor_scalar(qz[r, 4 * g + half:4 * g + 4:2, :],
                                             T[r, T_BANK["qT", g], :].rearrange("p (k n) -> p k n", k=2),
                                             sml[r, G_Q:G_Q + 1], HD ** -0.5, ALU.mult, ALU.mult)
                last.then_inc(t_done, 1)

            ahead(("kv", 3, 1))

            def output_gate(t):
                dve.tensor_tensor(xr[:, t, :], xr[:, t, :], gate_t[:, t, :], ALU.mult).then_inc(xr_ready, 1)

            def finish1(t):
                over_sums(t, HEADS).then_inc(o_done, 1)

            def beside1(i):
                if BESIDE1[i + 1]:
                    u = BESIDE1[i + 1][-1] // 2
                    ahead(("bi", 2 + u // 2, u % 2))
                if i == N_I1 - 1:
                    dve.wait_ge(o_done, o_no(0))
                    dve.wait_ge(proj_out, proj(("bi", 3)))
                    output_gate(0)

            softmax(ITEMS1, beside1, finish1)
            dve.wait_ge(o_done, o_no(1))
            output_gate(1)
            split_rows("oT", x_hi, x_lo, None)
            add_residual(("bo", 3))
            after_h(3)
            split_rows("nM", x_hi, x_lo, gains(G_M))
            row_scale(h, "M")
            dve.wait_ge(rs_ready, rs_no("M"))
            dve.wait_ge(s_gm, 16)
            for t in range(NT):
                last = dve.scalar_tensor_tensor(xr[:, t, :], h[:, t, :], late("M", t), gm_b, ALU.mult, ALU.mult)
            last.then_inc(xr_ready, 1)
            dve.wait_ge(r_logits, 1)
            order(dve.tensor_copy(lg, U[:, :, N_EXP:2 * N_EXP]))
            order(dve.tensor_tensor(lg, U[:, :, 0:N_EXP], lg, ALU.add))
            for t in range(NT):
                last = dve.tensor_scalar(lg[:, t, :], lg[:, t, :], late("M", t), None, ALU.mult)
            order(last)
            for t in range(NT):
                last = dve.max(mx8[:, t, :], lg[:, t, :])
            order(last)
            for t in range(NT):
                last = dve.max_index(mi8[:, t, :], mx8[:, t, :], lg[:, t, :])
            order(last)
            dve.tensor_tensor(gw[:, :, 0:1], mx8[:, :, 1:2], mx8[:, :, 0:1], ALU.subtract).then_inc(r_diff, 1)
            order(dve.tensor_copy(mif, mi8))
            for t in range(NT):
                last = dve.tensor_scalar(one1[:, t, :], iota8, mif[:, t, 0:1], None, ALU.is_equal)
            order(last)
            for t in range(NT):
                last = dve.scalar_tensor_tensor(chosen[:, t, :], iota8, mif[:, t, 1:2], one1[:, t, :], ALU.is_equal, ALU.add)
            last.then_inc(r_chosen, 1)
            dve.wait_ge(r_exp, 1)
            order(dve.tensor_scalar(gw[:, :, 2:3], gw[:, :, 1:2], 1.0, None, ALU.add))
            order(dve.reciprocal(gw[:, :, 2:3], gw[:, :, 2:3]))
            order(dve.tensor_tensor(gw[:, :, 3:4], gw[:, :, 1:2], gw[:, :, 2:3], ALU.mult))
            for t in range(NT):
                dve.tensor_scalar(gate1[:, t, :], iota8, mif[:, t, 0:1], gw[:, t, 2:3], ALU.is_equal, ALU.mult)
                last = dve.tensor_scalar(gate2[:, t, :], iota8, mif[:, t, 1:2], gw[:, t, 3:4], ALU.is_equal, ALU.mult)
            order(last)
            order(dve.memset(gates, 0.0))
            dve.memset(place, -1.0)
            dve.memset(comb, 0.0).then_inc(e_comb, 1)
            order(dve.tensor_tensor(gates[:, :, 0:N_EXP], gate1, gate2, ALU.add))
            dve.wait_ge(r_place, 1)
            order(dve.scalar_tensor_tensor(place[:, :, 0:N_EXP], U[:, :, 16:16 + N_EXP], 1.0, chosen, ALU.add, ALU.mult))
            dve.tensor_scalar(place[:, :, 0:N_EXP], place[:, :, 0:N_EXP], -1.0, None, ALU.add)
            order(dve.tensor_reduce(most[:, 0:1], U[:, 0, 32:32 + N_EXP], AX.X, ALU.max))
            order(dve.tensor_scalar(most[:, 1:2], most[:, 0:1], SLOTS + 0.5, 1.0, ALU.is_gt, ALU.add))
            dve.tensor_copy(npass_i[:, :], most[:, 1:2]).then_inc(r_done, 1)
            dve.wait_ge(r_done, 1)
            npass = dve.value_load(npass_i[0:1, 0:1], min_val=1, max_val=2)

            def dispatch(e):
                for t in range(NT):
                    col = place[:, t, bass.ds(e, 1)]
                    dve.tensor_scalar(disp[:, t, :], iota, col, None, ALU.is_equal)
                    last = dve.tensor_scalar(dispg[:, t, :], iota, col, gates[:, t, bass.ds(e, 1)], ALU.is_equal, ALU.mult)
                last.then_inc(e_disp, 1)

            def gather_lo(b, n):
                dve.wait_ge(e_ghi, n)
                dve.tensor_tensor(x_lo[:, 4 * b:4 * b + 4, 0:SLOTS], Y[:, 3 - b, :].rearrange("p (k n) -> p k n", k=4),
                                  x_hi[:, 4 * b:4 * b + 4, 0:SLOTS].bitcast(F32), ALU.subtract).then_inc(e_glo, 1)

            def put_back(j, n, banks):
                dve.wait_ge(e_scat, n)
                hs = h[:, j // 2, j % 2 * BANK:(j % 2 + 1) * BANK]
                dve.tensor_tensor(hs, hs, banks[j], ALU.add).then_inc(e_add, 1)

            in_loop = [Y[:, 2, :], Y[:, 3, :], Y[:, 2, :], Y[:, 3, :]]
            with dve.Fori(0, npass) as ps:
                dispatch(0)
                with dve.Fori(0, N_EXP) as e:
                    n = dve.snap(ps * N_EXP + e)
                    base = dve.snap(n * N_EU)
                    step0 = dve.snap(n * NS)
                    scat0 = dve.snap(n * E_SCAT)
                    k = 0

                    def e_lo_next():
                        nonlocal k
                        s = unit_slot(k)
                        dve.wait_ge(e_hi, base + (k + 1))
                        dve.tensor_tensor(w_lo[:, s, :], e_raw(k), w_hi[:, s, :].bitcast(F32), ALU.subtract).then_inc(e_lo, 1)
                        k += 1

                    def e_ahead(n):
                        while k < min(n + AHEAD + 1, N_EU):
                            e_lo_next()

                    e_lo_next()
                    for b in range(2):
                        gather_lo(b, n * 2 + (b + 1))
                    e_ahead(-1)
                    for s in range(NS):
                        e_ahead(EU["up", s, 3])
                        dve.wait_ge(e_silu, step0 + (s + 1))
                        dve.tensor_tensor(pr[:, 0, :], gu[:, 0, :], U[:, 1, :], ALU.mult).then_inc(e_hid, 1)
                        if s >= 1:
                            e_ahead(EU["dn", s - 1, 1])
                        dve.wait_ge(e_thi, step0 + (s + 1))
                        sl = slice(4 * (s % 2), 4 * (s % 2) + 4)
                        dve.tensor_tensor(t_lo[:, sl, 0:SLOTS], T[:, s % 2, :].rearrange("p (k n) -> p k n", k=4),
                                          t_hi[:, sl, 0:SLOTS].bitcast(F32), ALU.subtract).then_inc(e_tlo, 1)
                        if s < 2:
                            for j in (2 * s, 2 * s + 1):
                                put_back(j, scat0 + (j + 1), in_loop)
                        if s == 2:
                            dve.wait_ge(e_turn, n + 1)
                            dve.tensor_copy(comb, Y[:, 2, 0:S]).then_inc(e_comb, 1)
                            dispatch(e + 1)
                    e_ahead(N_EU)
                dve.tensor_scalar(place, place, -float(SLOTS), None, ALU.add).then_inc(e_pass, 1)
                dve.wait_ge(e_pass, ps + 1)
            first_steps = steps[0]
            with dve.Fori(0, DEPTH) as l:
                at[0] = N_FIRST
                steps[0], steps[1] = 0, dve.snap(l * V_STEPS_LAYER + first_steps)
                dve.tensor_copy(gcur[:, :], sml[:, bass.ds(l * (3 * KC) + G_L, 3 * KC)]).then_inc(g_cur, 1)
                dve.wait_ge(e_scat, npass * (N_EXP * E_SCAT) + E_SCAT)
                dve.wait_ge(y_tile, l * 2 + sums_no("bo"))
                add_tile(0)
                dve.wait_ge(unit_used, l * N_LAYER + N_FIRST)
                add_tile(1).then_inc(h_done, 1)
                lo(N_FIRST, l)
                at[0] += 1
                after_h(l * 2 + 4)
                dve.wait_ge(g_cur, l + 1)
                split_rows("nX", x_hi, x_lo, gcur[:, 0:KC], l)
                ahead(("in", 0, 0), l)
                row_scale(h, "X", l)
                ahead(("in", 1, 1), l)
                split_rows("nMem", t_hi, t_lo, gcur[:, KC:2 * KC], l, groups=2)
                ahead(("in", 2, 1), l)
                split_rows("nMem", t_hi, t_lo, gcur[:, KC:2 * KC], l, start=2)
                dve.wait_ge(s_mem, l * 16 + 16)
                row_scale(memr, "Mem", l)
                ahead(("mk", 0, 1), l)
                dve.wait_ge(proj_out, proj(("in", NQ - 1), l))
                for t in range(NT):
                    heads = qkv[:, t, 0:6 * W_A].rearrange("p (g z) -> p g z", g=2)[:, :, 0:2 * W_A]\
                        .rearrange("p g (h d) -> p g h d", d=HD)
                    x1, x2 = heads[:, :, :, 0:ROT], heads[:, :, :, ROT:2 * ROT]
                    shape = [P, 2, 12, ROT]
                    cs = cst[:, C_COS + t * ROT:C_COS + (t + 1) * ROT].unsqueeze(1).unsqueeze(1).to_broadcast(shape)
                    sn = cst[:, C_SIN + t * ROT:C_SIN + (t + 1) * ROT].unsqueeze(1).unsqueeze(1).to_broadcast(shape)
                    for f, (a, b) in enumerate(((x1, cs), (x2, sn), (x2, cs), (x1, sn))):
                        last = dve.tensor_tensor(rot[:, f], a, b, ALU.mult)
                    order(last)
                    dve.tensor_tensor(x1, rot[:, 0], rot[:, 1], ALU.subtract)
                    last = dve.tensor_tensor(x2, rot[:, 2], rot[:, 3], ALU.add)
                    if t == 0:
                        order(last)
                last.then_inc(v_ready, 1)

                def ahead_gate(b):
                    key, hf = gate_unit(b)
                    ahead((*key, hf), l)

                ahead_gate(0)
                for g in range(4):
                    dve.wait_ge(t_filled, filled(("qT2", g), l))
                    for half in range(2):
                        r = slice(half * HD, (half + 1) * HD)
                        last = dve.tensor_scalar(qz[r, 4 * g + half:4 * g + 4:2, :],
                                                 T[r, T_BANK["qT2", g], :].rearrange("p (k n) -> p k n", k=2),
                                                 HD ** -0.5, None, ALU.mult)
                    last.then_inc(t_done, 1)
                ahead_gate(1)
                for g in range(4):
                    dve.wait_ge(t_filled, filled(("kT2", g), l))
                    dve.tensor_copy(kT[:, 2 * g:2 * g + 2, :].rearrange("p k n -> p (k n)"),
                                    T[:, T_BANK["kT2", g], :]).then_inc(t_done, 1)

                ahead_gate(2)

                def finish2(t):
                    over_sums(t, H_A + H_B + H_M).then_inc(o_done, 1)

                softmax(ITEMS2, lambda i: ahead_gate(min(4 + i, 10)), finish2, l)
                dve.wait_ge(o_done, o_no(1, l))
                dve.sem_inc(xr_ready, 1)
                split_rows("oT2", t_hi, t_lo, None, l, groups=3)
                def gate_branch(br, t, src):
                    for n in range(2):
                        gs = gat[:, t, br * D + n * BANK:br * D + (n + 1) * BANK]
                        last = dve.tensor_tensor(gs, gs, src(t, n), ALU.mult)
                    return last

                sums_Y = lambda t, n: Y[:, 2 * t + n, :]
                sums_UT = lambda t, n: (U, T)[t][:, n, :]
                ahead(("pj", 0), l)
                dve.wait_ge(proj_out, proj(("in", NQ + GATES[-1]), l))
                dve.wait_ge(unit_used, used(("pj", 0), l))
                for t in range(NT):
                    last = gate_branch(0, t, sums_Y)
                last.then_inc(branch, 1)
                dve.wait_ge(pj_sums, l * 2 + 1)
                for t in range(NT):
                    last = gate_branch(2, t, sums_UT)
                last.then_inc(branch, 1)
                dve.wait_ge(branch, l * 4 + 2)
                for t in range(NT):
                    last = dve.tensor_tensor(xr[:, t, :], gat[:, t, 0:D], gat[:, t, 2 * D:3 * D], ALU.add)
                order(last)
                for t in range(NT):
                    if t == 0:
                        dve.wait_ge(pj_sums, l * 2 + 2)
                    else:
                        dve.wait_ge(unit_used, used(("pj", 2), l))
                    gate_branch(1, t, sums_Y).then_inc(branch, 1)
                    dve.wait_ge(branch, l * 4 + 3 + t)
                    dve.tensor_tensor(xr[:, t, :], xr[:, t, :], gat[:, t, D:2 * D], ALU.add).then_inc(xr_ready, 1)
                ahead(("pj", 1), l)
                split_rows("yT", x_hi, x_lo, None, l)
                ahead(("pj", 2), l)
                add_residual(("wo", 3), l)
                after_h(l * 2 + 5)
                split_rows("nU", x_hi, x_lo, gcur[:, 2 * KC:3 * KC], l)
                row_scale(h, "U", l)
                for c in range(NU):
                    gated(("mu", c), lambda t: gu[:, t, :], l)
                    split_hidden(("mu", c), 4, c % 2, ("mu", 0, 1) if c == 0 else ("md", c - 1, 1), l)
                ahead(("md", NU - 1, 1), l)
                assert steps[0] == V_STEPS_LAYER, steps
            steps[0], steps[1] = first_steps + DEPTH * V_STEPS_LAYER, None
            dve.wait_ge(y_tile, DEPTH * 2 + sums_no("bo"))
            add_tile(0)
            dve.wait_ge(unit_used, N_FIRST + DEPTH * N_LAYER)
            add_tile(1).then_inc(h_done, 1)
            after_h(DEPTH * 2 + 4)
            for t in range(NT):
                last = dve.scalar_tensor_tensor(xr[:, t, :], h[:, t, :], 1.0, h[:, t, :], ALU.mult, ALU.mult,
                                                accum_out=ss[:, t:t + 1])
            order(last)
            dve.tensor_scalar(var[:, 0:NT], ss[:, 0:NT], 1.0 / D, EPS, ALU.mult, ALU.add).then_inc(n_var, 1)
            dve.wait_ge(n_sd, norm_no("X") + DEPTH * 3)
            order(refine(NT, rs[:, 0:NT]))
            dve.wait_ge(s_gfin, 16)
            for t in range(NT):
                last = dve.scalar_tensor_tensor(xr[:, t, :], h[:, t, :], rs[:, t:t + 1], gfin, ALU.mult, ALU.mult)
            last.then_inc(xr_ready, 1)

        @block.tensor
        def _(pe):
            def products(acc, a_hi, a_lo, b_hi, b_lo, first, last):
                pe.matmul(acc, a_hi, b_hi, start=first, stop=False)
                pe.matmul(acc, a_lo, b_hi, start=False, stop=False)
                return pe.matmul(acc, a_hi, b_lo, start=False, stop=last)

            def up_unit(key, hf, banks, a_hi, a_lo, l=None, fresh=None, tile0=False):
                if fresh:
                    pe.wait_ge(t_done, filled((fresh, 2 * hf + 1), l))
                pe.wait_ge(lo_ready, used((*key, hf), l))
                for t in range(NT):
                    last = up_tile(key, hf, t, banks, a_hi, a_lo)
                    if tile0 and hf == 1 and t == 0:
                        last.then_inc(up_tile0, 1)
                last.then_inc(unit_used, 1)

            def up_tile(key, hf, t, banks, a_hi, a_lo):
                s = unit_slot(UNITS[(*key, hf)])
                for q in range(4):
                    kc = 4 * hf + q
                    w = slice(q * BANK, (q + 1) * BANK)
                    tok = slice(t * P, (t + 1) * P)
                    last = products(banks[t], a_hi[:, kc, tok], a_lo[:, kc, tok], w_hi[:, s, w], w_lo[:, s, w],
                                    kc == 0, kc == KC - 1)
                return last

            def up(key, banks, a_hi, a_lo, l=None, fresh=None, tile0=False):
                for hf in range(2):
                    up_unit(key, hf, banks, a_hi, a_lo, l, fresh, tile0)

            def beside_unit(key, hf, first, a_hi, a_lo, l=None):
                if hf == 0 and not first:
                    pe.wait_ge(proj_out, proj(key, l) - 1)
                up_unit(key, hf, side, a_hi, a_lo, l)

            def beside_half(key, hf, t, a_hi, a_lo, l=None):
                if t == 0:
                    if hf == 0:
                        pe.wait_ge(proj_out, proj(key, l) - 1)
                    pe.wait_ge(lo_ready, used((*key, hf), l))
                last = up_tile(key, hf, t, side, a_hi, a_lo)
                if t == NT - 1:
                    last.then_inc(unit_used, 1)

            def down(key, a_hi, a_lo, first, final, l=None, banks=None):
                u = UNITS[key]
                s = unit_slot(u)
                pe.wait_ge(lo_ready, used(key, l))
                for t in range(NT):
                    for q in range(2):
                        for n in range(2):
                            w = slice(q * D + n * BANK, q * D + (n + 1) * BANK)
                            tok = slice(t * P, (t + 1) * P)
                            last = products(Y[:, 2 * t + n, :], a_hi[:, q, tok], a_lo[:, q, tok], w_hi[:, s, w], w_lo[:, s, w],
                                            first and q == 0, final and q == 1)
                    if final and t == 0:
                        last.then_inc(y_tile, 1)
                last.then_inc(unit_used, 1)

            def fill(key, l=None):
                prev = T_PREV[key]
                if prev is not None:
                    pe.wait_ge(t_done, filled(prev, l))
                return T[:, T_BANK[key], :]

            def turn_rows(name, rows, l=None, groups=4, start=0):
                for g in range(start, groups):
                    bank = fill((name, g), l)
                    for i in range(2):
                        for t in range(NT):
                            c = (2 * g + i) * P
                            last = pe.transpose(bank[:, i * S + t * P:i * S + (t + 1) * P], rows[:, t, c:c + P], ident)
                    last.then_inc(t_filled, 1)

            def turn_hidden(key, chunks, l=None):
                pe.wait_ge(hid_ready, hid(key, l))
                for b in range(chunks // 2):
                    k = (*key, b) if chunks == 4 else key
                    bank = fill(k, l)
                    for i in range(2):
                        for t in range(NT):
                            c = (2 * b + i) * P
                            last = pe.transpose(bank[:, i * S + t * P:i * S + (t + 1) * P], pr[:, t, c:c + P], ident)
                    last.then_inc(t_filled, 1)

            def project(key, n, a_hi, a_lo, l=None, fresh=None):
                if n >= 2:
                    pe.wait_ge(proj_out, proj(key, l) - 2)
                up(key, pair(n), a_hi, a_lo, l, fresh)

            def mlp(name, dname, n_chunks, chunks, per, l=None, fresh=None):
                def downs(c, units):
                    last_fill = (name, c, chunks // 2 - 1) if chunks == 4 else (name, c)
                    pe.wait_ge(t_done, filled(last_fill, l))
                    for i in units:
                        sl = slice(4 * (c % 2) + 2 * i, 4 * (c % 2) + 2 * i + 2)
                        key = (dname, c, i) if per == 2 else (dname, c)
                        down(key, t_hi[:, sl, :], t_lo[:, sl, :], c == 0 and i == 0, c == n_chunks - 1 and i == per - 1, l)

                for c in range(n_chunks):
                    if c >= 1:
                        pe.wait_ge(hid_ready, hid((name, c - 1), l))
                    up((name, c), pair(0), x_hi, x_lo, l, fresh if c == 0 else None, tile0=c == 0)
                    if name == "au" and c == 0:
                        spatial()
                    if c >= 1:
                        downs(c - 1, range(0, 1))
                    turn_hidden((name, c), chunks, l)
                    if c >= 1:
                        downs(c - 1, range(1, per))
                downs(n_chunks - 1, range(per))

            def spatial():
                for j in range(NT * A_GROUPS):
                    t, g = j // A_GROUPS, j % A_GROUPS
                    pe.wait_ge(v_ready, t + 1)
                    if j < 2:
                        bank = fill(("sp", j))
                    else:
                        pe.wait_ge((sp_v, sp_a)[j % 2], j // 2)
                        bank = T[:, T_BANK["sp", j], :]
                    pe.matmul(bank[:, 0:A_GD], wsr[:, t, g, :], v_a[:, t, g * A_GD:(g + 1) * A_GD], start=True, stop=True)\
                        .then_inc(t_filled, 1)

            def softmax(items, value, beside, l=None):
                def logits(i):
                    if i >= 1:
                        pe.wait_ge(p_ready, item_no(i - 1, l))
                    c = 0
                    for o, tiles in items[i][1]:
                        for head, kp, kt, v, mask, forget in tiles:
                            dst = logit_bank[:, c:c + P]
                            q = qz[:, head, items[i][0] * P:(items[i][0] + 1) * P]
                            keys = slice(kt * P, (kt + 1) * P)
                            last = pe.matmul(dst, q, kT[:, kp, keys], start=True, stop=forget is None and mask is None)
                            if forget is not None:
                                last = pe.matmul(dst, sel[:, forget, :], ncum[:, keys], start=False, stop=mask is None)
                            if mask is not None:
                                last = pe.matmul(dst, identb[:, :], maskb[:, mask, :], start=False, stop=True)
                            c += P
                    last.then_inc(l_filled, 1)

                logits(0)
                beside(-1)
                for i in range(len(items)):
                    t, outs = items[i]
                    pe.wait_ge(p_ready, item_no(i, l))
                    n = sum(len(tiles) for _, tiles in outs)
                    for j in range(n):
                        last = pe.transpose(U[:, j // 4, j % 4 * P:(j % 4 + 1) * P], p_sb[:, j * P:(j + 1) * P], ident)
                    last.then_inc(p_turned, 1)
                    if i + 1 < len(items):
                        logits(i + 1)
                    beside(i)
                    pe.wait_ge(pT_a, item_no(i, l))
                    pe.wait_ge(pT_v, item_no(i, l))
                    if i >= 1 and items[i - 1][0] != t:
                        pe.wait_ge(o_done, o_no(t - 1, l))
                    j = 0
                    for o, tiles in outs:
                        for m, tile in enumerate(tiles):
                            last = pe.matmul(o_bank[:, o * HD:(o + 1) * HD], pT_sb[:, j * P:(j + 1) * P], value(tile),
                                             start=m == 0, stop=m == len(tiles) - 1)
                            j += 1
                    last.then_inc(pv_done, 1)

            pe.wait_ge(s_const, 32)
            pe.wait_ge(s_x, 16)
            turn_rows("nA", h)
            for c in range(NA):
                project(("av", c), c, x_hi, x_lo, fresh="nA" if c == 0 else None)
                if c == 0:
                    pe.wait_ge(s_wsp, 16)
                    for i in range(2):
                        bank = fill(("wsT", i))
                        for q in range(4):
                            last = pe.transpose(bank[:, q * P:(q + 1) * P], ws[:, 4 * i + q, :], ident)
                        last.then_inc(t_filled, 1)
            pe.wait_ge(proj_out, proj(("av", NA - 1)))
            mlp("au", "ad", NA, 4, 2)
            pe.wait_ge(h_done, 1)
            turn_rows("nF", h)
            mlp("fu", "fd", NF, 2, 1, fresh="nF")
            pe.wait_ge(h_done, 2)
            turn_rows("nKV", h)
            for n in range(4):
                project(QKVG[n], n, *((x_hi, x_lo) if QKVG[n][0] == "kv" else (t_hi, t_lo)), fresh={0: "nKV", 2: "nB"}.get(n))
                if n < 2:
                    turn_rows("nB", h, groups=2 * n + 2, start=2 * n)
            pe.wait_ge(s_wf, 16)
            bank = fill(("fT", 0))
            for n, part in enumerate((x_hi, x_lo)):
                for kc in range(KC):
                    last = pe.matmul(bank[0:HEADS, 0:S], wf[:, kc, :], part[:, kc, :].bitcast(F32),
                                     start=n == 0 and kc == 0, stop=n == 1 and kc == KC - 1)
            pe.wait_ge(f_diag, 1)
            for t in range(NT):
                last = pe.matmul(bank[0:HEADS, S + t * P:S + (t + 1) * P], ones[:, 0:HEADS], diag[:, t, :], start=True, stop=True)
            last.then_inc(t_filled, 1)
            def turn_heads(name, rows):
                for g in range(4):
                    bank = fill((name, g))
                    for i in range(2):
                        for t in range(NT):
                            c = (2 * g + i) * P
                            last = pe.transpose(bank[:, i * S + t * P:i * S + (t + 1) * P], rows[:, t, c:c + P], ident)
                    last.then_inc(t_filled, 1)

            for hf in range(2):
                beside_unit(("kv", 2), hf, True, x_hi, x_lo)
            pe.wait_ge(v_ready, NT + 1)
            turn_heads("kT", k_t)
            beside_unit(("kv", 3), 0, False, x_hi, x_lo)
            pe.wait_ge(v_ready, NT + 2)
            turn_heads("qT", q_t)
            beside_unit(("kv", 3), 1, False, x_hi, x_lo)
            pe.wait_ge(t_done, filled(("qT", 3)))
            pe.wait_ge(proj_out, proj(("bi", 1)))
            pe.wait_ge(ncum_ready, 1)
            pe.wait_ge(s_bf, 2)

            def beside1(i):
                for n in BESIDE1[i + 1]:
                    u, t = n // NT, n % NT
                    beside_half(("bi", 2 + u // 2), u % 2, t, t_hi, t_lo)

            softmax(ITEMS1, lambda tile: v_t[:, tile[2], tile[3][1] * HD:(tile[3][1] + 1) * HD], beside1)
            pe.wait_ge(xr_ready, xr_no("O"))
            turn_rows("oT", xr)
            pe.wait_ge(t_done, filled(("oT", 3)))
            for i in range(4):
                down(("bo", i), x_hi[:, 2 * i:2 * i + 2, :], x_lo[:, 2 * i:2 * i + 2, :], i == 0, i == 3)
            pe.wait_ge(h_done, 3)
            turn_rows("nM", h)
            pe.wait_ge(t_done, filled(("nM", 3)))
            pe.wait_ge(r_wr, 1)
            for t in range(NT):
                for n, part in enumerate((x_hi, x_lo)):
                    for kc in range(KC):
                        last = pe.matmul(U[:, t, 0:2 * N_EXP], part[:, kc, t * P:(t + 1) * P], wr2[:, kc, :],
                                         start=n == 0 and kc == 0, stop=n == 1 and kc == KC - 1)
            last.then_inc(r_logits, 1)
            pe.wait_ge(r_chosen, 1)
            pe.matmul(U[:, 0, 16:16 + N_EXP], tri, chosen[:, 0, :], start=True, stop=True)
            pe.matmul(U[:, 1, 16:16 + N_EXP], ones, chosen[:, 0, :], start=True, stop=False)
            pe.matmul(U[:, 1, 16:16 + N_EXP], tri, chosen[:, 1, :], start=False, stop=True)
            pe.matmul(U[:, 0, 32:32 + N_EXP], ones, chosen[:, 0, :], start=True, stop=False)
            pe.matmul(U[:, 0, 32:32 + N_EXP], ones, chosen[:, 1, :], start=False, stop=True).then_inc(r_place, 1)

            pe.wait_ge(xr_ready, xr_no("M"))

            def gather(b, disp_no):
                pe.wait_ge(e_disp, disp_no)
                for q in range(4):
                    kc = 4 * b + q
                    for t in range(NT):
                        last = pe.matmul(Y[:, 3 - b, q * SLOTS:(q + 1) * SLOTS], xr[:, t, kc * P:(kc + 1) * P], disp[:, t, :],
                                         start=t == 0, stop=t == NT - 1)
                last.then_inc(e_gath, 1)

            def put_back(j, bank):
                t, n = j // 2, j % 2
                pe.matmul(bank, comb[:, t * P:(t + 1) * P], ye[:, n * BANK:(n + 1) * BANK],
                          start=True, stop=True).then_inc(e_scat, 1)

            npass = pe.alloc_register("npass")
            with pe.Fori(0, npass) as ps:
                d0 = pe.snap(ps * (N_EXP + 1))
                for b in range(2):
                    gather(b, d0 + 1)
                with pe.Fori(0, N_EXP) as e:
                    n = pe.snap(ps * N_EXP + e)
                    base = pe.snap(n * N_EU)
                    step0 = pe.snap(n * NS)
                    scat0 = pe.snap(n * E_SCAT)
                    disp0 = pe.snap(d0 + e)
                    tok = slice(0, SLOTS)

                    def e_up(s):
                        if s >= 1:
                            pe.wait_ge(e_hid, step0 + s)
                        for j in range(4):
                            k = EU["up", s, j]
                            r = unit_slot(k)
                            pe.wait_ge(e_lo, base + (k + 1 + E_RAW))
                            for q in range(4):
                                kc = 4 * (j % 2) + q
                                w = slice(q * BANK, (q + 1) * BANK)
                                last = products(U[:, j // 2, :], x_hi[:, kc, tok], x_lo[:, kc, tok], w_hi[:, r, w], w_lo[:, r, w],
                                                kc == 0, kc == KC - 1)
                            last.then_inc(e_used, 1)

                    def e_down(s, units):
                        pe.wait_ge(e_tlo, step0 + (s + 1))
                        for i in units:
                            k = EU["dn", s, i]
                            r = unit_slot(k)
                            pe.wait_ge(e_lo, base + (k + 1 + E_RAW))
                            for q in range(2):
                                c = 4 * (s % 2) + 2 * i + q
                                for n in range(2):
                                    w = slice(q * D + n * BANK, q * D + (n + 1) * BANK)
                                    last = products(Y[:, n, :], t_hi[:, c, tok], t_lo[:, c, tok], w_hi[:, r, w], w_lo[:, r, w],
                                                    s == 0 and i == 0 and q == 0, s == NS - 1 and i == 1 and q == 1)
                            last.then_inc(e_used, 1)

                    pe.wait_ge(e_glo, n * 2 + 2)
                    for s in range(NS):
                        e_up(s)
                        if s == 0:
                            pe.wait_ge(e_y, n + 1)
                            pe.wait_ge(e_comb, n + 1)
                        if s >= 1:
                            e_down(s - 1, (0,))
                        if s < 2:
                            for j in (2 * s, 2 * s + 1):
                                if s == 1:
                                    pe.wait_ge(e_add, scat0 + (j - 1))
                                put_back(j, Y[:, 2 + j % 2, :])
                        if s == 2:
                            pe.wait_ge(e_add, scat0 + 4)
                            for t in range(NT):
                                last = pe.transpose(Y[:, 2, t * P:(t + 1) * P], dispg[:, t, :], ident)
                            last.then_inc(e_turn, 1)
                        if s == 4:
                            pe.wait_ge(e_comb, n + 2)
                        if s in (3, 4):
                            gather(s - 3, disp0 + 2)
                        pe.wait_ge(e_hid, step0 + (s + 1))
                        for q in range(4):
                            last = pe.transpose(T[:, s % 2, q * P:(q + 1) * P], pr[:, 0, q * P:(q + 1) * P], ident)
                        last.then_inc(e_tf, 1)
                        if s >= 1:
                            e_down(s - 1, (1,))
                    e_down(NS - 1, (0, 1))
                pe.wait_ge(r_done, 1)
                pe.reg_load(npass, npass_i[0:1, 0:1])
            passes = pe.value_load(npass_i[0:1, 0:1], min_val=1, max_val=2)
            pe.wait_ge(e_y, passes * N_EXP + 1)
            pe.wait_ge(e_comb, passes * N_EXP + 1)
            pe.wait_ge(e_glo, passes * (2 * N_EXP))
            for j in range(E_SCAT):
                put_back(j, Y[:, j, :])
            with pe.Fori(0, DEPTH) as l:
                pe.wait_ge(h_done, l * 2 + 4)
                turn_rows("nX", h, l)
                for c in range(NQ):
                    project(("in", c), c, x_hi, x_lo, l, fresh="nX" if c == 0 else None)
                    if c in (1, 2):
                        pe.wait_ge(s_mem, l * 16 + 16)
                        turn_rows("nMem", memr, l, groups=2 * c, start=2 * c - 2)
                pe.wait_ge(t_done, filled(("nMem", 3), l))
                project(("mk", 0), NQ, t_hi, t_lo, l)

                def gates(b):
                    key, hf = gate_unit(b)
                    beside_unit(key, hf, b == 0, x_hi, x_lo, l)

                def gates_half(n):
                    key, hf = gate_unit(n // NT)
                    beside_half(key, hf, n % NT, x_hi, x_lo, l)

                def beside2(i):
                    for n in BESIDE2[i + 1]:
                        gates_half(n)

                gates(0)
                pe.wait_ge(v_ready, l + (NT + 3))
                pe.wait_ge(proj_out, proj(("mk", 0), l))
                a0, b0, m0 = 0, 3 * W_A, 3 * W_A + 3 * W_B
                q_at = [(qkv, a0 + i * P) for i in range(3)] + [(qkv, b0 + i * P) for i in range(3)] + [(qkv, m0 + i * P) for i in range(2)]
                k_at = [(qkv, a0 + W_A + i * P) for i in range(3)] + [(qkv, b0 + W_B + i * P) for i in range(3)] + [(km, i * P) for i in range(2)]
                for name, cols in (("qT2", q_at), ("kT2", k_at)):
                    for g in range(4):
                        bank = fill((name, g), l)
                        for i in range(2):
                            rows, c = cols[2 * g + i]
                            for t in range(NT):
                                last = pe.transpose(bank[:, i * S + t * P:i * S + (t + 1) * P], rows[:, t, c:c + P], ident)
                        last.then_inc(t_filled, 1)
                    gates(1 if name == "qT2" else 2)
                pe.wait_ge(t_done, filled(("kT2", 3), l))

                def value(tile):
                    which, head = tile[3]
                    rows, c = {"a": (qkv, a0 + 2 * W_A), "b": (qkv, b0 + 2 * W_B), "m": (km, W_M)}[which]
                    return rows[:, tile[2], c + head * HD:c + (head + 1) * HD]

                softmax(ITEMS2, value, beside2, l)
                gates_half(2 * (2 * NG) - 2)
                pe.wait_ge(o_done, o_no(1, l))
                pe.wait_ge(xr_ready, xr_no("O2", l))
                turn_rows("oT2", xr, l, groups=3)
                gates_half(2 * (2 * NG) - 1)
                pe.wait_ge(t_done, filled(("oT2", 2), l))
                def branch_part(kc, t):
                    u, q = ("pj", kc // 2), kc % 2
                    s = unit_slot(UNITS[u])
                    tok = slice(t * P, (t + 1) * P)
                    for n in range(2):
                        w = slice(q * D + n * BANK, q * D + (n + 1) * BANK)
                        acc = (U, T)[t][:, n, :] if kc in (1, 2) else Y[:, 2 * t + n, :]
                        last = products(acc, t_hi[:, kc, tok], t_lo[:, kc, tok], w_hi[:, s, w], w_lo[:, s, w],
                                        kc in (0, 1, 3), kc in (0, 2, 5))
                    return last

                pe.wait_ge(lo_ready, used(("pj", 0), l))
                for kc in (1, 0):
                    if kc == 0:
                        pe.wait_ge(proj_out, proj(("in", NQ + GATES[-1]), l))
                    for t in range(NT):
                        last = branch_part(kc, t)
                last.then_inc(unit_used, 1)
                pe.wait_ge(lo_ready, used(("pj", 1), l))
                for kc, signal in ((2, pj_sums), (3, unit_used)):
                    if kc == 3:
                        pe.wait_ge(branch, l * 4 + 1)
                    for t in range(NT):
                        last = branch_part(kc, t)
                    last.then_inc(signal, 1)
                pe.wait_ge(lo_ready, used(("pj", 2), l))
                for t, signal in ((0, pj_sums), (1, unit_used)):
                    for kc in (4, 5):
                        last = branch_part(kc, t)
                    last.then_inc(signal, 1)
                pe.wait_ge(xr_ready, xr_no("Y", l))
                turn_rows("yT", xr, l)
                pe.wait_ge(t_done, filled(("yT", 3), l))
                for i in range(4):
                    down(("wo", i), x_hi[:, 2 * i:2 * i + 2, :], x_lo[:, 2 * i:2 * i + 2, :], i == 0, i == 3, l)
                pe.wait_ge(h_done, l * 2 + 5)
                turn_rows("nU", h, l)
                mlp("mu", "md", NU, 4, 2, l, fresh="nU")


def constants(np):
    i = np.arange(P)
    q, k = i[:, None], i[None, :]
    c = np.zeros((P, N_CST), np.float32)
    c[:, C_ID:C_ID + P] = np.eye(P)
    c[:, C_TRI:C_TRI + P] = q < k
    c[:, C_IOTA:C_IOTA + P] = k
    c[:, C_ONES:C_ONES + S] = 1.0
    allowed = [q >= k, k >= q, (q >= k) & ((q - k) % 4 == 0), (q - k) % 4 == 0,
               (q >= k) & ((q - k) % 16 == 0), (q - k) % 16 == 0]
    masks = np.concatenate([np.where(a, 0.0, -1e30) for a in allowed], axis=1).astype(np.float32)
    inv_freq = (1.0 / (np.float32(500000.0) ** (np.arange(0, 2 * ROT, 2, dtype=np.float32) / np.float32(2 * ROT)))).astype(np.float32)
    angle = np.arange(S, dtype=np.float32)[:, None] * inv_freq[None, :]
    for t in range(NT):
        c[:, C_COS + t * ROT:C_COS + (t + 1) * ROT] = np.cos(angle[t * P:(t + 1) * P])
        c[:, C_SIN + t * ROT:C_SIN + (t + 1) * ROT] = np.sin(angle[t * P:(t + 1) * P])
    return c, masks


_WEIGHTS = ["a_w_in", "a_w_spatial", "a_w_out", "f_w_in", "f_w_out", "kv_w", "b_w_in", "b_w_out", "m_w_router", "m_w_in",
            "m_w_out", "w_in_2", "w_proj_2", "w_out_2", "w_mem_kv_2", "w_up_2", "w_down_2"]


def kernel(**inputs):
    import numpy as np
    import concourse.bacc as bacc
    from concourse.bass_utils import run_bass_kernel_spmd

    a = {k: np.ascontiguousarray(v) for k, v in inputs.items()}
    f32 = np.float32
    sml = np.zeros((P, N_SML), f32)
    for at, name in ((G_A, "a_norm_g"), (G_F, "f_norm_g"), (G_KV, "kv_norm_g"), (G_B, "b_norm_g"), (G_M, "m_norm_g")):
        sml[:, at:at + KC] = a[name].reshape(KC, P).T
    sml[:, G_BT:G_BT + A_GROUPS] = a["a_b_spatial"][0].T
    sml[:, G_K] = np.tile(a["k_norm_g"], 2)
    sml[:, G_Q] = np.tile(a["q_norm_g"][0], 2)
    sml[0:HEADS, G_BF] = a["kv_b_f"]
    for l in range(DEPTH):
        for j, name in enumerate(("norm_mix_2", "norm_mem_2", "norm_mlp_2")):
            at = G_L + (l * 3 + j) * KC
            sml[:, at:at + KC] = a[name][l].reshape(KC, P).T
    a["w_proj_2"] = np.concatenate([a["w_proj_a_2"], a["w_proj_m_2"], a["w_proj_b_2"]], axis=1)
    cst, masks = constants(np)
    arrays = {"x": a["x"], "mem": a["mem_2"], "cst": cst, "masks": masks, "sml": sml, "gv": a["a_v_norm_g"].reshape(-1),
              "gm": a["m_norm_g"].reshape(-1), "gfin": a["norm_final_2"]}
    arrays.update({n: a[n] for n in _WEIGHTS})

    nc = bacc.Bacc("TRN2", target_bir_lowering=False, num_devices=1)
    args, feeds = [], {}
    for name, v in arrays.items():
        feeds[f"in_{name}"] = v
        args.append(nc.dram_tensor(f"in_{name}", v.shape, mybir.dt.from_np(v.dtype), kind="ExternalInput").ap())
    out = nc.dram_tensor("out", (1, S, D), F32, kind="ExternalOutput").ap()
    program(nc, *args, out)
    return run_bass_kernel_spmd(nc, [feeds], core_ids=[0]).results[0]["out"]
```
